# Optimizing a Trainium2 kernel written in Bass

```python
import jax
import jax.numpy as jnp
from jax import lax
import numpy as np

D_MODEL = 1024
BATCH = 1
SEQ = 512
DEPTH = 2
DEC_BATCH = 8
DEC_SEQ = 1
PAST_LEN = 1024
PAGE_SIZE = 128

N_EVEN = (DEPTH + 1) // 2
N_ODD = DEPTH // 2
FOX_HEADS = 8
FOX_HEAD_DIM = 64
FOX_DIM = FOX_HEADS * FOX_HEAD_DIM
Q_BLOCK = 128
CONV_CH = D_MODEL // 2
CONV_GROUPS = 8
CONV_WIDTH = 31
RET_HEADS = 4
RET_KEY_DIM = D_MODEL // RET_HEADS
RET_VAL_DIM = 2 * D_MODEL // RET_HEADS
RET_CHUNK = 128
FFN_HIDDEN = -(-8 * D_MODEL // (3 * 256)) * 256
EVEN_IN = 3 * FOX_DIM + FOX_HEADS + 2 * CONV_CH
ODD_IN = 2 * RET_HEADS * RET_KEY_DIM + 2 * RET_HEADS * RET_VAL_DIM
EPS = 1e-6
ROPE_BASE = 10000.0

kernel_name = 'fox_conformer_retnet_adaln_step'

def _rmsnorm(x, g):
    xf = x.astype(jnp.float32)
    y = xf * lax.rsqrt(jnp.mean(xf * xf, axis=-1, keepdims=True) + EPS)
    return (y * g.astype(jnp.float32)).astype(x.dtype)

def _group_norm(x, groups):
    shp = x.shape
    xf = x.astype(jnp.float32).reshape(shp[:-1] + (groups, shp[-1] // groups))
    mu = jnp.mean(xf, axis=-1, keepdims=True)
    var = jnp.mean(jnp.square(xf - mu), axis=-1, keepdims=True)
    return ((xf - mu) * lax.rsqrt(var + EPS)).reshape(shp)

def _rope(x, pos):
    half = x.shape[-1] // 2
    inv = 1.0 / (ROPE_BASE ** jnp.linspace(0.0, 1.0, half, dtype=jnp.float32))
    ang = pos.astype(jnp.float32)[:, None] * inv[None, :]
    cos = jnp.cos(ang)[None, :, None, :]
    sin = jnp.sin(ang)[None, :, None, :]
    x1, x2 = x[..., :half], x[..., half:]
    return jnp.concatenate([x1 * cos - x2 * sin, x1 * sin + x2 * cos], axis=-1)

def _fox_prompt(q, k, v, logf):
    B, L, H, hd = q.shape
    cum = jnp.cumsum(logf, axis=1)
    nb = L // Q_BLOCK
    qb = q.reshape(B, nb, Q_BLOCK, H, hd).transpose(1, 0, 2, 3, 4)
    cb = cum.reshape(B, nb, Q_BLOCK, H).transpose(1, 0, 2, 3)
    qpos = jnp.arange(L).reshape(nb, Q_BLOCK)
    kpos = jnp.arange(L)
    cum_k = cum.transpose(0, 2, 1)[:, :, None, :]
    scale = FOX_HEAD_DIM ** -0.5

    def block(args):
        qi, ci, pi = args
        s = jnp.einsum('bqhd,bkhd->bhqk', qi, k, preferred_element_type=jnp.float32) * scale
        s = s + ci.transpose(0, 2, 1)[..., None] - cum_k
        s = jnp.where(kpos[None, :] <= pi[:, None], s, -jnp.inf)
        p = jax.nn.softmax(s, axis=-1)
        return jnp.einsum('bhqk,bkhd->bqhd', p.astype(v.dtype), v)

    o = lax.map(block, (qb, cb, qpos))
    return o.transpose(1, 0, 2, 3, 4).reshape(B, L, H * hd)

def _fox_sample(q, k, v, logf, cache_k, cache_v, cache_logf, page_table, e):
    Bd, T, H, hd = q.shape
    kp = cache_k[e, page_table].reshape(Bd, -1, H, hd)
    vp = cache_v[e, page_table].reshape(Bd, -1, H, hd)
    lp = cache_logf[e, page_table].reshape(Bd, -1, H).astype(jnp.float32)
    P = kp.shape[1]
    cum_p = jnp.cumsum(lp, axis=1)
    cum_n = cum_p[:, -1:, :] + jnp.cumsum(logf, axis=1)
    cq = cum_n.transpose(0, 2, 1)
    scale = FOX_HEAD_DIM ** -0.5
    s_p = jnp.einsum('bqhd,bkhd->bhqk', q, kp, preferred_element_type=jnp.float32) * scale
    s_p = s_p + cq[..., None] - cum_p.transpose(0, 2, 1)[:, :, None, :]
    s_n = jnp.einsum('bqhd,bkhd->bhqk', q, k, preferred_element_type=jnp.float32) * scale
    s_n = s_n + cq[..., None] - cq[:, :, None, :]
    tri = jnp.arange(T)[None, :] <= jnp.arange(T)[:, None]
    s_n = jnp.where(tri, s_n, -jnp.inf)
    p = jax.nn.softmax(jnp.concatenate([s_p, s_n], axis=-1), axis=-1)
    o = (jnp.einsum('bhqk,bkhd->bqhd', p[..., :P].astype(v.dtype), vp)
         + jnp.einsum('bhqk,bkhd->bqhd', p[..., P:].astype(v.dtype), v))
    return o.reshape(Bd, T, H * hd)

def _retention(q, k, v, s0, chunk):
    B, L, H, dk = q.shape
    dv = v.shape[-1]
    n = L // chunk
    lg = jnp.log(1.0 - 2.0 ** (-5.0 - jnp.arange(H, dtype=jnp.float32)))
    i = jnp.arange(chunk, dtype=jnp.float32)
    diff = i[:, None] - i[None, :]
    dmask = jnp.where(diff >= 0, jnp.exp(jnp.where(diff >= 0, diff, 0.0)[None] * lg[:, None, None]), 0.0)
    q_dec = jnp.exp((i[None, :] + 1.0) * lg[:, None]).T
    k_dec = jnp.exp((chunk - 1.0 - i)[None, :] * lg[:, None]).T
    c_dec = jnp.exp(chunk * lg)

    def split(t):
        return t.reshape(B, n, chunk, H, t.shape[-1]).transpose(1, 0, 2, 3, 4)

    def step(S, xs):
        qc, kc, vc = xs
        a = jnp.einsum('bihd,bjhd->bhij', qc, kc) * dmask[None]
        o = (jnp.einsum('bhij,bjhe->bihe', a, vc)
             + jnp.einsum('bihd,bhde->bihe', qc * q_dec[None, :, :, None], S))
        S = S * c_dec[None, :, None, None] + jnp.einsum('bjhd,bjhe->bhde', kc * k_dec[None, :, :, None], vc)
        return S, o

    S, o = lax.scan(step, s0, (split(q), split(k), split(v)))
    return o.transpose(1, 0, 2, 3, 4).reshape(B, L, H, dv), S

def _even_mixer(h, e, fox_attend, conv_buf, W):
    B, L, _ = h.shape
    z = h @ W['w_in_even'][e]
    cuts = [FOX_DIM, 2 * FOX_DIM, 3 * FOX_DIM, 3 * FOX_DIM + FOX_HEADS, 3 * FOX_DIM + FOX_HEADS + CONV_CH]
    q, k, v, fl, a, b = jnp.split(z, cuts, axis=-1)
    q = q.reshape(B, L, FOX_HEADS, FOX_HEAD_DIM)
    k = k.reshape(B, L, FOX_HEADS, FOX_HEAD_DIM)
    v = v.reshape(B, L, FOX_HEADS, FOX_HEAD_DIM)
    logf = jax.nn.log_sigmoid(fl.astype(jnp.float32) + W['b_forget'][e].astype(jnp.float32))
    o_fox = fox_attend(e, q, k, v, logf)
    u = a * jax.nn.sigmoid(b)
    xp = jnp.concatenate([conv_buf.astype(u.dtype), u], axis=1)
    new_buf = xp[:, -(CONV_WIDTH - 1):]
    cv = lax.conv_general_dilated(
        xp, W['conv_w'][e][:, None, :].astype(u.dtype), window_strides=(1,), padding='VALID',
        dimension_numbers=('NWC', 'WIO', 'NWC'), feature_group_count=CONV_CH) + W['conv_b'][e]
    cv = _group_norm(cv, CONV_GROUPS) * W['conv_norm_g'][e].astype(jnp.float32) + W['conv_norm_b'][e].astype(jnp.float32)
    cv = jax.nn.silu(cv).astype(h.dtype)
    out = jnp.concatenate([o_fox.astype(h.dtype), cv], axis=-1) @ W['w_out_even'][e]
    return out, (k, v, logf, new_buf)

def _odd_mixer(h, o, pos, s0, chunk, W):
    B, L, _ = h.shape
    nk = RET_HEADS * RET_KEY_DIM
    nv = RET_HEADS * RET_VAL_DIM
    z = h @ W['w_in_odd'][o]
    q, k, v, g = jnp.split(z, [nk, 2 * nk, 2 * nk + nv], axis=-1)
    q = _rope(q.reshape(B, L, RET_HEADS, RET_KEY_DIM).astype(jnp.float32), pos)
    k = _rope(k.reshape(B, L, RET_HEADS, RET_KEY_DIM).astype(jnp.float32), pos) * (RET_KEY_DIM ** -0.5)
    v = v.reshape(B, L, RET_HEADS, RET_VAL_DIM).astype(jnp.float32)
    r, S = _retention(q, k, v, s0.astype(jnp.float32), chunk)
    r = _group_norm(r.reshape(B, L, nv), RET_HEADS) * W['ret_norm_g'][o].astype(jnp.float32)
    out = (jax.nn.silu(g) * r.astype(h.dtype)) @ W['w_out_odd'][o]
    return out, S

def _trunk(x, c, pos, fox_attend, conv_init, ret_init, ret_chunk, W):
    ks, vs, lfs, cbs, rs = [], [], [], [], []
    cmod = jax.nn.silu(c)
    for l in range(DEPTH):
        mod = cmod @ W['ada_w'][l] + W['ada_b'][l]
        sh1, sc1, g1, sh2, sc2, g2 = [m[:, None, :] for m in jnp.split(mod, 6, axis=-1)]
        hm = _rmsnorm(x, W['norm_mix_g'][l]) * (1.0 + sc1) + sh1
        if l % 2 == 0:
            e = l // 2
            out, (k, v, lf, cb) = _even_mixer(hm, e, fox_attend, conv_init(e), W)
            ks.append(k); vs.append(v); lfs.append(lf); cbs.append(cb)
        else:
            o = l // 2
            out, S = _odd_mixer(hm, o, pos, ret_init(o), ret_chunk, W)
            rs.append(S)
        x = x + g1 * out
        hf = _rmsnorm(x, W['norm_ffn_g'][l]) * (1.0 + sc2) + sh2
        ff = (jax.nn.silu(hf @ W['w_ffn_gate'][l]) * (hf @ W['w_ffn_up'][l])) @ W['w_ffn_down'][l]
        x = x + g2 * ff
    y = _rmsnorm(x, W['final_norm_g'])
    return y, (jnp.stack(ks), jnp.stack(vs), jnp.stack(lfs), jnp.stack(cbs), jnp.stack(rs))

def setup_inputs(seed: int = 0) -> dict:
    key = jax.random.key(seed)
    ks = jax.random.split(key, 32)
    f32 = jnp.float32
    D = D_MODEL
    n_pages = PAST_LEN // PAGE_SIZE
    n_used = DEC_BATCH * n_pages
    n_phys = n_used + n_used // 4

    def nrm(k, shape, s=1.0):
        return s * jax.random.normal(k, shape, f32)

    nv = RET_HEADS * RET_VAL_DIM
    return {
        'x_prompt': nrm(ks[0], (BATCH, SEQ, D)),
        'x_sample': nrm(ks[1], (DEC_BATCH, DEC_SEQ, D)),
        'cache_k': nrm(ks[2], (N_EVEN, n_phys, PAGE_SIZE, FOX_HEADS, FOX_HEAD_DIM)),
        'cache_v': nrm(ks[3], (N_EVEN, n_phys, PAGE_SIZE, FOX_HEADS, FOX_HEAD_DIM)),
        'cache_logf': jax.nn.log_sigmoid(nrm(ks[4], (N_EVEN, n_phys, PAGE_SIZE, FOX_HEADS)) + 3.0),
        'state_conv': nrm(ks[5], (N_EVEN, DEC_BATCH, CONV_WIDTH - 1, CONV_CH), 0.5),
        'state_ret': nrm(ks[6], (N_ODD, DEC_BATCH, RET_HEADS, RET_KEY_DIM, RET_VAL_DIM), 0.1),
        'page_table': jax.random.permutation(ks[7], n_phys)[:n_used].reshape(DEC_BATCH, n_pages).astype(jnp.int32),
        'c_prompt': nrm(ks[8], (BATCH, D)),
        'c_sample': nrm(ks[9], (DEC_BATCH, D)),
        'ada_w': nrm(ks[10], (DEPTH, D, 6 * D), 0.5 * D ** -0.5),
        'ada_b': nrm(ks[11], (DEPTH, 6 * D), 0.02),
        'norm_mix_g': 1.0 + nrm(ks[12], (DEPTH, D), 0.05),
        'norm_ffn_g': 1.0 + nrm(ks[13], (DEPTH, D), 0.05),
        'w_in_even': nrm(ks[14], (N_EVEN, D, EVEN_IN), D ** -0.5),
        'b_forget': jax.random.uniform(ks[15], (N_EVEN, FOX_HEADS), f32, 1.0, 4.0),
        'conv_w': nrm(ks[16], (N_EVEN, CONV_WIDTH, CONV_CH), CONV_WIDTH ** -0.5),
        'conv_b': nrm(ks[17], (N_EVEN, CONV_CH), 0.02),
        'conv_norm_g': 1.0 + nrm(ks[18], (N_EVEN, CONV_CH), 0.05),
        'conv_norm_b': nrm(ks[19], (N_EVEN, CONV_CH), 0.02),
        'w_out_even': nrm(ks[20], (N_EVEN, FOX_DIM + CONV_CH, D), (FOX_DIM + CONV_CH) ** -0.5),
        'w_in_odd': nrm(ks[21], (N_ODD, D, ODD_IN), D ** -0.5),
        'ret_norm_g': 1.0 + nrm(ks[22], (N_ODD, nv), 0.05),
        'w_out_odd': nrm(ks[23], (N_ODD, nv, D), nv ** -0.5),
        'w_ffn_gate': nrm(ks[24], (DEPTH, D, FFN_HIDDEN), D ** -0.5),
        'w_ffn_up': nrm(ks[25], (DEPTH, D, FFN_HIDDEN), D ** -0.5),
        'w_ffn_down': nrm(ks[26], (DEPTH, FFN_HIDDEN, D), FFN_HIDDEN ** -0.5),
        'final_norm_g': 1.0 + nrm(ks[27], (D,), 0.05),
    }

def reference(x_prompt, x_sample, cache_k, cache_v, cache_logf, state_conv, state_ret, page_table,
              c_prompt, c_sample, ada_w, ada_b, norm_mix_g, norm_ffn_g, w_in_even, b_forget,
              conv_w, conv_b, conv_norm_g, conv_norm_b, w_out_even, w_in_odd, ret_norm_g, w_out_odd,
              w_ffn_gate, w_ffn_up, w_ffn_down, final_norm_g):
    W = dict(ada_w=ada_w, ada_b=ada_b, norm_mix_g=norm_mix_g, norm_ffn_g=norm_ffn_g,
             w_in_even=w_in_even, b_forget=b_forget, conv_w=conv_w, conv_b=conv_b,
             conv_norm_g=conv_norm_g, conv_norm_b=conv_norm_b, w_out_even=w_out_even,
             w_in_odd=w_in_odd, ret_norm_g=ret_norm_g, w_out_odd=w_out_odd,
             w_ffn_gate=w_ffn_gate, w_ffn_up=w_ffn_up, w_ffn_down=w_ffn_down,
             final_norm_g=final_norm_g)
    bp, lp, _ = x_prompt.shape
    bs, ls, _ = x_sample.shape
    past_len = page_table.shape[1] * PAGE_SIZE

    y_prompt, (k_p, v_p, lf_p, conv_p, ret_p) = _trunk(
        x_prompt, c_prompt, jnp.arange(lp),
        lambda e, q, k, v, lf: _fox_prompt(q, k, v, lf),
        lambda e: jnp.zeros((bp, CONV_WIDTH - 1, CONV_CH), x_prompt.dtype),
        lambda o: jnp.zeros((bp, RET_HEADS, RET_KEY_DIM, RET_VAL_DIM), jnp.float32),
        min(RET_CHUNK, lp), W)

    y_sample, (k_s, v_s, lf_s, conv_s, ret_s) = _trunk(
        x_sample, c_sample, past_len + jnp.arange(ls),
        lambda e, q, k, v, lf: _fox_sample(q, k, v, lf, cache_k, cache_v, cache_logf, page_table, e),
        lambda e: state_conv[e],
        lambda o: state_ret[o],
        ls, W)
    ret_s = ret_s.astype(state_ret.dtype)

    return (y_prompt, y_sample, k_p, v_p, lf_p, conv_p, ret_p, k_s, v_s, lf_s, conv_s, ret_s)


_drawn_inputs = setup_inputs


def setup_inputs(seed=0):
    import zlib

    import numpy as np

    out = dict(_drawn_inputs(seed))
    spreads = {}
    factors = {'cache_logf': 6.576,
     'norm_ffn_g': 2.751,
     'conv_b': 5.081,
     'conv_norm_g': 4.539,
     'conv_norm_b': 8.0,
     'ret_norm_g': 5.988}
    for name, (base, spread) in spreads.items():
        noise = np.random.default_rng([zlib.crc32(name.encode()), seed]).standard_normal(out[name].shape)
        drawn = base * np.exp(spread * noise) if base else spread * noise
        out[name] = jnp.asarray(drawn.astype(out[name].dtype))
    for name, factor in factors.items():
        out[name] = (out[name] * factor).astype(out[name].dtype)
    return out
```

```python
import math
from contextlib import ExitStack

import concourse.bass as bass
import concourse.mybir as mybir
import numpy as np

P = 128
D = 1024
KD = D // P
L = 512
TB = L // P
NB = 8
T = NB + L
CH = T // 2
HEADS = 8
HD = 64
PAST = 1024
PAGES = PAST // P
NPG = NB * PAGES
CW = 31
RH = 4
DK = 256
DV = 512
FF = 2816
EPS = 1e-6
FOX_SCALE = HD ** -0.5
MASKED = -1e30
THIRDS = ((0, 8), (8, 8), (16, 6))
GAMMA = [1.0 - 2.0 ** (-5.0 - h) for h in range(RH)]

C_ID, C_MEAN, C_B64, C_M512, C_ONE, C_TRI, C_NEG = (P * i for i in range(7))
C_COS = 7 * P
C_SIN = C_COS + T
C_KDEC = C_SIN + T
C_END = C_KDEC + TB * RH

N_IN_EVEN = 0
N_OUT_EVEN = 20
N_FFN = (28, 160)
N_ODD = 96
N_BLOCKS = 228
N_ADA = 96
ADA_FIRST = 4
ADA_ATT = 8


def ada_turned(x):
    return ADA_ATT + x // 2 - 1 if x % 2 == 0 and x > 0 else None


def ffn_starts(layer):
    at, out = N_FFN[layer], []
    for _, tiles in THIRDS:
        out.append((at, at + 2 * tiles))
        at += 2 * tiles + KD
    return out


def k_tiles(n):
    for layer in range(2):
        down = ffn_starts(layer)[2][1]
        if down <= n < down + KD:
            return THIRDS[2][1]
    return KD


V_MIXG, V_FFNG, V_FING, V_CB, V_CG, V_CNB, V_RG = 0, 16, 32, 40, 44, 48, 52
V_ROWS = 68
V_ADAB = V_ROWS
V_CW = V_ADAB + N_ADA
V_END = V_CW + CW * 4


def psum_jobs():
    jobs = [("xs", "D")] + [(("xT", k), "D") for k in range(KD)]
    jobs += [("cT", "D"), ("vec", "D"), (("sc", 0), "D"), (("sc", 1), "D")]

    def norm(i):
        return [(("ss", i, 0), "D"), (("ss", i, 1), "D")]

    jobs += norm(0) + [(("ada", g), "D") for g in range(ADA_FIRST)] + [("fl", "D")]
    jobs += [(("ada", g), "D") for g in range(ADA_FIRST, ADA_ATT)]
    jobs += [(("cm", t, c), "D") for t in range(4) for c in range(2)]
    jobs += [("cpo", "A"), ("cso", "A")]
    jobs += [("qs", "A")] + [(("qb", b), "A") for b in range(NB)]
    jobs += [(("cq", t, c), "D") for t in range(4) for c in range(2)]
    jobs += [("cum", "D"), ("cumT", "A")]
    jobs += [(("kn", tb), "A") for tb in range(TB)] + [(("vn", tb), "A") for tb in range(TB)]
    jobs += [("ks", "A"), ("vs", "A")]
    jobs += [(("ckb", 0), "A")] + [(("s", 0, q), "D") for q in range(TB)]
    for h in range(HEADS):
        if h + 1 < HEADS:
            jobs += [(("ckb", h + 1), "A")]
        for q in range(TB):
            jobs += [(("pt", h, q), "A")]
            if h + 1 < HEADS:
                jobs += [(("s", h + 1, q), "D")]
            if ada_turned(h * TB + q) is not None:
                jobs += [(("ada", ada_turned(h * TB + q)), "D")]
        jobs += [(("o", h), "D")]
    jobs += [(("ada", N_ADA // 4 - 1), "D")]
    jobs += [("lt", "A"), ("cc", "D"), ("cl", "A"), ("sn", "D")]
    jobs += [("mt", "D"), ("mb", "D"), ("dn", "D"), ("ov", "D")]
    jobs += norm(1) + norm(2)
    for h in range(RH):
        jobs += [(("rvn", h, tb), "A") for tb in range(TB)]
        jobs += [(("rvs", h), "A")]
        jobs += [(("rkn", h, tb), "A") for tb in range(TB)]
        jobs += [(("ra", h, j), "D") for j in range(TB)]
        jobs += [(("rst", h, d), "A") for d in range(2)]
        jobs += [(("ro", h, e), "A") for e in range(4)]
        for b in range(NB):
            jobs += [(("vb", h, b), "D")]
        jobs += [(("rm", h, c), "D") for c in range(2)] + [(("rv", h, c), "D") for c in range(2)]
    jobs += norm(3) + norm(4)
    jobs += [(("y", tb, f), "A") for tb in range(TB) for f in range(2)]
    jobs += [(("ys", f), "A") for f in range(2)]
    return jobs


class Jobs:

    def __init__(self):
        jobs = psum_jobs()
        self.index = {name: i for i, (name, _) in enumerate(jobs)}
        assert len(self.index) == len(jobs)
        self.engine = [e for _, e in jobs]
        count = {"A": 0, "D": 0}
        self.nth = []
        for e in self.engine:
            count[e] += 1
            self.nth.append(count[e])

    def bank(self, name):
        return self.index[name] % 4

    def done(self, name):
        return self.index[name] + 1

    def emptied(self, name):
        i = self.index[name]
        return self.engine[i], self.nth[i]


class Tally:

    def __init__(self, eng):
        self.eng, self.count = eng, {}

    def up(self, instruction, sem):
        instruction.then_inc(sem, 1)
        self.count[sem.name] = self.count.get(sem.name, 0) + 1

    def skip(self, sem, n):
        self.count[sem.name] = self.count.get(sem.name, 0) + n

    def own(self, sem, back=0):
        if self.count[sem.name] > back:
            self.eng.wait_ge(sem, self.count[sem.name] - back)


def build(nc, A):
    f32, f32r, i32 = mybir.dt.float32, mybir.dt.float32r, mybir.dt.int32
    ACT, ALU, AX = mybir.ActivationFunctionType, mybir.AluOpType, mybir.AxisListType
    ds = bass.ds
    jobs = Jobs()

    at = [(nc.sbuf_base + 63) // 64 * 64]

    def sb(name, shape, dtype=f32):
        t = nc.alloc_sbuf_tensor_at(name, shape, dtype, offset=at[0])
        at[0] += (math.prod(shape[1:]) * 4 + 31) // 32 * 32
        assert at[0] <= nc.sbuf_usable_end, (name, at[0])
        return t

    X = sb("X", [P, KD, T])
    con = sb("con", [P, C_END])
    vec = sb("vec", [P, V_END])
    mod = sb("mod", [P, N_ADA, 9])
    coef = sb("coef", [P, KD, 9])
    raw = sb("raw", [P, 4, KD, P])
    w_hi = sb("w_hi", [P, 4, KD, P], f32r)
    w_lo = sb("w_lo", [P, 4, KD, P], f32r)
    lf = sb("lf", [P, 5, HEADS])
    lf_a = sb("lf_a", [P, 5, HEADS])
    lf_b = sb("lf_b", [P, 5, HEADS])
    bfg = sb("bfg", [P, HEADS])
    cT = sb("cT", [P, KD, 9])
    g_at = at[0]
    G_hi = sb("G_hi", [P, KD, T], f32r)
    gl_at = at[0]
    G_lo = sb("G_lo", [P, KD, T], f32r)
    h_at = at[0]
    H_hi = sb("H_hi", [P, KD, T], f32r)
    H_lo = sb("H_lo", [P, KD, T], f32r)
    free_at = at[0]
    sq = sb("sq", [P, 2, T])
    rstd = sb("rstd", [P, T])
    scaled = sb("scaled", [P, 2, T])
    full = sb("full", [P, 2, T])
    full_s = sb("full_s", [P, KD, NB])
    upd_s = sb("upd_s", [P, 2, NB])
    gate_at = at[0]
    gate = sb("gate", [P, 2, T])
    wf = sb("wf", [P, KD, 8])
    wf_hi = sb("wf_hi", [P, KD, 8], f32r)
    wf_lo = sb("wf_lo", [P, KD, 8], f32r)
    scratch_end = max(at[0], free_at + 10 * 512 * 4)
    at[0] = h_at
    xn = sb("xn", [P, TB, D])
    xsn = sb("xsn", [NB, D])
    cn = sb("cn", [9, D])
    cn_silu = sb("cn_silu", [9, D])
    rows_s = sb("rows_s", [120, 2, 512])
    at[0] = scratch_end
    rows_v = sb("rows_v", [V_ROWS, P])
    rows_a = sb("rows_a", [N_ADA, P])
    rows_c = sb("rows_c", [CW * 4, P])
    at[0] = scratch_end
    QT = sb("QT", [P, 4, T])
    KT = sb("KT", [P, 4, T])
    vt_at = at[0]
    VT = sb("VT", [P, 4, T])
    us_at = at[0]
    US = sb("US", [P, 4, NB, CW + 1])
    SC = sb("SC", [P, HEADS, NB, 8])
    small = sb("small", [P, 8, 64])
    up_at = at[0]
    UP = sb("UP", [P, 4, CW - 1 + L])
    usw = sb("usw", [P, NB, CW])
    even_end = at[0]
    at[0] = vt_at
    AT = sb("AT", [P, 4, T])
    at[0] = g_at
    CV = sb("CV", [P, 4, T])
    at[0] = gl_at
    CR = sb("CR", [P, 4, T])
    at[0] = h_at
    QB = sb("QB", [P, NB, 512])
    VN = sb("VN", [P, TB, 512])
    PTS = sb("PTS", [P, TB, 512])
    assert at[0] <= free_at
    at[0] = h_at + NB * 512 * 4
    sq4 = sb("sq4", [P, 4, T])
    at[0] = free_at
    SS = sb("SS", [P, TB, 512])
    kp = sb("kp", [P, 4, 512])
    prod = sb("prod", [P, 2, 512])
    assert at[0] <= scratch_end
    at[0] = free_at
    LT = sb("LT", [P, HEADS, NB, 8])
    EX = sb("EX", [P, HEADS, NB, 8])
    CC = sb("CC", [P, HEADS, NB, 8])
    at[0] = vt_at
    vp = sb("vp", [P, 4, 512])
    at[0] = gate_at
    rows_early = sb("rows_early", [9, 2, 512])
    at[0] = vt_at
    rows_late = sb("rows_late", [9, 2, 512])
    at[0] = h_at
    vm = sb("vm", [HEADS, 2, 512])
    at[0] = up_at
    ckb = sb("ckb", [P, 2, L])
    ko_at = at[0]
    kn_out = sb("kn_out", [P, 2, 512])
    assert at[0] <= even_end
    at[0] = us_at
    qsn = sb("qsn", [NB, 512])
    cum8 = sb("cum8", [HEADS, L])
    at[0] = even_end
    cumul = sb("cumul", [P, TB, HEADS])
    nm = sb("nm", [P, HEADS * TB])
    rs = sb("rs", [P, HEADS * TB])
    ri = sb("ri", [P, HEADS * TB])
    pt_row = sb("pt_row", [1, NPG], i32)
    pt_col = sb("pt_col", [NPG, 1], i32)
    at[0] = ko_at
    lg = sb("lg", [NPG, P * HEADS])
    vts = sb("vts", [P, 4, NB])
    at[0] = free_at
    dec = sb("dec", [P, L])
    raw_at = at[0]
    QK = sb("QK", [P, 4, T])
    QKR = sb("QKR", [P, 4, T])
    RVT = sb("RVT", [P, 4, T])
    RVN = sb("RVN", [P, TB, DV])
    KDN = sb("KDN", [P, TB, DK])
    GS = sb("GS", [P, 4, T])
    tmp_at = at[0]
    tmp = sb("tmp", [P, 2, T])
    st = sb("st", [P, 2, 2, DV])
    so = sb("so", [P, 2, DV])
    rsd = sb("rsd", [P, T])
    at[0] = raw_at
    AD = sb("AD", [P, TB, L])
    at[0] = raw_at
    RSQ = sb("RSQ", [P, 4, T])
    at[0] = tmp_at
    vsn = sb("vsn", [NB, DV])
    at[0] = g_at
    YT = sb("YT", [P, KD, T])
    yo = sb("yo", [P, 2, 512])

    ctx = ExitStack()
    with ctx:
        def sem(name):
            return ctx.enter_context(nc.semaphore(name))

        Gp = [ctx.enter_context(nc.psum_tensor(f"product{i}", [P, 2, 512], f32)) for i in range(2)]
        Jp = [ctx.enter_context(nc.psum_tensor(f"job{i}", [P, 512], f32)) for i in range(4)]

        x_loaded, rows_loaded, pages_loaded = sem("x_loaded"), sem("rows_loaded"), sem("pages_loaded")
        raw_loaded = [sem(f"raw_loaded{i}") for i in range(4)]
        k_page = [sem(f"k_page{i}") for i in range(4)]
        v_page = [sem(f"v_page{i}") for i in range(4)]
        lg_loaded, dec_loaded = sem("lg_loaded"), sem("dec_loaded")
        st_loaded = [sem(f"st_loaded{i}") for i in range(2)]
        st_stored = [sem(f"st_stored{i}") for i in range(2)]
        stage_stored = [sem(f"stage_stored{i}") for i in range(2)]
        out_done, v_stored = sem("out_done"), sem("v_stored")
        block_done, ada_used, job_done = sem("block_done"), sem("ada_used"), sem("job_done")
        ada_taken = sem("ada_taken")
        sq_used, v_used, st_used = sem("sq_used"), sem("v_used"), sem("st_used")
        vm_used = sem("vm_used")
        slot_act, slot_dve = sem("slot_act"), sem("slot_dve")
        emptied = {"A": sem("emptied_act"), "D": sem("emptied_dve")}
        c_silu, sq_ready, rstd_ready = sem("c_silu"), sem("sq_ready"), sem("rstd_ready")
        full_ready, hh_ready, hi_ready = sem("full_ready"), sem("hh_ready"), sem("hi_ready")
        ghi_ready, exp_ready, lf_act = sem("ghi_ready"), sem("exp_ready"), sem("lf_act")
        conv_act, ohi_ready, st_scaled = sem("conv_act"), sem("ohi_ready"), sem("st_scaled")
        samp_act, ret_act = sem("samp_act"), sem("ret_act")
        x_ready, var_ready, vm_ready = sem("x_ready"), sem("var_ready"), sem("vm_ready")
        scaled_ready, h_ready, lo_ready = sem("scaled_ready"), sem("h_ready"), sem("lo_ready")
        g_ready, dve_step, lf_dve = sem("g_ready"), sem("dve_step"), sem("lf_dve")
        u_ready, cv_ready, conv_var = sem("u_ready"), sem("cv_ready"), sem("conv_var")
        conv_normed, conv_step, ret_gated = sem("conv_normed"), sem("conv_step"), sem("ret_gated")
        max_ready, ri_ready, page_dot = sem("max_ready"), sem("ri_ready"), sem("page_dot")
        samp_dve, rope_ready = sem("samp_dve"), sem("rope_ready")
        ret_dve = sem("ret_dve")
        pad_ready, p_ready, prod_ready = sem("pad_ready"), sem("p_ready"), sem("prod_ready")
        outs = []

        def store(eng, dst, src, done=None):
            s = done or out_done
            outs.append(s)
            eng.dma_start(dst, src).then_inc(s, 16)

        def wait_job(eng, name):
            eng.wait_ge(job_done, jobs.done(name))

        def wait_emptied(eng, name):
            e, n = jobs.emptied(name)
            eng.wait_ge(emptied[e], n)

        ident = con[:, C_ID:C_ID + P]
        ones = con[:, C_ONE:C_ONE + P]
        one_col = con[:, C_ONE:C_ONE + 1]

        runs, ra, rd = {}, 2, 1
        for name, a, d in (
            [("in_even", 20, 0), ("out_even", 0, KD)]
            + [x for t, (_, n) in enumerate(THIRDS) for x in ((("gu", 0, t), n, n), (("dn", 0, t), 0, KD))]
            + [x for p in range(2) for x in ((("head", 2 * p), 13, 0), (("head", 2 * p + 1), 13, 0), (("out", p), 0, KD))]
            + [x for t, (_, n) in enumerate(THIRDS) for x in ((("gu", 1, t), n, n), (("dn", 1, t), 0, KD))]
        ):
            runs[name] = (ra, rd)
            ra, rd = ra + a, rd + d
        N_ROW_LOADS, G_FFN, FULL_END = 13, (5, 43), 44
        X_BEFORE = (0, 0, 24, 40, 64)
        L_OF = (0, 0, 1, 1)

        def raw_count(n, ada=False):
            if ada:
                before = 0 if n < 4 * ADA_FIRST else N_OUT_EVEN
            else:
                before = 4 * ADA_FIRST if n < N_OUT_EVEN else N_ADA
            return 16 * ((n + before) // 4 + 1)

        def ada_rows(g):
            return (rows_early if g < ADA_ATT else rows_late)[:, g % 2, :]

        def mod_at(layer, part):
            return layer * 48 + part * KD

        block = ctx.enter_context(nc.Block())


        @block.tensor
        def _(pe):
            def open_job(name):
                i = jobs.index[name]
                if i >= 4:
                    pe.wait_ge(emptied[jobs.engine[i - 4]], jobs.nth[i - 4])
                return Jp[i % 4]

            def close(mm):
                mm.then_inc(job_done, 1)

            def turn(out, src, n=P):
                return pe.transpose(out, src, ident[0:n, 0:n])

            pe.wait_ge(x_loaded, 80)
            bank = open_job("xs")
            for k in range(KD):
                mm = turn(bank[:, k * NB:(k + 1) * NB], xsn[:, k * P:(k + 1) * P], NB)
            close(mm)
            for k in range(KD):
                bank = open_job(("xT", k))
                for b in range(TB):
                    mm = turn(bank[:, b * P:(b + 1) * P], xn[:, b, k * P:(k + 1) * P])
                close(mm)
            bank = open_job("cT")
            pe.wait_ge(c_silu, 1)
            for k in range(KD):
                mm = turn(bank[:, k * 9:(k + 1) * 9], cn_silu[:, k * P:(k + 1) * P], 9)
            close(mm)
            bank = open_job("vec")
            pe.wait_ge(rows_loaded, 16 * N_ROW_LOADS)
            turn(bank[:, 0:V_ROWS], rows_v[:], V_ROWS)
            turn(bank[:, V_ADAB:V_ADAB + N_ADA], rows_a[:], N_ADA)
            close(turn(bank[:, V_CW:V_END], rows_c[:], CW * 4))
            for g in range(2):
                bank = open_job(("sc", g))
                for t in range(4):
                    mm = turn(bank[:, t * 120:(t + 1) * 120], rows_s[:, g, t * P:(t + 1) * P], 120)
                close(mm)

            def norm(i):
                banks = [open_job(("ss", i, c)) for c in range(2)]
                for k in range(KD):
                    pe.wait_ge(sq_ready, KD * i + k + 1)
                    for c in range(2):
                        mm = pe.matmul(banks[c][:, 0:CH], con[:, C_MEAN:C_MEAN + P],
                                       sq[:, k % 2, c * CH:(c + 1) * CH], start=k == 0, stop=k == KD - 1)
                        if k == KD - 1:
                            close(mm)
                    if k < KD - 1:
                        mm.then_inc(sq_used, 1)

            norm(0)

            def ada_block(m):
                g, j = m // 4, m % 4
                if j == 0 and g >= 2:
                    pe.wait_ge(ada_taken, g - 1)
                pe.wait_ge(raw_loaded[j], raw_count(m, ada=True))
                for k in range(KD):
                    mm = pe.matmul(Gp[g % 2][0:9, 0, j * P:(j + 1) * P], cT[:, k, :], raw[:, j, k, :],
                                   start=k == 0, stop=k == KD - 1)
                mm.then_inc(ada_used, 1)

            def ada_turn(g):
                bank = open_job(("ada", g))
                pe.wait_ge(ada_taken, g + 1)
                for j in range(4):
                    mm = turn(bank[:, j * 9:(j + 1) * 9], ada_rows(g)[:, j * P:(j + 1) * P], 9)
                close(mm)

            def ada_groups(first, end):
                for g in range(first, end):
                    for j in range(4):
                        ada_block(4 * g + j)
                    if g > first:
                        ada_turn(g - 1)
                ada_turn(end - 1)

            wait_emptied(pe, "cT")
            ada_groups(0, ADA_FIRST)

            def product(j, slot, kt, hi, lo):
                for c in range(2):
                    cols = slice(c * CH, (c + 1) * CH)
                    for k in range(kt):
                        for p, (w, x) in enumerate(((w_lo, hi), (w_hi, lo), (w_hi, hi))):
                            mm = pe.matmul(Gp[slot][:, c, 0:CH], w[:, j, k, :], x[:, k, cols],
                                           start=k == 0 and p == 0, stop=k == kt - 1 and p == 2)
                return mm

            def run(name, n0, bodies, kt, hi, lo, engine):
                base_a, base_d = runs[name]
                pe.wait_ge(slot_act, base_a)
                if base_d:
                    pe.wait_ge(slot_dve, base_d)

                def body(i):
                    for j in range(4):
                        pe.wait_ge(lo_ready, n0 + 4 * i + j + 1)
                        if engine == "gu":
                            s, base = (slot_act, base_a) if j % 2 == 0 else (slot_dve, base_d)
                            pe.wait_ge(s, base + 2 * i + j // 2)
                        elif engine == "A":
                            pe.wait_ge(slot_act, base_a + 4 * i + j - 1)
                        else:
                            pe.wait_ge(slot_dve, base_d + 4 * i + j - 1)
                        product(j, j % 2, kt, hi, lo).then_inc(block_done, 1)

                with pe.Fori(0, bodies) as i:
                    body(i)

            def inputs_ready(i):
                pe.wait_ge(h_ready, KD * (i + 1))

            inputs_ready(0)
            bank = open_job("fl")
            pe.wait_ge(lf_dve, 1)
            for b in range(5):
                cols = slice(0, P) if b == 0 else slice(NB + (b - 1) * P, NB + b * P)
                for k in range(KD):
                    for p, (x, w) in enumerate(((H_lo, wf_hi), (H_hi, wf_lo), (H_hi, wf_hi))):
                        mm = pe.matmul(bank[:, b * 8:(b + 1) * 8], x[:, k, cols], w[:, k, :],
                                       start=k == 0 and p == 0, stop=k == KD - 1 and p == 2)
            close(mm)
            run("in_even", N_IN_EVEN, 5, KD, H_hi, H_lo, "A")

            pe.wait_ge(slot_act, runs["in_even"][0] + 20)
            ada_groups(ADA_FIRST, ADA_ATT)

            for t in range(4):
                pe.wait_ge(cv_ready, t + 1)
                for c in range(2):
                    bank = open_job(("cm", t, c))
                    close(pe.matmul(bank[:, 0:CH], con[:, C_B64:C_B64 + P], CV[:, t, c * CH:(c + 1) * CH],
                                    start=True, stop=True))
            bank = open_job("cpo")
            for t in range(4):
                mm = turn(bank[0:CW - 1, t * P:(t + 1) * P], UP[:, t, L:L + CW - 1])
            close(mm)
            bank = open_job("cso")
            for t in range(4):
                mm = turn(bank[0:NB, t * P:(t + 1) * P], US[:, t, :, CW - 1])
            close(mm)

            def rows_of(name, src):
                bank = open_job(name)
                for t in range(4):
                    mm = turn(bank[0:NB, t * P:(t + 1) * P], src[:, t, 0:NB])
                close(mm)

            rows_of("qs", QT)
            wait_emptied(pe, "qs")
            for b in range(NB):
                bank = open_job(("qb", b))
                close(pe.matmul(bank[:, :], con[0:NB, C_ID + b:C_ID + b + 1].broadcast_to((NB, P)), qsn[:],
                                start=True, stop=True))
            for t in range(4):
                pe.wait_ge(conv_act, t + 1)
                for c in range(2):
                    bank = open_job(("cq", t, c))
                    close(pe.matmul(bank[:, 0:CH], con[:, C_B64:C_B64 + P], sq4[:, t, c * CH:(c + 1) * CH],
                                    start=True, stop=True))

            bank = open_job("cum")
            pe.wait_ge(lf_dve, 3)
            for q in range(TB):
                for b in range(q + 1):
                    mm = pe.matmul(bank[:, q * 8:(q + 1) * 8], con[:, C_TRI:C_TRI + P] if b == q else ones,
                                   lf[:, 1 + b, :], start=b == 0, stop=b == q)
            close(mm)
            wait_emptied(pe, "cum")
            bank = open_job("cumT")
            for q in range(TB):
                mm = turn(bank[0:8, q * P:(q + 1) * P], cumul[:, q, :])
            close(mm)
            for name, src in (("kn", KT), ("vn", VT)):
                for b in range(TB):
                    bank = open_job((name, b))
                    for t in range(4):
                        mm = turn(bank[:, t * P:(t + 1) * P], src[:, t, NB + b * P:NB + (b + 1) * P])
                    close(mm)
            rows_of("ks", KT)
            rows_of("vs", VT)

            def cum_rows(h):
                bank = open_job(("ckb", h))
                close(pe.matmul(bank[:, :], con[0:8, C_ID + h:C_ID + h + 1].broadcast_to((8, P)), cum8[:],
                                start=True, stop=True))

            def scores(h, q):
                bank = open_job(("s", h, q))
                rows = slice(HD * (h % 2), HD * (h % 2) + HD)
                n = (q + 1) * P
                pe.matmul(bank[:, 0:n], QT[rows, h // 2, NB + q * P:NB + (q + 1) * P],
                          KT[rows, h // 2, NB:NB + n], start=True, stop=False)
                close(pe.matmul(bank[:, n - P:n], ident, con[:, C_NEG:C_NEG + P], start=False, stop=True))

            wait_emptied(pe, "cumT")
            cum_rows(0)
            for q in range(TB):
                scores(0, q)
            for h in range(HEADS):
                if h + 1 < HEADS:
                    cum_rows(h + 1)
                for q in range(TB):
                    bank = open_job(("pt", h, q))
                    pe.wait_ge(p_ready, h * TB + q + 1)
                    for b in range(q + 1):
                        mm = turn(bank[:, b * P:(b + 1) * P], SS[:, q, b * P:(b + 1) * P])
                    close(mm)
                    if h + 1 < HEADS:
                        scores(h + 1, q)
                    x = h * TB + q
                    for m in range(4 * ADA_ATT + 2 * x, 4 * ADA_ATT + 2 * x + 2):
                        ada_block(m)
                    if ada_turned(x) is not None:
                        ada_turn(ada_turned(x))
                bank = open_job(("o", h))
                wait_emptied(pe, ("pt", h, TB - 1))
                rows = slice(HD * (h % 2), HD * (h % 2) + HD)
                for b in range(TB):
                    mm = pe.matmul(bank[rows, b * P:L], VN[:, b, h * HD:(h + 1) * HD], PTS[:, b, b * P:L],
                                   start=b == 0, stop=b == TB - 1)
                close(mm)

            ada_turn(N_ADA // 4 - 1)

            bank = open_job("lt")
            pe.wait_ge(lg_loaded, 16)
            for h in range(HEADS):
                mm = turn(bank[:, h * NPG:(h + 1) * NPG], lg[:].rearrange("g (t h) -> g t h", h=HEADS)[:, :, h], NPG)
            close(mm)
            bank = open_job("cc")
            pe.wait_ge(samp_dve, 2)
            pe.matmul(bank[:, :], con[:, C_TRI:C_TRI + P], LT[:].rearrange("p h b g -> p (h b g)"),
                      start=True, stop=False)
            close(pe.matmul(bank[:, :], ones, EX[:].rearrange("p h b g -> p (h b g)"), start=False, stop=True))
            bank = open_job("cl")
            pe.matmul(bank[:, 0:64], ones, small[:, 0, :], start=True, stop=False)
            close(pe.matmul(bank[:, 0:64], ones[0:NB, :], small[0:NB, 1, :], start=False, stop=True))
            bank = open_job("sn")
            for h in range(HEADS):
                c = C_B64 + HD * (h % 2)
                mm = pe.matmul(bank[:, h * NB:(h + 1) * NB], con[:, c:c + 1].broadcast_to((P, P)),
                               small[:, 3, (h // 2) * NB:(h // 2 + 1) * NB], start=True, stop=True)
            close(mm)
            bank = open_job("mt")
            pe.wait_ge(samp_dve, 3)
            close(turn(bank[0:64, 0:P], small[:, 5, :]))
            bank = open_job("mb")
            pe.wait_ge(samp_dve, 4)
            close(pe.matmul(bank[:, 0:64], ones[0:64, :], small[0:64, 7, :], start=True, stop=True))
            bank = open_job("dn")
            pe.wait_ge(samp_dve, 6)
            close(pe.matmul(bank[:, 0:64], ones, small[:, 6, :], start=True, stop=True))
            pe.wait_ge(samp_dve, 7)
            turned = open_job("ov")

            def gather(b):
                pe.wait_ge(vm_ready, b + 1)
                for t in range(4):
                    mm = pe.matmul(turned[:, t * NB + b:t * NB + b + 1], vm[:, b % 2, t * P:(t + 1) * P],
                                   ones[0:HEADS, 0:1], start=True, stop=True)
                return mm

            for b in range(NB):
                if b >= 4:
                    pe.wait_ge(vm_ready, b - 3)
                for g in range(8):
                    n = b * 8 + g
                    pe.wait_ge(v_page[n % 4], 16 * (n // 4 + 1))
                    mm = pe.matmul(Gp[b // 2 % 2][0:HEADS, b % 2, :], SC[:, :, b, g], vp[:, n % 4, :],
                                   start=g == 0, stop=g == 7)
                    mm.then_inc(v_used, 1)
                if b >= 1:
                    gather(b - 1).then_inc(vm_used, 1)
            close(gather(NB - 1))

            pe.wait_ge(g_ready, 5)
            wait_emptied(pe, ("o", HEADS - 1))
            run("out_even", N_OUT_EVEN, 2, KD, G_hi, G_lo, "D")

            def ffn(layer, i):
                norm(i)
                inputs_ready(i)
                for t, ((_, kt), (n0, n1)) in enumerate(zip(THIRDS, ffn_starts(layer))):
                    run(("gu", layer, t), n0, kt // 2, KD, H_hi, H_lo, "gu")
                    pe.wait_ge(g_ready, G_FFN[layer] + sum(x for _, x in THIRDS[:t + 1]))
                    run(("dn", layer, t), n1, 2, kt, G_hi, G_lo, "D")

            ffn(0, 1)

            norm(2)
            inputs_ready(2)
            for h in range(RH):
                n0 = N_ODD + 12 * h + (h // 2) * KD
                run(("head", h), n0, 3, KD, H_hi, H_lo, "A")
                pe.wait_ge(slot_act, runs[("head", h)][0] + 12)
                for b in range(TB):
                    bank = open_job(("rvn", h, b))
                    for e in range(4):
                        mm = turn(bank[:, e * P:(e + 1) * P], RVT[:, e, NB + b * P:NB + (b + 1) * P])
                    close(mm)
                rows_of(("rvs", h), RVT)
                pe.wait_ge(rope_ready, 4 * h + 4)
                for b in range(TB):
                    bank = open_job(("rkn", h, b))
                    for d in range(2):
                        mm = turn(bank[:, d * P:(d + 1) * P], QKR[:, 2 + d, NB + b * P:NB + (b + 1) * P])
                    close(mm)
                for j in range(TB):
                    bank = open_job(("ra", h, j))
                    for d in range(2):
                        mm = pe.matmul(bank[:, 0:L - j * P], QKR[:, 2 + d, NB + j * P:NB + (j + 1) * P],
                                       QKR[:, d, NB + j * P:T], start=d == 0, stop=d == 1)
                    close(mm)
                wait_emptied(pe, ("rkn", h, TB - 1))
                for d in range(2):
                    bank = open_job(("rst", h, d))
                    for b in range(TB):
                        mm = pe.matmul(bank[:, :], KDN[:, b, d * P:(d + 1) * P], RVN[:, b, :],
                                       start=b == 0, stop=b == TB - 1)
                    close(mm)
                wait_emptied(pe, ("ra", h, TB - 1))
                for e in range(4):
                    bank = open_job(("ro", h, e))
                    for j in range(TB):
                        mm = pe.matmul(bank[:, j * P:L], RVN[:, j, e * P:(e + 1) * P], AD[:, j, 0:L - j * P],
                                       start=j == 0, stop=j == TB - 1)
                    close(mm)
                for b in range(NB + 1):
                    if b < NB:
                        bank = open_job(("vb", h, b))
                        close(pe.matmul(bank[:, :], con[0:NB, C_ID + b:C_ID + b + 1].broadcast_to((NB, P)), vsn[:],
                                        start=True, stop=True))
                    if b >= 1:
                        g = h * NB + b - 1
                        wait_emptied(pe, ("vb", h, b - 1))
                        for e in range(4):
                            for d in range(2):
                                mm = pe.matmul(Gp[0][:, 0, e * NB + b - 1:e * NB + b],
                                               st[:, g % 2, d, e * P:(e + 1) * P], QKR[:, d, b - 1:b],
                                               start=d == 0, stop=d == 1)
                        mm.then_inc(st_used, 1)
                pe.wait_ge(slot_act, runs[("head", h)][0] + 13)
                for c in range(2):
                    bank = open_job(("rm", h, c))
                    for e in range(4):
                        mm = pe.matmul(bank[:, 0:CH], con[:, C_M512:C_M512 + P], RVT[:, e, c * CH:(c + 1) * CH],
                                       start=e == 0, stop=e == 3)
                    close(mm)
                pe.wait_ge(ret_act, 5 * h + 4)
                for c in range(2):
                    bank = open_job(("rv", h, c))
                    for e in range(4):
                        mm = pe.matmul(bank[:, 0:CH], con[:, C_M512:C_M512 + P], RSQ[:, e, c * CH:(c + 1) * CH],
                                       start=e == 0, stop=e == 3)
                    close(mm)
                if h % 2:
                    pe.wait_ge(g_ready, 5 + 22 + 4 * (h + 1))
                    run(("out", h // 2), n0 + 12, 2, KD, G_hi, G_lo, "D")
            ffn(1, 3)

            norm(4)
            pe.wait_ge(full_ready, FULL_END)
            for b in range(TB):
                for f in range(2):
                    bank = open_job(("y", b, f))
                    for k in range(4):
                        mm = turn(bank[:, k * P:(k + 1) * P], YT[:, 4 * f + k, NB + b * P:NB + (b + 1) * P])
                    close(mm)
            for f in range(2):
                bank = open_job(("ys", f))
                for k in range(4):
                    mm = turn(bank[0:NB, k * P:(k + 1) * P], YT[:, 4 * f + k, 0:NB])
                close(mm)

        @block.scalar
        def _(act):
            n = Tally(act)

            def f(out, in_, func, **kw):
                return nc.scalar.activation(out, in_, func, **kw)

            rows = [(rows_v[V_MIXG:V_MIXG + 16], A["norm_mix_g"].rearrange("l (k p) -> (l k) p", p=P)),
                    (rows_v[V_FFNG:V_FFNG + 16], A["norm_ffn_g"].rearrange("l (k p) -> (l k) p", p=P)),
                    (rows_v[V_FING:V_FING + 8], A["final_norm_g"].rearrange("(k p) -> k p", p=P)),
                    (rows_v[V_CB:V_CB + 4], A["conv_b"][0].rearrange("(k p) -> k p", p=P)),
                    (rows_v[V_CG:V_CG + 4], A["conv_norm_g"][0].rearrange("(k p) -> k p", p=P)),
                    (rows_v[V_CNB:V_CNB + 4], A["conv_norm_b"][0].rearrange("(k p) -> k p", p=P)),
                    (rows_v[V_RG:V_RG + 16], A["ret_norm_g"][0].rearrange("(k p) -> k p", p=P)),
                    (rows_a[:], A["ada_b"].rearrange("l (k p) -> (l k) p", p=P)),
                    (rows_c[:], A["conv_w"][0].rearrange("w (k p) -> (w k) p", p=P)),
                    (rows_s[:, 0, :], A["state_conv"][0, 0:4].rearrange("b w c -> (b w) c")),
                    (rows_s[:, 1, :], A["state_conv"][0, 4:8].rearrange("b w c -> (b w) c")),
                    (wf[:], A["w_in_even"][0][:, 1536:1544].rearrange("(k p) m -> p k m", p=P)),
                    (bfg[:], A["b_forget"].broadcast_to((P, HEADS)))]
            assert len(rows) == N_ROW_LOADS
            for dst, src in rows:
                act.dma_start(dst, src).then_inc(rows_loaded, 16)
            store(act, A["conv_sample"][0, :, 0:CW - 2, :], A["state_conv"][0, :, 1:CW - 1, :])
            act.wait_ge(x_loaded, 80)
            n.up(f(cn_silu[:], cn[:], ACT.Silu), c_silu)

            def squares(i):
                for k in range(KD):
                    if i == 0:
                        wait_emptied(act, ("xT", k))
                    else:
                        act.wait_ge(x_ready, X_BEFORE[i] + k + 1)
                    if k >= 2:
                        act.wait_ge(sq_used, (KD - 1) * i + k - 1)
                    n.up(f(sq[:, k % 2, :], X[:, k, :], ACT.Square), sq_ready)
                act.wait_ge(var_ready, i + 1)
                n.up(f(rstd[:], rstd[:], ACT.Sqrt), rstd_ready)

            def modulate(i):
                shift = mod_at(L_OF[i], 0 if i % 2 == 0 else 3)
                for k in range(KD):
                    act.wait_ge(scaled_ready, KD * i + k + 1)
                    if k >= 2:
                        act.wait_ge(h_ready, KD * i + k - 1)
                    n.up(f(full[:, k % 2, NB:T], scaled[:, k % 2, NB:T], ACT.Identity,
                           bias=mod[:, shift + k, 0:1], scale=coef[:, k, 0:1]), full_ready)
                    n.own(full_ready)
                    n.up(f(H_hi[:, k, NB:T], full[:, k % 2, NB:T], ACT.Copy), hh_ready)

            def split_hi(j, m, kt):
                act.wait_ge(raw_loaded[j], raw_count(m) if isinstance(m, int) else m[0])
                if not isinstance(m, int):
                    act.wait_ge(block_done, m[1])
                elif m >= 4:
                    act.wait_ge(block_done, m - 3)
                f(w_hi[:, j, 0:kt, :], raw[:, j, 0:kt, :], ACT.Copy).then_inc(hi_ready, 1)

            def ahead(m):
                if m < N_BLOCKS:
                    split_hi(m % 4, m, k_tiles(m))

            def product_done(m):
                act.wait_ge(block_done, m + 1)

            def slot(j):
                return Gp[j % 2][:, :, 0:CH]

            def halves(ap):
                return ap.rearrange("p (c n) -> p c n", c=2)

            def take_rows(g):
                act.wait_ge(ada_used, 4 * g + 4)
                if g >= 2:
                    wait_job(act, ("ada", g - 2))
                n.up(f(ada_rows(g), Gp[g % 2][0:9, 0, :], ACT.Copy), ada_taken)

            squares(0)
            for g in range(ADA_FIRST):
                take_rows(g)
            modulate(0)
            act.wait_ge(rows_loaded, 16 * N_ROW_LOADS)
            n.up(f(wf_hi[:], wf[:], ACT.Copy), lf_act)
            for i in range(2):
                n.up(f(small[:, i, 0:1], one_col, ACT.Copy), slot_act)
            ahead(0)
            ahead(1)
            for m in range(20):
                if m + 2 < N_OUT_EVEN:
                    ahead(m + 2)
                product_done(m)
                kind, j = m // 4, m % 4
                if kind == 1:
                    if j >= 2:
                        act.wait_ge(u_ready, j - 1)
                    n.up(f(halves(gate[:, j % 2, :]), slot(m), ACT.Sigmoid), slot_act)
                else:
                    if kind == 4:
                        act.wait_ge(u_ready, 4)
                    n.up(f(halves((AT, None, QT, KT, VT)[kind][:, j, :]), slot(m), ACT.Copy), slot_act)
                if m == 1:
                    act.wait_ge(lf_dve, 2)
                    n.up(f(lf[:], lf[:], ACT.Exp), lf_act)
                    n.own(lf_act)
                    n.up(f(lf[:], lf[:], ACT.Ln, bias=one_col), lf_act)

            stage = [0, 0]
            turn_ = [0]

            def stage_out(name, part, width, dst):
                s = turn_[0] % 2
                turn_[0] += 1
                wait_job(act, name)
                if stage[s]:
                    act.wait_ge(stage_stored[s], 16 * stage[s])
                bank = Jp[jobs.bank(name)]
                n.up(f(kn_out[0:part, s, 0:width], bank[0:part, 0:width], ACT.Copy), emptied["A"])
                n.own(emptied["A"])
                store(act, dst, kn_out[0:part, s, 0:width], stage_stored[s])
                stage[s] += 1

            for g in range(ADA_FIRST, ADA_ATT):
                take_rows(g)
            act.wait_ge(lf_dve, 3)
            store(act, A["logf_prompt"][0, 0].rearrange("(b p) h -> p b h", p=P), lf[:, 1:5, :])
            store(act, A["logf_sample"][0, :, 0, :], lf[0:NB, 0, :])
            act.wait_ge(cv_ready, 4)
            stage_out("cpo", CW - 1, 512, A["conv_prompt"][0, 0])
            stage_out("cso", NB, 512, A["conv_sample"][0, :, CW - 2, :])
            wait_job(act, "qs")
            n.up(f(qsn[:], Jp[jobs.bank("qs")][0:NB, :], ACT.Copy), emptied["A"])
            for b in range(NB):
                wait_job(act, ("qb", b))
                n.up(f(QB[:, b, :], Jp[jobs.bank(("qb", b))][:, :], ACT.Copy, scale=FOX_SCALE), emptied["A"])
            for t in range(4):
                wait_emptied(act, ("cm", t, 1))
                n.up(f(sq4[:, t, :], CV[:, t, :], ACT.Square), conv_act)
            act.wait_ge(conv_var, 1)
            n.up(f(CR[:], CR[:], ACT.Sqrt), conv_act)
            for t in range(4):
                act.wait_ge(conv_normed, t + 1)
                if t >= 2:
                    act.wait_ge(g_ready, t - 1)
                n.up(f(full[:, t % 2, :], CV[:, t, :], ACT.Silu, bias=vec[:, V_CNB + t:V_CNB + t + 1],
                       scale=vec[:, V_CG + t:V_CG + t + 1]), full_ready)
                n.own(full_ready)
                n.up(f(G_hi[:, 4 + t, :], full[:, t % 2, :], ACT.Copy), ghi_ready)
            wait_job(act, "cumT")
            n.up(f(cum8[:], Jp[jobs.bank("cumT")][0:8, :], ACT.Copy), emptied["A"])
            for b in range(TB):
                stage_out(("kn", b), P, 512, A["k_prompt"][0, 0, b * P:(b + 1) * P].rearrange("p h d -> p (h d)"))
            for b in range(TB):
                wait_job(act, ("vn", b))
                n.up(f(VN[:, b, :], Jp[jobs.bank(("vn", b))][:, :], ACT.Copy), emptied["A"])
                n.own(emptied["A"])
                store(act, A["v_prompt"][0, 0, b * P:(b + 1) * P].rearrange("p h d -> p (h d)"), VN[:, b, :], v_stored)
            stage_out("ks", NB, 512, A["k_sample"][0, :, 0].rearrange("p h d -> p (h d)"))
            stage_out("vs", NB, 512, A["v_sample"][0, :, 0].rearrange("p h d -> p (h d)"))

            def row_of_sums(h):
                wait_job(act, ("ckb", h))
                if h >= 2:
                    wait_emptied(act, ("s", h - 2, TB - 1))
                n.up(f(ckb[:, h % 2, :], Jp[jobs.bank(("ckb", h))][:, :], ACT.Copy), emptied["A"])

            def exps(h, q):
                x = h * TB + q
                act.wait_ge(max_ready, x + 1)
                w = SS[:, q, 0:(q + 1) * P]
                n.up(f(w, w, ACT.Exp, bias=nm[:, x:x + 1], accum_out=rs[:, x:x + 1]), exp_ready)

            row_of_sums(0)
            for q in range(TB):
                exps(0, q)
            for h in range(HEADS):
                if h + 1 < HEADS:
                    row_of_sums(h + 1)
                if h >= 1:
                    wait_job(act, ("o", h - 1))
                for q in range(TB):
                    wait_job(act, ("pt", h, q))
                    n.up(f(PTS[:, 0:q + 1, q * P:(q + 1) * P],
                           Jp[jobs.bank(("pt", h, q))][:, 0:(q + 1) * P].rearrange("p (b c) -> p b c", c=P),
                           ACT.Copy), emptied["A"])
                    if h + 1 < HEADS:
                        exps(h + 1, q)
                    if q % 2:
                        take_rows(ADA_ATT + (h * TB + q) // 2)
                wait_job(act, ("o", h))
                rows_ = slice(HD * (h % 2), HD * (h % 2) + HD)
                n.up(f(G_hi[rows_, h // 2, NB:T], Jp[jobs.bank(("o", h))][rows_, :], ACT.Copy), ohi_ready)

            wait_job(act, "lt")
            n.up(f(LT[:].rearrange("p h b g -> p (h b g)"), Jp[jobs.bank("lt")][:, :], ACT.Copy), emptied["A"])
            wait_job(act, "cl")
            n.up(f(small[:, 2, :], Jp[jobs.bank("cl")][:, 0:64], ACT.Copy), emptied["A"])
            act.wait_ge(samp_dve, 5)
            n.up(f(small[:, 4, :], small[:, 4, :], ACT.Exp), samp_act)
            n.up(f(SC[:], SC[:], ACT.Exp), samp_act)

            def gates(layer):
                for t, ((_, kt), (n0, n1)) in enumerate(zip(THIRDS, ffn_starts(layer))):
                    base_a, base_d = runs[("gu", layer, t)]
                    g0 = G_FFN[layer] + sum(x for _, x in THIRDS[:t])

                    def body(i, n0=n0, base_d=base_d, g0=g0):
                        for j in range(4):
                            m = n0 + 4 * i + j + 2
                            jj = (j + 2) % 4
                            if isinstance(i, int):
                                ahead(m)
                            else:
                                split_hi(jj, (16 * (n0 // 4 + N_ADA // 4 + 1 + (j + 2) // 4) + 16 * i, m - 3), KD)
                            if j % 2 == 0:
                                act.wait_ge(block_done, n0 + 4 * i + j + 1)
                                act.wait_ge(slot_dve, base_d + 2 * i + j // 2 - 1)
                                f(halves(gate[:, j // 2, :]), slot(0), ACT.Silu).then_inc(slot_act, 1)
                            else:
                                act.wait_ge(slot_dve, base_d + 2 * i + j // 2 + 1)
                                f(G_hi[:, ds(2 * i + j // 2, 1), :].rearrange("p o n -> p (o n)"),
                                  full[:, j // 2, :], ACT.Copy).then_inc(ghi_ready, 1)

                    with act.Fori(0, kt // 2 - 1) as i:
                        body(i)
                    body(kt // 2 - 1)
                    for q in range(KD):
                        ahead(n1 + q + 2)

            ahead(N_OUT_EVEN)
            ahead(N_OUT_EVEN + 1)
            for q in range(KD):
                ahead(N_OUT_EVEN + q + 2)
            squares(1)
            modulate(1)
            gates(0)
            squares(2)
            modulate(2)

            sto = [0, 0]
            for h in range(RH):
                n0 = N_ODD + 12 * h + (h // 2) * KD
                for q in range(12):
                    ahead(n0 + q + 2)
                    product_done(n0 + q)
                    src = slot(q)
                    if q < 2:
                        o = f(halves(QK[:, q, :]), src, ACT.Copy)
                    elif q < 4:
                        o = f(halves(QK[:, q, :]), src, ACT.Copy, scale=DK ** -0.5)
                    elif q < 8:
                        o = f(halves(RVT[:, q - 4, :]), src, ACT.Copy)
                    else:
                        o = f(halves(GS[:, q - 8, :]), src, ACT.Silu)
                    n.up(o, slot_act)
                for b in range(TB):
                    wait_job(act, ("rvn", h, b))
                    n.up(f(RVN[:, b, :], Jp[jobs.bank(("rvn", h, b))][:, :], ACT.Copy), emptied["A"])
                wait_job(act, ("rvs", h))
                act.wait_ge(rope_ready, 4 * h + 4)
                n.up(f(vsn[:], Jp[jobs.bank(("rvs", h))][0:NB, :], ACT.Copy), emptied["A"])
                for b in range(TB):
                    wait_job(act, ("rkn", h, b))
                    c0 = C_KDEC + b * RH + h
                    n.up(f(KDN[:, b, :], Jp[jobs.bank(("rkn", h, b))][:, 0:DK], ACT.Copy,
                           scale=con[:, c0:c0 + 1]), emptied["A"])
                for d in range(2):
                    wait_job(act, ("rst", h, d))
                    if sto[d]:
                        act.wait_ge(stage_stored[d], 16 * (stage[d] + sto[d]))
                    n.up(f(so[:, d, :], Jp[jobs.bank(("rst", h, d))][:, :], ACT.Copy), emptied["A"])
                    n.own(emptied["A"])
                    store(act, A["ret_prompt"][0, 0, h, d * P:(d + 1) * P, :], so[:, d, :], stage_stored[d])
                    sto[d] += 1
                for e in range(4):
                    wait_job(act, ("ro", h, e))
                    n.up(f(RVT[:, e, NB:T], Jp[jobs.bank(("ro", h, e))][:, :], ACT.Copy), emptied["A"])
                for b in range(NB + 1):
                    g = h * NB + b
                    if b < NB:
                        act.wait_ge(st_loaded[g % 2], 16 * (g // 2 + 1))
                        n.up(f(st[:, g % 2], st[:, g % 2], ACT.Copy, scale=GAMMA[h]), st_scaled)
                    if b >= 1:
                        wait_emptied(act, ("vb", h, b - 1))
                        store(act, A["ret_sample"][0, b - 1, h].rearrange("(d p) e -> p d e", p=P),
                              st[:, (g - 1) % 2], st_stored[(g - 1) % 2])
                act.wait_ge(st_used, NB * (h + 1))
                n.up(f(RVT[:, :, 0:NB], Gp[0][:, 0, 0:4 * NB].rearrange("p (e b) -> p e b", b=NB), ACT.Copy), slot_act)
                for e in range(4):
                    wait_emptied(act, ("rm", h, 1))
                    n.up(f(RSQ[:, e, :], RVT[:, e, :], ACT.Square), ret_act)
                act.wait_ge(ret_dve, h + 1)
                n.up(f(rsd[:], rsd[:], ACT.Sqrt), ret_act)
                for e in range(4):
                    act.wait_ge(ret_gated, 4 * h + e + 1)
                    n.up(f(G_hi[:, 4 * (h % 2) + e, :], GS[:, e, :], ACT.Copy), ghi_ready)
                if h % 2:
                    for q in range(KD):
                        ahead(n0 + 12 + q + 2)
            squares(3)
            modulate(3)
            gates(1)
            squares(4)
            for k in range(KD):
                act.wait_ge(scaled_ready, KD * 4 + k + 1)
                n.up(f(YT[:, k, :], scaled[:, k % 2, :], ACT.Copy, scale=vec[:, V_FING + k:V_FING + k + 1]),
                     full_ready)
            used = [stage[s] + sto[s] for s in range(2)]
            turn = 0
            for name, part, dst in (
                [(("y", b, x), P, A["y_prompt"][0, b * P:(b + 1) * P, x * 512:(x + 1) * 512]) for b in range(TB) for x in range(2)]
                + [(("ys", x), NB, A["y_sample"][:, 0, x * 512:(x + 1) * 512]) for x in range(2)]
            ):
                s = turn % 2
                turn += 1
                wait_job(act, name)
                act.wait_ge(stage_stored[s], 16 * used[s])
                n.up(f(yo[0:part, s, :], Jp[jobs.bank(name)][0:part, :], ACT.Copy), emptied["A"])
                n.own(emptied["A"])
                store(act, dst, yo[0:part, s, :], stage_stored[s])
                used[s] += 1

        @block.vector
        def _(dve):
            n = Tally(dve)
            v = nc.vector

            def step(instruction):
                n.up(instruction, dve_step)
                n.own(dve_step)

            def bank_of(name):
                wait_job(dve, name)
                return Jp[jobs.bank(name)]

            def lo(m, j=None, kt=KD):
                if isinstance(m, int):
                    if m >= N_BLOCKS:
                        return
                    j, kt = m % 4, k_tiles(m)
                dve.wait_ge(hi_ready, m + 1)
                v.tensor_tensor(w_lo[:, j, 0:kt, :], raw[:, j, 0:kt, :], w_hi[:, j, 0:kt, :].bitcast(f32),
                                ALU.subtract).then_inc(lo_ready, 1)

            def minus_hi(out, whole, hi):
                return v.tensor_tensor(out, whole, hi.bitcast(f32), ALU.subtract)

            n.up(v.memset(full_s[:, 0, 0:1], 0.0), slot_dve)
            bank = bank_of("xs")
            n.up(v.tensor_copy(X[:, :, 0:NB], bank[:, 0:KD * NB].rearrange("p (k b) -> p k b", b=NB)), emptied["D"])
            for k in range(KD):
                n.up(v.tensor_copy(X[:, k, NB:T], bank_of(("xT", k))[:, :]), emptied["D"])
            n.up(v.tensor_copy(cT[:].rearrange("p k b -> p (k b)"), bank_of("cT")[:, 0:KD * 9]), emptied["D"])
            n.up(v.tensor_copy(vec[:], bank_of("vec")[:, 0:V_END]), emptied["D"])
            for g in range(2):
                bank = bank_of(("sc", g))
                for t in range(4):
                    o = v.tensor_copy(US[:, t, 4 * g:4 * g + 4, 0:CW - 1],
                                      bank[:, t * 120:(t + 1) * 120].rearrange("p (b w) -> p b w", b=4))
                n.up(o, emptied["D"])

            def rstd_parts(i):
                for c in range(2):
                    n.up(v.tensor_scalar(rstd[:, c * CH:(c + 1) * CH], bank_of(("ss", i, c))[:, 0:CH],
                                         EPS, None, ALU.add), emptied["D"])
                n.own(emptied["D"])
                n.up(v.reciprocal(rstd[:], rstd[:]), var_ready)

            def scale_x(i, k, full_before):
                if k >= 2:
                    dve.wait_ge(full_ready, full_before + k - 1)
                n.up(v.tensor_tensor(scaled[:, k % 2, :], X[:, k, :], rstd[:], ALU.mult), scaled_ready)

            def modulate(i):
                layer, second = L_OF[i], i % 2
                shift, scale = mod_at(layer, 3 * second), mod_at(layer, 3 * second + 1)
                g = (V_FFNG if second else V_MIXG) + layer * KD
                step(v.scalar_tensor_tensor(coef[:], mod[:, scale:scale + KD, :], 1.0,
                                            vec[:, g:g + KD].unsqueeze(2).broadcast_to((P, KD, 9)),
                                            ALU.add, ALU.mult))
                dve.wait_ge(rstd_ready, i + 1)
                if i == 1:
                    dve.wait_ge(v_stored, 16 * TB)
                step(v.tensor_tensor(full_s[:], X[:, :, 0:NB],
                                     rstd[:, 0:NB].unsqueeze(1).broadcast_to((P, KD, NB)), ALU.mult))
                step(v.tensor_tensor(full_s[:], full_s[:], coef[:, :, 1:9], ALU.mult))
                step(v.tensor_tensor(full_s[:], full_s[:], mod[:, shift:shift + KD, 1:9], ALU.add))
                step(v.tensor_copy(H_hi[:, :, 0:NB], full_s[:]))
                minus_hi(H_lo[:, :, 0:NB], full_s[:], H_hi[:, :, 0:NB])
                for k in range(KD + 1):
                    if k < KD:
                        scale_x(i, k, KD * i + (4 if i else 0))
                    if k >= 1:
                        dve.wait_ge(hh_ready, KD * i + k)
                        n.up(minus_hi(H_lo[:, k - 1, NB:T], full[:, (k - 1) % 2, NB:T], H_hi[:, k - 1, NB:T]),
                             h_ready)

            def update(m, n_block, part):
                g = part + m
                dve.wait_ge(block_done, n_block + 1)
                src = Gp[n_block % 2]
                if m >= 2:
                    n.own(x_ready, back=1)
                n.up(v.tensor_tensor(upd_s[:, m % 2, :], src[:, 0, 0:NB], mod[:, g, 1:9], ALU.mult), dve_step)
                v.scalar_tensor_tensor(X[:, m, NB:CH], src[:, 0, NB:CH], mod[:, g, 0:1], X[:, m, NB:CH],
                                       ALU.mult, ALU.add)
                n.up(v.scalar_tensor_tensor(X[:, m, CH:T], src[:, 1, 0:CH], mod[:, g, 0:1], X[:, m, CH:T],
                                            ALU.mult, ALU.add), slot_dve)
                n.own(dve_step)
                n.up(v.tensor_tensor(X[:, m, 0:NB], X[:, m, 0:NB], upd_s[:, m % 2, :], ALU.add), x_ready)

            rstd_parts(0)
            def ada_mod(g):
                n.up(v.tensor_tensor(mod[:, 4 * g:4 * g + 4, :],
                                     bank_of(("ada", g))[:, 0:36].rearrange("p (m c) -> p m c", c=9),
                                     vec[:, V_ADAB + 4 * g:V_ADAB + 4 * g + 4].unsqueeze(2).broadcast_to((P, 4, 9)),
                                     ALU.add), emptied["D"])

            for g in range(ADA_FIRST):
                ada_mod(g)
            n.own(emptied["D"])
            modulate(0)
            dve.wait_ge(lf_act, 1)
            n.up(minus_hi(wf_lo[:], wf[:], wf_hi[:]), lf_dve)
            lo(0)
            lo(1)
            n.up(v.tensor_tensor(lf_a[:], bank_of("fl")[:, 0:40].rearrange("p (b h) -> p b h", h=8),
                                 bfg[:].unsqueeze(1).broadcast_to((P, 5, HEADS)), ALU.add), emptied["D"])
            n.own(emptied["D"])
            step(v.tensor_scalar(lf_b[:], lf_a[:], 0.0, None, ALU.min))
            n.up(v.scalar_tensor_tensor(lf[:], lf_a[:], -1.0, lf_a[:], ALU.mult, ALU.min), lf_dve)

            def tap(t, w):
                cw = vec[:, V_CW + w * 4 + t:V_CW + w * 4 + t + 1]
                n.own(conv_step, back=1)
                if w == 0:
                    o = v.tensor_scalar(CV[:, t, NB:T], UP[:, t, 0:L], cw, vec[:, V_CB + t:V_CB + t + 1],
                                        ALU.mult, ALU.add)
                else:
                    o = v.scalar_tensor_tensor(CV[:, t, NB:T], UP[:, t, w:w + L], cw, CV[:, t, NB:T],
                                               ALU.mult, ALU.add)
                n.up(o, conv_step)

            taps = [(t, w) for t0 in (0, 2) for w in range(CW) for t in (t0, t0 + 1)]
            n.count[conv_step.name] = 0
            for m in range(20):
                if m + 2 < N_OUT_EVEN:
                    lo(m + 2)
                if m == 3:
                    dve.wait_ge(lf_act, 3)
                    n.up(v.tensor_tensor(lf[:], lf_b[:], lf[:], ALU.subtract), lf_dve)
                if 4 <= m < 8:
                    t = m - 4
                    dve.wait_ge(slot_act, runs["in_even"][0] + m + 1)
                    v.tensor_tensor(UP[:, t, CW - 1:], AT[:, t, NB:T], gate[:, t % 2, NB:T], ALU.mult)
                    n.up(v.tensor_tensor(US[:, t, :, CW - 1], AT[:, t, 0:NB], gate[:, t % 2, 0:NB], ALU.mult), u_ready)
                    if m == 7:
                        dve.wait_ge(pad_ready, 1)
                        n.own(u_ready)
                if m >= 8:
                    for t, w in taps[(m - 8) * len(taps) // 12:(m - 7) * len(taps) // 12]:
                        tap(t, w)
            for t in range(4):
                step(v.tensor_tensor(usw[:], US[:, t, :, 0:CW],
                                     vec[:, V_CW + t:V_END:4].unsqueeze(1).broadcast_to((P, NB, CW)), ALU.mult))
                step(v.tensor_reduce(CV[:, t, 0:NB], usw[:], AX.X, ALU.add))
                n.own(conv_step)
                n.up(v.tensor_scalar(CV[:, t, 0:NB], CV[:, t, 0:NB], vec[:, V_CB + t:V_CB + t + 1], None, ALU.add),
                     cv_ready)
            for g in range(ADA_FIRST, ADA_ATT):
                ada_mod(g)
            for t in range(4):
                for c in range(2):
                    cols = slice(c * CH, (c + 1) * CH)
                    n.own(cv_ready)
                    n.up(v.tensor_tensor(CV[:, t, cols], CV[:, t, cols], bank_of(("cm", t, c))[:, 0:CH], ALU.subtract),
                         emptied["D"])
            for t in range(4):
                for c in range(2):
                    n.up(v.tensor_scalar(CR[:, t, c * CH:(c + 1) * CH], bank_of(("cq", t, c))[:, 0:CH], EPS, None,
                                         ALU.add), emptied["D"])
            n.own(emptied["D"])
            n.up(v.reciprocal(CR[:], CR[:]), conv_var)
            dve.wait_ge(conv_act, 5)
            for t in range(4):
                n.up(v.tensor_tensor(CV[:, t, :], CV[:, t, :], CR[:, t, :], ALU.mult), conv_normed)
            for t in range(4):
                dve.wait_ge(ghi_ready, t + 1)
                n.up(minus_hi(G_lo[:, 4 + t, :], full[:, t % 2, :], G_hi[:, 4 + t, :]), g_ready)
            n.up(v.tensor_copy(cumul[:].rearrange("p b h -> p (b h)"), bank_of("cum")[:, 0:32]), emptied["D"])
            wait_emptied(dve, "vs")
            n.up(v.tensor_copy(vts[:], VT[:, :, 0:NB]), samp_dve)

            def weigh(h, q):
                x, w = h * TB + q, (q + 1) * P
                if q == 0:
                    wait_emptied(dve, ("ckb", h))
                n.up(v.scalar_tensor_tensor(SS[:, q, 0:w], bank_of(("s", h, q))[:, 0:w], FOX_SCALE,
                                            ckb[:, h % 2, 0:w], ALU.mult, ALU.subtract), emptied["D"])
                n.own(emptied["D"])
                n.up(v.tensor_reduce(nm[:, x:x + 1], SS[:, q, 0:w], AX.X, ALU.max, negate=True), max_ready)

            def inverse(x):
                dve.wait_ge(exp_ready, x + 1)
                n.up(v.reciprocal(ri[:, x:x + 1], rs[:, x:x + 1]), ri_ready)

            def dots(x):
                for g in range(2 * x, 2 * x + 2):
                    dve.wait_ge(prod_ready, g + 1)
                    n.up(v.tensor_reduce(SC[:, :, g // 8, g % 8], prod[:, g % 2, :].rearrange("p (h d) -> p h d", d=HD),
                                         AX.X, ALU.add), page_dot)

            for q in range(TB):
                weigh(0, q)
            for h in range(HEADS):
                for q in range(TB):
                    x = h * TB + q
                    inverse(x)
                    if h + 1 < HEADS:
                        weigh(h + 1, q)
                    if ada_turned(x) is not None:
                        ada_mod(ada_turned(x))
                    dots(x)
                rows_ = slice(HD * (h % 2), HD * (h % 2) + HD)
                dve.wait_ge(ohi_ready, h + 1)
                n.up(minus_hi(G_lo[rows_, h // 2, NB:T], bank_of(("o", h))[rows_, :], G_hi[rows_, h // 2, NB:T]),
                     emptied["D"])

            ada_mod(N_ADA // 4 - 1)
            wait_emptied(dve, "lt")
            step(v.memset(EX[:, :, :, 0], 0.0))
            for g in range(1, 8):
                step(v.tensor_tensor(EX[:, :, :, g], EX[:, :, :, g - 1], LT[:, :, :, g - 1], ALU.add))

            def hb(ap):
                return ap.rearrange("p (h b) -> p h b", b=NB)

            v.tensor_tensor(hb(small[:, 0, :]), EX[:, :, :, 7], LT[:, :, :, 7], ALU.add)
            v.tensor_tensor(hb(small[0:NB, 1, :]), con[0:NB, C_ID:C_ID + NB].unsqueeze(1).broadcast_to((NB, HEADS, NB)),
                            lf[0:NB, 0, :].unsqueeze(2).broadcast_to((NB, HEADS, NB)), ALU.mult)
            n.up(v.tensor_tensor(small[:, 3, 0:32].rearrange("p (t b) -> p t b", b=NB), QT[:, :, 0:NB], KT[:, :, 0:NB],
                                 ALU.mult), samp_dve)
            n.own(page_dot)
            sc = SC[:].rearrange("p h b g -> p (h b g)")
            n.up(v.tensor_tensor(sc, sc, bank_of("cc")[:, :], ALU.subtract), emptied["D"])
            wait_emptied(dve, "cl")
            n.up(v.scalar_tensor_tensor(small[:, 4, :], bank_of("sn")[:, 0:64], FOX_SCALE * HD, small[:, 2, :], ALU.mult,
                                        ALU.subtract), emptied["D"])
            n.own(emptied["D"])
            n.up(v.tensor_reduce(hb(small[:, 5, :]), SC[:], AX.X, ALU.max), samp_dve)
            n.up(v.tensor_reduce(small[0:64, 6, 0:1], bank_of("mt")[0:64, 0:P], AX.X, ALU.max), emptied["D"])
            n.own(emptied["D"])
            n.up(v.tensor_scalar(small[0:64, 7, :], ident[0:64, 0:64], small[0:64, 6, 0:1], None, ALU.mult), samp_dve)
            n.up(v.tensor_tensor(small[:, 5, :], bank_of("mb")[:, 0:64], small[:, 4, :], ALU.max), emptied["D"])
            n.own(emptied["D"])

            def over_pages(i):
                return hb(small[:, i, :]).unsqueeze(3).broadcast_to((P, HEADS, NB, 8))

            v.tensor_tensor(small[:, 4, :], small[:, 4, :], small[:, 5, :], ALU.subtract)
            n.up(v.tensor_tensor(SC[:], SC[:], over_pages(5), ALU.subtract), samp_dve)
            dve.wait_ge(samp_act, 2)
            n.up(v.tensor_reduce(hb(small[:, 6, :]), SC[:], AX.X, ALU.add), samp_dve)
            n.up(v.tensor_tensor(small[:, 0, :], bank_of("dn")[:, 0:64], small[:, 4, :], ALU.add), emptied["D"])
            n.own(emptied["D"])
            step(v.reciprocal(small[:, 0, :], small[:, 0, :]))
            v.tensor_tensor(small[:, 4, :], small[:, 4, :], small[:, 0, :], ALU.mult)
            n.up(v.tensor_tensor(SC[:], SC[:], over_pages(0), ALU.mult), samp_dve)
            n.own(samp_dve)
            for e in range(2):
                r = slice(HD * e, HD * e + HD)
                o = v.tensor_tensor(full_s[r, 0:4, :], vts[r], small[r, 4, :].rearrange("p (t e b) -> p t e b", e=2, b=NB)[:, :, e, :],
                                    ALU.mult)
            step(o)
            own_head = con[0:HEADS, C_ID:C_ID + HEADS].unsqueeze(2).broadcast_to((HEADS, HEADS, HD))
            for b in range(NB):
                dve.wait_ge(v_used, 8 * b + 8)
                if b >= 2:
                    dve.wait_ge(vm_used, b - 1)
                n.up(v.tensor_tensor(vm[:, b % 2, :].rearrange("p (h d) -> p h d", d=HD),
                                     Gp[b // 2 % 2][0:HEADS, b % 2, :].rearrange("p (h d) -> p h d", d=HD),
                                     own_head, ALU.mult), vm_ready)
            n.up(v.tensor_tensor(full_s[:, 0:4, :], full_s[:, 0:4, :],
                                 bank_of("ov")[:, 0:32].rearrange("p (t b) -> p t b", b=NB), ALU.add), emptied["D"])
            n.own(emptied["D"])
            step(v.tensor_copy(G_hi[:, 0:4, 0:NB], full_s[:, 0:4, :]))
            n.up(minus_hi(G_lo[:, 0:4, 0:NB], full_s[:, 0:4, :], G_hi[:, 0:4, 0:NB]), g_ready)

            lo(N_OUT_EVEN)
            lo(N_OUT_EVEN + 1)
            for q in range(KD):
                lo(N_OUT_EVEN + q + 2)
                update(q, N_OUT_EVEN + q, mod_at(0, 2))

            def ffn(layer, i):
                rstd_parts(i)
                modulate(i)
                ghi0 = 4 + 38 * layer
                for t, ((_, kt), (n0, n1)) in enumerate(zip(THIRDS, ffn_starts(layer))):
                    base_a, base_d = runs[("gu", layer, t)]
                    done = sum(x for _, x in THIRDS[:t])

                    def body(i, n0=n0, base_a=base_a, done=done):
                        for j in range(4):
                            m = n0 + 4 * i + j + 2
                            if isinstance(i, int):
                                lo(m)
                            else:
                                lo(m, (j + 2) % 4, KD)
                            if j % 2 == 0:
                                dve.wait_ge(block_done, n0 + 4 * i + j + 2)
                                dve.wait_ge(slot_act, base_a + 2 * i + j // 2 + 1)
                                dve.wait_ge(ghi_ready, ghi0 + done + 2 * i + j // 2 - 1)
                                dst, up = full[:, j // 2, :], gate[:, j // 2, :]
                                v.tensor_tensor(dst.rearrange("p (c n) -> p c n", c=2), up.rearrange("p (c n) -> p c n", c=2),
                                                Gp[1][:, :, 0:CH], ALU.mult).then_inc(slot_dve, 1)
                            else:
                                dve.wait_ge(ghi_ready, ghi0 + done + 2 * i + j // 2 + 1)
                                g = ds(2 * i + j // 2, 1)
                                minus_hi(G_lo[:, g, :].rearrange("p o n -> p (o n)"), full[:, j // 2, :],
                                         G_hi[:, g, :].rearrange("p o n -> p (o n)")).then_inc(g_ready, 1)

                    with dve.Fori(0, kt // 2 - 1) as i_:
                        body(i_)
                    body(kt // 2 - 1)
                    n.skip(slot_dve, kt)
                    n.skip(g_ready, kt)
                    for q in range(KD):
                        lo(n1 + q + 2)
                        update(q, n1 + q, mod_at(layer, 5))

            ffn(0, 1)

            rstd_parts(2)
            modulate(2)
            cos, sin = con[:, C_COS:C_COS + T], con[:, C_SIN:C_SIN + T]

            def rope(x):
                a, b = QK[:, x, :], QK[:, x + 1, :]
                for out, c, s, op in ((x, cos, sin, ALU.subtract), (x + 1, sin, cos, ALU.add)):
                    v.tensor_tensor(tmp[:, 0, :], a, c, ALU.mult)
                    step(v.tensor_tensor(tmp[:, 1, :], b, s, ALU.mult))
                    n.up(v.tensor_tensor(QKR[:, out, :], tmp[:, 0, :], tmp[:, 1, :], op), rope_ready)
                    n.own(rope_ready)

            for h in range(RH):
                n0 = N_ODD + 12 * h + (h // 2) * KD
                for q in range(12):
                    lo(n0 + q + 2)
                    if q in (4, 6):
                        dve.wait_ge(slot_act, runs[("head", h)][0] + q - 2)
                        rope(q - 4)
                dve.wait_ge(dec_loaded, 16 * (h + 1))
                for j in range(TB):
                    w = L - j * P
                    n.up(v.tensor_tensor(AD[:, j, 0:w], bank_of(("ra", h, j))[:, 0:w], dec[:, 0:w], ALU.mult),
                         emptied["D"])
                for b in range(NB):
                    g = h * NB + b
                    dve.wait_ge(st_scaled, g + 1)
                    bank = bank_of(("vb", h, b))
                    for d in range(2):
                        o = v.scalar_tensor_tensor(st[:, g % 2, d, :], bank[:, :], QKR[:, 2 + d, b:b + 1],
                                                   st[:, g % 2, d, :], ALU.mult, ALU.add)
                    n.up(o, emptied["D"])
                for c in range(2):
                    cols = slice(c * CH, (c + 1) * CH)
                    bank = bank_of(("rm", h, c))
                    n.up(v.tensor_tensor(RVT[:, :, cols], RVT[:, :, cols],
                                         bank[:, 0:CH].unsqueeze(1).broadcast_to((P, 4, CH)), ALU.subtract), emptied["D"])
                for c in range(2):
                    n.up(v.tensor_scalar(rsd[:, c * CH:(c + 1) * CH], bank_of(("rv", h, c))[:, 0:CH], EPS, None,
                                         ALU.add), emptied["D"])
                n.own(emptied["D"])
                n.up(v.reciprocal(rsd[:], rsd[:]), ret_dve)
                dve.wait_ge(ret_act, 5 * h + 5)
                for e in range(4):
                    g = V_RG + 4 * h + e
                    step(v.scalar_tensor_tensor(RVT[:, e, :], RVT[:, e, :], vec[:, g:g + 1], rsd[:], ALU.mult, ALU.mult))
                    n.up(v.tensor_tensor(GS[:, e, :], RVT[:, e, :], GS[:, e, :], ALU.mult), ret_gated)
                for e in range(4):
                    dve.wait_ge(ghi_ready, 26 + 4 * h + e + 1)
                    n.up(minus_hi(G_lo[:, 4 * (h % 2) + e, :], GS[:, e, :], G_hi[:, 4 * (h % 2) + e, :]), g_ready)
                if h % 2:
                    for q in range(KD):
                        lo(n0 + 12 + q + 2)
                        update(q, n0 + 12 + q, mod_at(1, 2))
            ffn(1, 3)
            rstd_parts(4)
            dve.wait_ge(rstd_ready, 5)
            for k in range(KD):
                scale_x(4, k, KD * 4 + 4)

        @block.gpsimd
        def _(pool):
            v = nc.gpsimd
            v.memset(UP[:, :, 0:CW - 1], 0.0).then_inc(pad_ready, 1)
            for h in range(HEADS):
                for q in range(TB):
                    x = h * TB + q
                    pool.wait_ge(ri_ready, x + 1)
                    w = SS[:, q, 0:(q + 1) * P]
                    v.tensor_scalar(w, w, ri[:, x:x + 1], 1.0, ALU.mult, ALU.mult).then_inc(p_ready, 1)
                    for g in range(2 * x, 2 * x + 2):
                        pool.wait_ge(k_page[g % 4], 16 * (g // 4 + 1))
                        if g % 8 == 0:
                            wait_emptied(pool, ("qb", g // 8))
                        if g >= 2:
                            pool.wait_ge(page_dot, g - 1)
                        v.tensor_tensor(prod[:, g % 2, :], kp[:, g % 4, :], QB[:, g // 8, :], ALU.mult).then_inc(prod_ready, 1)
            pool.wait_ge(pages_loaded, 32)
            wait_emptied(pool, "vs")
            for s in range(2):
                pool.wait_ge(stage_stored[s], 16 * 4)
            v.indirect_dma_start(lg[:], None, A["cache_logf"][0].rearrange("n p h -> n (p h)"),
                                 bass.IndirectOffsetOnAxis(pt_col[:, 0:1], 0)).then_inc(lg_loaded, 16)

        @block.sync
        def _(sp):
            sp.dma_start(con[:], A["consts"]).then_inc(x_loaded, 16)
            sp.dma_start(xn[:], A["x_prompt"][0].rearrange("(b p) d -> p b d", p=P)).then_inc(x_loaded, 16)
            sp.dma_start(xsn[:], A["x_sample"][:, 0, :]).then_inc(x_loaded, 16)
            sp.dma_start(cn[0:1, :], A["c_prompt"]).then_inc(x_loaded, 16)
            sp.dma_start(cn[1:9, :], A["c_sample"]).then_inc(x_loaded, 16)
            sp.dma_start(pt_row[:], A["page_table"].rearrange("b g -> (b g)").rearrange("(o n) -> o n", o=1)).then_inc(pages_loaded, 16)
            sp.dma_start(pt_col[:], A["page_table"].rearrange("b g -> (b g)").rearrange("(n o) -> n o", o=1)).then_inc(pages_loaded, 16)

            def columns(w, k0, kt, c0):
                return w[k0 * P:(k0 + kt) * P, ds(c0, P)].rearrange("(k p) m -> p k m", p=P)

            def load(j, src, kt=KD):
                sp.dma_start(raw[:, j, 0:kt, :], src).then_inc(raw_loaded[j], 16)

            def load_ada(m, layer, c0):
                load(m % 4, columns(A["ada_w"][layer], 0, KD, c0))

            for m in range(4 * ADA_FIRST):
                if m >= 4:
                    sp.wait_ge(ada_used, m - 3)
                load_ada(m, 0, m * P)

            def load_n(n, w, k0, c0, kt=KD):
                if n < 4:
                    sp.wait_ge(ada_used, 4 * ADA_FIRST + n - 3)
                elif N_OUT_EVEN <= n < N_OUT_EVEN + 4:
                    sp.wait_ge(ada_used, N_ADA + n - N_OUT_EVEN - 3)
                else:
                    sp.wait_ge(lo_ready, n - 3)
                load(n % 4, columns(w, k0, kt, c0), kt)

            w = A["w_in_even"][0]
            for n, c0 in enumerate([1544 + P * j for j in range(4)] + [2056 + P * j for j in range(4)]
                                   + [P * j for j in range(12)]):
                load_n(n, w, 0, c0)
            for m in range(4 * ADA_FIRST, 4 * ADA_ATT):
                if m < 4 * ADA_FIRST + 4:
                    sp.wait_ge(lo_ready, N_OUT_EVEN + m - 4 * ADA_FIRST - 3)
                else:
                    sp.wait_ge(ada_used, m - 3)
                load_ada(m, 0, m * P)

            for m in range(4 * ADA_ATT, 4 * ADA_ATT + 4):
                sp.wait_ge(ada_used, m - 3)
                load_ada(m, 0, m * P)
            sp.wait_ge(pages_loaded, 32)
            sp.wait_ge(g_ready, 4)

            def page(g, cache, ring, j, arrived):
                n = sp.value_load(pt_row[0:1, ds(g, 1)], min_val=0, max_val=cache.shape[0] - 1)
                sp.dma_start(ring[:, j, :], cache[ds(n, 1), :, :].rearrange("o p n -> p (o n)")).then_inc(arrived[j], 16)

            cache_k = A["cache_k"][0].rearrange("n p h d -> n p (h d)")
            cache_v = A["cache_v"][0].rearrange("n p h d -> n p (h d)")
            for j in range(4):
                page(j, cache_k, kp, j, k_page)
            in_layer0 = N_ADA // 8 - ADA_ATT
            for layer, first, end in ((0, 1, in_layer0), (1, in_layer0, NPG // 4)):
                with sp.Fori(first, end) as i:
                    for j in range(4):
                        sp.wait_ge(ada_used, 4 * ADA_ATT + 4 * i + j - 3)
                        load(j, columns(A["ada_w"][layer], 0, KD, (4 * ADA_ATT - 48 * layer + j) * P + i * 512))
                        sp.wait_ge(prod_ready, 4 * i + j - 3)
                        page(4 * i + j, cache_k, kp, j, k_page)
            sp.wait_ge(samp_dve, 1)
            wait_emptied(sp, ("ada", N_ADA // 4 - 1))
            for j in range(4):
                page(j, cache_v, vp, j, v_page)
            with sp.Fori(1, NPG // 4) as i:
                for j in range(4):
                    sp.wait_ge(v_used, 4 * i + j - 3)
                    page(4 * i + j, cache_v, vp, j, v_page)
            for j in range(8):
                load_n(N_OUT_EVEN + j, A["w_out_even"][0], 0, P * j)

            def ffn(layer):
                wg, wu, wd = A["w_ffn_gate"][layer], A["w_ffn_up"][layer], A["w_ffn_down"][layer]
                for (k0, kt), (n0, n1) in zip(THIRDS, ffn_starts(layer)):
                    with sp.Fori(0, kt // 2) as i:
                        for j in range(4):
                            sp.wait_ge(lo_ready, n0 + 4 * i + j - 3)
                            load(j, columns(wu if j % 2 else wg, 0, KD, (k0 + j // 2) * P + 2 * P * i))
                    with sp.Fori(0, 2) as i:
                        for j in range(4):
                            sp.wait_ge(lo_ready, n1 + 4 * i + j - 3)
                            load(j, columns(wd, k0, kt, 4 * P * i + j * P), kt)

            ffn(0)
            w = A["w_in_odd"][0]
            states = A["state_ret"][0]
            for h in range(RH):
                cols = ([h * DK + P * j for j in range(2)] + [D + h * DK + P * j for j in range(2)]
                        + [2 * D + h * DV + P * j for j in range(4)] + [4 * D + h * DV + P * j for j in range(4)])
                n0 = N_ODD + h * 12 + (h // 2) * KD
                for j in range(0 if h % 2 == 0 and h == 0 else 4, 12):
                    load_n(n0 + j, w, 0, cols[j])
                if h >= 1:
                    wait_emptied(sp, ("ra", h - 1, TB - 1))
                sp.dma_start(dec[:], A["decay"][h]).then_inc(dec_loaded, 16)
                if h % 2:
                    for j in range(4):
                        load_n(n0 + 12 + j, A["w_out_odd"][0], (h // 2) * KD, P * j)
                else:
                    nxt = ([(h + 1) * DK + P * j for j in range(2)] + [D + (h + 1) * DK + P * j for j in range(2)])
                    for j in range(4):
                        load_n(n0 + 12 + j, w, 0, nxt[j])
                for b in range(NB):
                    g = h * NB + b
                    if g >= 2:
                        sp.wait_ge(st_stored[g % 2], 16 * (g // 2))
                        sp.wait_ge(st_used, g - 1)
                    sp.dma_start(st[:, g % 2], states[b, h].rearrange("(d p) e -> p d e", p=P)).then_inc(st_loaded[g % 2], 16)
                if h % 2:
                    for j in range(4, KD):
                        load_n(n0 + 12 + j, A["w_out_odd"][0], (h // 2) * KD, P * j)
                    if h == 1:
                        nxt = ([2 * DK + P * j for j in range(2)] + [D + 2 * DK + P * j for j in range(2)])
                        for j in range(4):
                            load_n(n0 + 20 + j, w, 0, nxt[j])
            ffn(1)
            for s in {s.name: s for s in outs}.values():
                sp.wait_ge(s, 16 * sum(o.name == s.name for o in outs))


def constants():
    c = np.zeros((P, C_END), np.float32)
    i = np.arange(P)
    c[:, C_ID:C_ID + P] = np.eye(P)
    c[:, C_MEAN:C_MEAN + P] = 1.0 / D
    c[:, C_B64:C_B64 + P] = (i[:, None] // 64 == i[None, :] // 64) / 64.0
    c[:, C_M512:C_M512 + P] = 1.0 / DV
    c[:, C_ONE:C_ONE + P] = 1.0
    c[:, C_TRI:C_TRI + P] = i[:, None] <= i[None, :]
    c[:, C_NEG:C_NEG + P] = np.where(i[None, :] <= i[:, None], 0.0, MASKED)
    inv = (np.float32(1) / np.power(np.float32(10000), np.linspace(0, 1, P, dtype=np.float32))).astype(np.float32)
    pos = np.concatenate([np.full(NB, PAST), np.arange(L)]).astype(np.float32)
    angle = (pos[None, :] * inv[:, None]).astype(np.float32).astype(np.float64)
    c[:, C_COS:C_COS + T] = np.cos(angle)
    c[:, C_SIN:C_SIN + T] = np.sin(angle)
    for b in range(TB):
        for h in range(RH):
            c[:, C_KDEC + b * RH + h] = GAMMA[h] ** (L - 1 - (b * P + i))
    dist = np.arange(L)[None, :] - i[:, None]
    decay = np.stack([np.where(dist >= 0, g ** np.maximum(dist, 0.0), 0.0) for g in GAMMA]).astype(np.float32)
    return c, decay


_INS = ["x_prompt", "x_sample", "cache_k", "cache_v", "cache_logf", "state_conv", "state_ret", "page_table",
        "c_prompt", "c_sample", "ada_w", "ada_b", "norm_mix_g", "norm_ffn_g", "w_in_even", "b_forget",
        "conv_w", "conv_b", "conv_norm_g", "conv_norm_b", "w_out_even", "w_in_odd", "ret_norm_g", "w_out_odd",
        "w_ffn_gate", "w_ffn_up", "w_ffn_down", "final_norm_g"]
_OUTS = [("y_prompt", (1, L, D)), ("y_sample", (NB, 1, D)), ("k_prompt", (1, 1, L, HEADS, HD)),
         ("v_prompt", (1, 1, L, HEADS, HD)), ("logf_prompt", (1, 1, L, HEADS)),
         ("conv_prompt", (1, 1, CW - 1, 512)), ("ret_prompt", (1, 1, RH, DK, DV)),
         ("k_sample", (1, NB, 1, HEADS, HD)), ("v_sample", (1, NB, 1, HEADS, HD)),
         ("logf_sample", (1, NB, 1, HEADS)), ("conv_sample", (1, NB, CW - 1, 512)),
         ("ret_sample", (1, NB, RH, DK, DV))]


def kernel(**inputs):
    import concourse.bacc as bacc
    from concourse.bass_utils import run_bass_kernel_spmd

    nc = bacc.Bacc("TRN2", target_bir_lowering=False, num_devices=1)
    arrays = {f"in_{n}": np.ascontiguousarray(inputs[n]) for n in _INS}
    arrays["in_consts"], arrays["in_decay"] = constants()
    aps = {n[3:]: nc.dram_tensor(n, a.shape, mybir.dt.from_np(a.dtype), kind="ExternalInput").ap()
           for n, a in arrays.items()}
    for n, shape in _OUTS:
        aps[n] = nc.dram_tensor(f"out_{n}", shape, mybir.dt.float32, kind="ExternalOutput").ap()
    build(nc, aps)
    r = run_bass_kernel_spmd(nc, [arrays], core_ids=[0])
    return tuple(r.results[0][f"out_{n}"] for n, _ in _OUTS)
```

```python
import math
from contextlib import ExitStack

import concourse.bass as bass
import concourse.mybir as mybir
import numpy as np

P = 128
D = 1024
KD = D // P
L = 512
TB = L // P
NB = 8
T = NB + L
CH = T // 2
HEADS = 8
HD = 64
PAST = 1024
PAGES = PAST // P
NPG = NB * PAGES
CW = 31
RH = 4
DK = 256
DV = 512
FF = 2816
EPS = 1e-6
FOX_SCALE = HD ** -0.5
MASKED = -1e30
THIRDS = ((0, 8), (8, 8), (16, 6))
GAMMA = [1.0 - 2.0 ** (-5.0 - h) for h in range(RH)]

C_ID, C_MEAN, C_B64, C_M512, C_ONE, C_TRI, C_NEG = (P * i for i in range(7))
C_COS = 7 * P
C_SIN = C_COS + T
C_KDEC = C_SIN + T
C_END = C_KDEC + TB * RH

N_IN_EVEN = 0
N_OUT_EVEN = 20
N_FFN = (28, 160)
N_ODD = 96
N_BLOCKS = 228
HEAD_BLOCKS = 12
N_ADA = 96
ADA_FIRST = 4
ADA_ATT = 8


def ada_turned(x):
    return ADA_ATT + x // 2 - 1 if x % 2 == 0 and x > 0 else None


def ffn_starts(layer):
    at, out = N_FFN[layer], []
    for _, tiles in THIRDS:
        out.append((at, at + 2 * tiles))
        at += 2 * tiles + KD
    return out


def head_start(h):
    return N_ODD + HEAD_BLOCKS * h + (KD if h == RH - 1 else 0)


def out_start(pair):
    return head_start(2 + pair) + HEAD_BLOCKS


def k_tiles(n):
    for layer in range(2):
        down = ffn_starts(layer)[2][1]
        if down <= n < down + KD:
            return THIRDS[2][1]
    return KD


V_MIXG, V_FFNG, V_FING, V_CB, V_CG, V_CNB, V_RG = 0, 16, 32, 40, 44, 48, 52
V_ROWS = 68
V_ADAB = V_ROWS
V_CW = V_ADAB + N_ADA
V_END = V_CW + CW * 4


def psum_jobs():
    jobs = [("xs", "D")] + [(("xT", k), "D") for k in range(KD)]
    jobs += [("cT", "D"), ("vec", "D"), (("sc", 0), "D"), (("sc", 1), "D")]

    def norm(i):
        return [(("ss", i, 0), "D"), (("ss", i, 1), "D")]

    jobs += norm(0) + [(("ada", g), "D") for g in range(ADA_FIRST)] + [(("flT", c), "A") for c in range(2)] + [("fl", "D")]
    jobs += [(("ada", g), "D") for g in range(ADA_FIRST, ADA_ATT)]
    jobs += [(("cm", t, c), "D") for t in range(4) for c in range(2)]
    jobs += [("cpo", "A"), ("cso", "A")]
    jobs += [("qs", "A")] + [(("qb", b), "A") for b in range(NB)]
    jobs += [(("cq", t, c), "D") for t in range(4) for c in range(2)]
    jobs += [("cum", "D"), ("cumT", "A")]
    jobs += [(("kn", tb), "A") for tb in range(TB)] + [(("vn", tb), "A") for tb in range(TB)]
    jobs += [("ks", "A"), ("vs", "A")]
    jobs += [(("ckb", 0), "A")] + [(("s", 0, q), "D") for q in range(TB)]
    for h in range(HEADS):
        if h + 1 < HEADS:
            jobs += [(("ckb", h + 1), "A")]
        for q in range(TB):
            jobs += [(("pt", h, q), "A")]
            if h + 1 < HEADS:
                jobs += [(("s", h + 1, q), "D")]
            if ada_turned(h * TB + q) is not None:
                jobs += [(("ada", ada_turned(h * TB + q)), "D")]
        jobs += [(("o", h), "D")]
    jobs += [(("ada", N_ADA // 4 - 1), "D")]
    jobs += [("lt", "A"), ("cc", "D"), ("cl", "A"), ("sn", "D")]
    jobs += [("mt", "D"), ("mb", "D"), ("dn", "D"), ("ov", "D")]
    jobs += norm(1) + norm(2)
    for h in range(RH + 1):
        for q in range(HEAD_BLOCKS):
            if h > 0 and q >= 4:
                jobs += [(("vb", h - 1, q - 4), "D"), (("so", h - 1, q - 4), "D")]
            elif h > 0 and q == 0:
                jobs += [(("rm", h - 1, c), "D") for c in range(2)]
            elif h > 0 and q == 1:
                jobs += [(("rv", h - 1, c), "D") for c in range(2)]
        if h < RH:
            jobs += [(("rvn", h, tb), "A") for tb in range(TB)]
            jobs += [(("rvs", h), "A")]
            jobs += [(("rkn", h, tb), "A") for tb in range(TB)]
        if h > 0:
            jobs += [(("sot", h - 1), "D")]
        if h < RH:
            jobs += [(("ra", h, j), "D") for j in range(TB)]
            jobs += [(("rst", h, d), "A") for d in range(2)]
            jobs += [(("ro", h, e), "A") for e in range(4)]
    jobs += norm(3) + norm(4)
    for f in range(2):
        jobs += [(("y", tb, f), "D" if tb % 2 and f else "A") for tb in range(TB)] + [(("ys", f), "A")]
    return jobs


class Jobs:

    def __init__(self):
        jobs = psum_jobs()
        self.index = {name: i for i, (name, _) in enumerate(jobs)}
        assert len(self.index) == len(jobs)
        self.engine = [e for _, e in jobs]
        count = {"A": 0, "D": 0}
        self.nth = []
        for e in self.engine:
            count[e] += 1
            self.nth.append(count[e])

    def bank(self, name):
        return self.index[name] % 4

    def done(self, name):
        return self.index[name] + 1

    def emptied(self, name):
        i = self.index[name]
        return self.engine[i], self.nth[i]


class Tally:

    def __init__(self, eng):
        self.eng, self.count = eng, {}

    def up(self, instruction, sem):
        instruction.then_inc(sem, 1)
        self.count[sem.name] = self.count.get(sem.name, 0) + 1

    def skip(self, sem, n):
        self.count[sem.name] = self.count.get(sem.name, 0) + n

    def own(self, sem, back=0):
        count = self.count.get(sem.name, 0)
        if count > back:
            self.eng.wait_ge(sem, count - back)


def build(nc, A):
    f32, f32r, i32 = mybir.dt.float32, mybir.dt.float32r, mybir.dt.int32
    ACT, ALU, AX = mybir.ActivationFunctionType, mybir.AluOpType, mybir.AxisListType
    ds = bass.ds
    jobs = Jobs()

    at = [(nc.sbuf_base + 63) // 64 * 64]

    def sb(name, shape, dtype=f32):
        t = nc.alloc_sbuf_tensor_at(name, shape, dtype, offset=at[0])
        at[0] += (math.prod(shape[1:]) * 4 + 31) // 32 * 32
        assert at[0] <= nc.sbuf_usable_end, (name, at[0])
        return t

    X = sb("X", [P, KD, T])
    con = sb("con", [P, C_END])
    vec = sb("vec", [P, V_END])
    mod = sb("mod", [P, N_ADA, 9])
    coef = sb("coef", [P, KD, 9])
    raw = sb("raw", [P, 4, KD, P])
    w_hi = sb("w_hi", [P, 4, KD, P], f32r)
    w_lo = sb("w_lo", [P, 4, KD, P], f32r)
    lf = sb("lf", [P, 5, HEADS])
    lf_a = sb("lf_a", [P, 5, HEADS])
    lf_b = sb("lf_b", [P, 5, HEADS])
    bfg = sb("bfg", [P, HEADS])
    cT = sb("cT", [P, KD, 9])
    g_at = at[0]
    G_hi = sb("G_hi", [P, KD, T], f32r)
    gl_at = at[0]
    G_lo = sb("G_lo", [P, KD, T], f32r)
    h_at = at[0]
    H_hi = sb("H_hi", [P, KD, T], f32r)
    H_lo = sb("H_lo", [P, KD, T], f32r)
    free_at = at[0]
    sq = sb("sq", [P, 2, T])
    rstd = sb("rstd", [P, T])
    scaled_at = at[0]
    scaled = sb("scaled", [P, 2, T])
    full = sb("full", [P, 2, T])
    full_s = sb("full_s", [P, KD, NB])
    upd_s = sb("upd_s", [P, 2, NB])
    gate_at = at[0]
    gate = sb("gate", [P, 2, T])
    scratch_end = max(at[0], free_at + 10 * 512 * 4)
    at[0] = h_at
    xn = sb("xn", [P, TB, D])
    xsn = sb("xsn", [NB, D])
    cn = sb("cn", [9, D])
    cn_silu = sb("cn_silu", [9, D])
    rows_s = sb("rows_s", [120, 2, 512])
    at[0] = scratch_end
    QT = sb("QT", [P, 4, T])
    KT = sb("KT", [P, 4, T])
    vt_at = at[0]
    VT = sb("VT", [P, 4, T])
    us_at = at[0]
    US = sb("US", [P, 4, NB, CW + 1])
    SC = sb("SC", [P, HEADS, NB, 8])
    small = sb("small", [P, 8, 64])
    up_at = at[0]
    UP = sb("UP", [P, 4, CW - 1 + L])
    usw = sb("usw", [P, NB, CW])
    even_end = at[0]
    at[0] = scratch_end
    wf = sb("wf", [P, KD, P])
    wf_hi = sb("wf_hi", [P, KD, P], f32r)
    wf_lo = sb("wf_lo", [P, KD, P], f32r)
    assert at[0] <= vt_at
    at[0] = scaled_at
    flt = sb("flt", [HEADS, T])
    at[0] = vt_at
    rows_v = sb("rows_v", [V_ROWS, P])
    rows_a = sb("rows_a", [N_ADA, P])
    rows_c = sb("rows_c", [CW * 4, P])
    at[0] = vt_at
    AT = sb("AT", [P, 4, T])
    at[0] = g_at
    CV = sb("CV", [P, 4, T])
    at[0] = gl_at
    CR = sb("CR", [P, 4, T])
    at[0] = h_at
    QB = sb("QB", [P, NB, 512])
    VN = sb("VN", [P, TB, 512])
    PTS = sb("PTS", [P, TB, 512])
    assert at[0] <= free_at
    at[0] = h_at + NB * 512 * 4
    sq4 = sb("sq4", [P, 4, T])
    at[0] = free_at
    SS = sb("SS", [P, TB, 512])
    kp = sb("kp", [P, 4, 512])
    prod = sb("prod", [P, 2, 512])
    assert at[0] <= scratch_end
    at[0] = free_at
    LT = sb("LT", [P, HEADS, NB, 8])
    EX = sb("EX", [P, HEADS, NB, 8])
    CC = sb("CC", [P, HEADS, NB, 8])
    at[0] = h_at + NB * 512 * 4
    vp = sb("vp", [P, 8, 512])
    at[0] = gate_at
    rows_early = sb("rows_early", [9, 2, 512])
    at[0] = vt_at
    rows_late = sb("rows_late", [9, 2, 512])
    at[0] = h_at
    vm = sb("vm", [HEADS, 2, 512])
    at[0] = up_at
    ckb = sb("ckb", [P, 2, L])
    ko_at = at[0]
    kn_out = sb("kn_out", [P, 2, 512])
    assert at[0] <= even_end
    at[0] = us_at
    qsn = sb("qsn", [NB, 512])
    cum8 = sb("cum8", [HEADS, L])
    at[0] = even_end
    cumul = sb("cumul", [P, TB, HEADS])
    nm = sb("nm", [P, HEADS * TB])
    rs = sb("rs", [P, HEADS * TB])
    ri = sb("ri", [P, HEADS * TB])
    pt_row = sb("pt_row", [1, NPG], i32)
    pt_col = sb("pt_col", [NPG, 1], i32)
    at[0] = ko_at
    lg = sb("lg", [NPG, P * HEADS])
    vts = sb("vts", [P, 4, NB])
    at[0] = free_at
    dec = sb("dec", [P, L])
    raw_at = at[0]
    QK = sb("QK", [P, 4, T])
    QKR = sb("QKR", [P, 4, T])
    RVT = sb("RVT", [P, 4, T])
    rvn_at = at[0]
    RVN = sb("RVN", [P, TB, DV])
    KDN = sb("KDN", [P, TB, DK])
    GS = sb("GS", [P, 4, T])
    st = sb("st", [P, 2, 2, DV])
    so = sb("so", [P, 2, DV])
    rsd = sb("rsd", [P, T])
    vsn = sb("vsn", [NB, DV])
    osum = sb("osum", [NB, DV])
    kq_s = sb("kq_s", [P, 4, NB])
    gs_s = sb("gs_s", [P, 4, NB])
    qz = sb("qz", [P, 2, NB * NB])
    stat = sb("stat", [NB, 2])
    at[0] = raw_at
    AD = sb("AD", [P, TB, L])
    at[0] = rvn_at
    RSQ = sb("RSQ", [P, 4, T])
    at[0] = g_at
    YT = sb("YT", [P, KD, T])
    yo = sb("yo", [P, 10, 512])
    assert at[0] <= free_at

    ctx = ExitStack()
    with ctx:
        def sem(name):
            return ctx.enter_context(nc.semaphore(name))

        Gp = [ctx.enter_context(nc.psum_tensor(f"product{i}", [P, 2, 512], f32)) for i in range(2)]
        Jp = [ctx.enter_context(nc.psum_tensor(f"job{i}", [P, 512], f32)) for i in range(4)]

        x_loaded, rows_loaded, pages_loaded = sem("x_loaded"), sem("rows_loaded"), sem("pages_loaded")
        raw_loaded = [sem(f"raw_loaded{i}") for i in range(4)]
        k_page = [sem(f"k_page{i}") for i in range(4)]
        v_page = [sem(f"v_page{i}") for i in range(8)]
        lg_loaded, dec_loaded = sem("lg_loaded"), sem("dec_loaded")
        st_loaded = [sem(f"st_loaded{i}") for i in range(2)]
        st_stored = [sem(f"st_stored{i}") for i in range(2)]
        stage_stored = [sem(f"stage_stored{i}") for i in range(2)]
        out_done, v_stored = sem("out_done"), sem("v_stored")
        block_done, ada_used, job_done = sem("block_done"), sem("ada_used"), sem("job_done")
        ada_taken = sem("ada_taken")
        sq_used, v_used, st_used = sem("sq_used"), sem("v_used"), sem("st_used")
        vm_used = sem("vm_used")
        slot_act, slot_dve = sem("slot_act"), sem("slot_dve")
        emptied = {"A": sem("emptied_act"), "D": sem("emptied_dve")}
        c_silu, sq_ready, rstd_ready = sem("c_silu"), sem("sq_ready"), sem("rstd_ready")
        full_ready, hh_ready, hi_ready = sem("full_ready"), sem("hh_ready"), sem("hi_ready")
        ghi_ready, exp_ready, lf_act = sem("ghi_ready"), sem("exp_ready"), sem("lf_act")
        conv_act, ohi_ready, st_scaled = sem("conv_act"), sem("ohi_ready"), sem("st_scaled")
        samp_act, ret_act, osum_root = sem("samp_act"), sem("ret_act"), sem("osum_root")
        x_ready, var_ready, vm_ready = sem("x_ready"), sem("var_ready"), sem("vm_ready")
        scaled_ready, h_ready, lo_ready = sem("scaled_ready"), sem("h_ready"), sem("lo_ready")
        g_ready, dve_step, lf_dve = sem("g_ready"), sem("dve_step"), sem("lf_dve")
        u_ready, cv_ready, conv_var = sem("u_ready"), sem("cv_ready"), sem("conv_var")
        conv_normed, conv_step, ret_gated = sem("conv_normed"), sem("conv_step"), sem("ret_gated")
        max_ready, ri_ready, page_dot = sem("max_ready"), sem("ri_ready"), sem("page_dot")
        samp_dve, rope_ready = sem("samp_dve"), sem("rope_ready")
        ret_dve, st_updated, qs_ready = sem("ret_dve"), sem("st_updated"), sem("qs_ready")
        osum_ready, y_ready = sem("osum_ready"), sem("y_ready")
        pad_ready, p_ready, prod_ready = sem("pad_ready"), sem("p_ready"), sem("prod_ready")
        outs = []

        def store(eng, dst, src, done=None):
            s = done or out_done
            outs.append(s)
            eng.dma_start(dst, src).then_inc(s, 16)

        cache_k = A["cache_k"][0].rearrange("n p h d -> n p (h d)")
        cache_v = A["cache_v"][0].rearrange("n p h d -> n p (h d)")

        def page(eng, g, cache, ring, j, arrived):
            n = eng.value_load(pt_row[0:1, ds(g, 1)], min_val=0, max_val=cache.shape[0] - 1)
            eng.dma_start(ring[:, j, :], cache[ds(n, 1), :, :].rearrange("o p n -> p (o n)")).then_inc(arrived[j], 16)

        def value_pages(eng, first):
            for j in range(first, PAGES, 2):
                page(eng, j, cache_v, vp, j, v_page)
            with eng.Fori(1, NB) as i:
                for j in range(first, PAGES, 2):
                    eng.wait_ge(v_used, PAGES * i + j - PAGES + 1)
                    page(eng, PAGES * i + j, cache_v, vp, j, v_page)

        def wait_job(eng, name):
            eng.wait_ge(job_done, jobs.done(name))

        def wait_emptied(eng, name):
            e, n = jobs.emptied(name)
            eng.wait_ge(emptied[e], n)

        ident = con[:, C_ID:C_ID + P]
        ones = con[:, C_ONE:C_ONE + P]
        one_col = con[:, C_ONE:C_ONE + 1]

        runs, ra, rd = {}, 2, 1
        for name, a, d in (
            [("in_even", 20, 0), ("out_even", 0, KD)]
            + [x for t, (_, n) in enumerate(THIRDS) for x in ((("gu", 0, t), n, n), (("dn", 0, t), 0, KD))]
            + [(("head", h), HEAD_BLOCKS, 0) for h in range(3)] + [(("out", 0), 0, KD), (("head", 3), HEAD_BLOCKS, 0), (("out", 1), 0, KD)]
            + [x for t, (_, n) in enumerate(THIRDS) for x in ((("gu", 1, t), n, n), (("dn", 1, t), 0, KD))]
        ):
            runs[name] = (ra, rd)
            ra, rd = ra + a, rd + d
        N_ROW_LOADS, G_FFN = 13, (5, 47)
        X_BEFORE = (0, 0, 24, 40, 64)
        L_OF = (0, 0, 1, 1)

        def raw_count(n, ada=False):
            if ada:
                before = 0 if n < 4 * ADA_FIRST else N_OUT_EVEN
            else:
                before = 4 * ADA_FIRST if n < N_OUT_EVEN else N_ADA
            return 16 * ((n + before) // 4 + 1)

        def ada_rows(g):
            return (rows_early if g < ADA_ATT else rows_late)[:, g % 2, :]

        def mod_at(layer, part):
            return layer * 48 + part * KD

        block = ctx.enter_context(nc.Block())


        @block.tensor
        def _(pe):
            def open_job(name):
                i = jobs.index[name]
                if i >= 4:
                    pe.wait_ge(emptied[jobs.engine[i - 4]], jobs.nth[i - 4])
                return Jp[i % 4]

            def close(mm):
                mm.then_inc(job_done, 1)

            def turn(out, src, n=P):
                return pe.transpose(out, src, ident[0:n, 0:n])

            pe.wait_ge(x_loaded, 80)
            bank = open_job("xs")
            for k in range(KD):
                mm = turn(bank[:, k * NB:(k + 1) * NB], xsn[:, k * P:(k + 1) * P], NB)
            close(mm)
            for k in range(KD):
                bank = open_job(("xT", k))
                for b in range(TB):
                    mm = turn(bank[:, b * P:(b + 1) * P], xn[:, b, k * P:(k + 1) * P])
                close(mm)
            bank = open_job("cT")
            pe.wait_ge(c_silu, 1)
            for k in range(KD):
                mm = turn(bank[:, k * 9:(k + 1) * 9], cn_silu[:, k * P:(k + 1) * P], 9)
            close(mm)
            bank = open_job("vec")
            pe.wait_ge(rows_loaded, 16 * N_ROW_LOADS)
            turn(bank[:, 0:V_ROWS], rows_v[:], V_ROWS)
            turn(bank[:, V_ADAB:V_ADAB + N_ADA], rows_a[:], N_ADA)
            close(turn(bank[:, V_CW:V_END], rows_c[:], CW * 4))
            for g in range(2):
                bank = open_job(("sc", g))
                for t in range(4):
                    mm = turn(bank[:, t * 120:(t + 1) * 120], rows_s[:, g, t * P:(t + 1) * P], 120)
                close(mm)

            def norm(i):
                banks = [open_job(("ss", i, c)) for c in range(2)]
                for k in range(KD):
                    pe.wait_ge(sq_ready, KD * i + k + 1)
                    for c in range(2):
                        mm = pe.matmul(banks[c][:, 0:CH], con[:, C_MEAN:C_MEAN + P],
                                       sq[:, k % 2, c * CH:(c + 1) * CH], start=k == 0, stop=k == KD - 1)
                        if k == KD - 1:
                            close(mm)
                    if k < KD - 1:
                        mm.then_inc(sq_used, 1)

            norm(0)

            def ada_block(m):
                g, j = m // 4, m % 4
                if j == 0 and g >= 2:
                    pe.wait_ge(ada_taken, g - 1)
                pe.wait_ge(raw_loaded[j], raw_count(m, ada=True))
                for k in range(KD):
                    mm = pe.matmul(Gp[g % 2][0:9, 0, j * P:(j + 1) * P], cT[:, k, :], raw[:, j, k, :],
                                   start=k == 0, stop=k == KD - 1)
                mm.then_inc(ada_used, 1)

            def ada_turn(g):
                bank = open_job(("ada", g))
                pe.wait_ge(ada_taken, g + 1)
                for j in range(4):
                    mm = turn(bank[:, j * 9:(j + 1) * 9], ada_rows(g)[:, j * P:(j + 1) * P], 9)
                close(mm)

            def ada_groups(first, end):
                for g in range(first, end):
                    for j in range(4):
                        ada_block(4 * g + j)
                    if g > first:
                        ada_turn(g - 1)
                ada_turn(end - 1)

            wait_emptied(pe, "cT")
            ada_groups(0, ADA_FIRST)

            def product(j, slot, kt, hi, lo):
                for c in range(2):
                    cols = slice(c * CH, (c + 1) * CH)
                    for k in range(kt):
                        for p, (w, x) in enumerate(((w_lo, hi), (w_hi, lo), (w_hi, hi))):
                            mm = pe.matmul(Gp[slot][:, c, 0:CH], w[:, j, k, :], x[:, k, cols],
                                           start=k == 0 and p == 0, stop=k == kt - 1 and p == 2)
                return mm

            def first_pair(i, n0, base_a, base_d):
                pe.wait_ge(slot_act, base_a)
                pe.wait_ge(slot_dve, base_d)
                pe.wait_ge(lo_ready, n0 + 2)
                for k in range(KD):
                    pe.wait_ge(h_ready, KD * i + k + 1)
                    for j in range(2):
                        for c in range(2):
                            for p, (w, x) in enumerate(((w_lo, H_hi), (w_hi, H_lo), (w_hi, H_hi))):
                                mm = pe.matmul(Gp[j][:, c, 0:CH], w[:, j, k, :], x[:, k, c * CH:(c + 1) * CH],
                                               start=k == 0 and p == 0, stop=k == KD - 1 and p == 2)
                        if k == KD - 1:
                            mm.then_inc(block_done, 1)

            def run(name, n0, bodies, kt, hi, lo, engine, first=None, between=None):
                base_a, base_d = runs[name]
                if first is None:
                    pe.wait_ge(slot_act, base_a)
                    pe.wait_ge(slot_dve, base_d)

                def body(i, js=range(4)):
                    for j in js:
                        pe.wait_ge(lo_ready, n0 + 4 * i + j + 1)
                        if engine == "gu":
                            s, base = (slot_act, base_a) if j % 2 == 0 else (slot_dve, base_d)
                            pe.wait_ge(s, base + 2 * i + j // 2)
                        elif engine == "A":
                            pe.wait_ge(slot_act, base_a + 4 * i + j - 1)
                        else:
                            pe.wait_ge(slot_dve, base_d + 4 * i + j - 1)
                        product(j, j % 2, kt, hi, lo).then_inc(block_done, 1)

                if first is not None:
                    first_pair(first, n0, base_a, base_d)
                    if between:
                        between()
                    body(0, range(2, 4))
                with pe.Fori(0 if first is None else 1, bodies) as i:
                    body(i)

            def forget_gates():
                pe.wait_ge(lf_dve, 1)
                for c in range(2):
                    bank = open_job(("flT", c))
                    for k in range(KD):
                        for p, (w, x) in enumerate(((wf_lo, H_hi), (wf_hi, H_lo), (wf_hi, H_hi))):
                            mm = pe.matmul(bank[:, 0:CH], w[:, k, :], x[:, k, c * CH:(c + 1) * CH],
                                           start=k == 0 and p == 0, stop=k == KD - 1 and p == 2)
                    close(mm)

            def forget_columns():
                wait_emptied(pe, ("flT", 1))
                bank = open_job("fl")
                for b in range(5):
                    c0 = 0 if b == 0 else NB + (b - 1) * P
                    mm = turn(bank[:, b * 8:(b + 1) * 8], flt[:, c0:c0 + P], HEADS)
                close(mm)

            run("in_even", N_IN_EVEN, 5, KD, H_hi, H_lo, "A", first=0, between=forget_gates)
            forget_columns()

            pe.wait_ge(slot_act, runs["in_even"][0] + 20)
            ada_groups(ADA_FIRST, ADA_ATT)

            for t in range(4):
                pe.wait_ge(cv_ready, t + 1)
                for c in range(2):
                    bank = open_job(("cm", t, c))
                    close(pe.matmul(bank[:, 0:CH], con[:, C_B64:C_B64 + P], CV[:, t, c * CH:(c + 1) * CH],
                                    start=True, stop=True))
            bank = open_job("cpo")
            for t in range(4):
                mm = turn(bank[0:CW - 1, t * P:(t + 1) * P], UP[:, t, L:L + CW - 1])
            close(mm)
            bank = open_job("cso")
            for t in range(4):
                mm = turn(bank[0:NB, t * P:(t + 1) * P], US[:, t, :, CW - 1])
            close(mm)

            def rows_of(name, src):
                bank = open_job(name)
                for t in range(4):
                    mm = turn(bank[0:NB, t * P:(t + 1) * P], src[:, t, 0:NB])
                close(mm)

            rows_of("qs", QT)
            wait_emptied(pe, "qs")
            for b in range(NB):
                bank = open_job(("qb", b))
                close(pe.matmul(bank[:, :], con[0:NB, C_ID + b:C_ID + b + 1].broadcast_to((NB, P)), qsn[:],
                                start=True, stop=True))
            for t in range(4):
                pe.wait_ge(conv_act, t + 1)
                for c in range(2):
                    bank = open_job(("cq", t, c))
                    close(pe.matmul(bank[:, 0:CH], con[:, C_B64:C_B64 + P], sq4[:, t, c * CH:(c + 1) * CH],
                                    start=True, stop=True))

            bank = open_job("cum")
            pe.wait_ge(lf_dve, 3)
            for q in range(TB):
                for b in range(q + 1):
                    mm = pe.matmul(bank[:, q * 8:(q + 1) * 8], con[:, C_TRI:C_TRI + P] if b == q else ones,
                                   lf[:, 1 + b, :], start=b == 0, stop=b == q)
            close(mm)
            wait_emptied(pe, "cum")
            bank = open_job("cumT")
            for q in range(TB):
                mm = turn(bank[0:8, q * P:(q + 1) * P], cumul[:, q, :])
            close(mm)
            for name, src in (("kn", KT), ("vn", VT)):
                for b in range(TB):
                    bank = open_job((name, b))
                    for t in range(4):
                        mm = turn(bank[:, t * P:(t + 1) * P], src[:, t, NB + b * P:NB + (b + 1) * P])
                    close(mm)
            rows_of("ks", KT)
            rows_of("vs", VT)

            def cum_rows(h):
                bank = open_job(("ckb", h))
                close(pe.matmul(bank[:, :], con[0:8, C_ID + h:C_ID + h + 1].broadcast_to((8, P)), cum8[:],
                                start=True, stop=True))

            def scores(h, q):
                bank = open_job(("s", h, q))
                rows = slice(HD * (h % 2), HD * (h % 2) + HD)
                n = (q + 1) * P
                pe.matmul(bank[:, 0:n], QT[rows, h // 2, NB + q * P:NB + (q + 1) * P],
                          KT[rows, h // 2, NB:NB + n], start=True, stop=False)
                close(pe.matmul(bank[:, n - P:n], ident, con[:, C_NEG:C_NEG + P], start=False, stop=True))

            wait_emptied(pe, "cumT")
            cum_rows(0)
            for q in range(TB):
                scores(0, q)
            for h in range(HEADS):
                if h + 1 < HEADS:
                    cum_rows(h + 1)
                for q in range(TB):
                    bank = open_job(("pt", h, q))
                    pe.wait_ge(p_ready, h * TB + q + 1)
                    for b in range(q + 1):
                        mm = turn(bank[:, b * P:(b + 1) * P], SS[:, q, b * P:(b + 1) * P])
                    close(mm)
                    if h + 1 < HEADS:
                        scores(h + 1, q)
                    x = h * TB + q
                    for m in range(4 * ADA_ATT + 2 * x, 4 * ADA_ATT + 2 * x + 2):
                        ada_block(m)
                    if ada_turned(x) is not None:
                        ada_turn(ada_turned(x))
                bank = open_job(("o", h))
                wait_emptied(pe, ("pt", h, TB - 1))
                rows = slice(HD * (h % 2), HD * (h % 2) + HD)
                for b in range(TB):
                    mm = pe.matmul(bank[rows, b * P:L], VN[:, b, h * HD:(h + 1) * HD], PTS[:, b, b * P:L],
                                   start=b == 0, stop=b == TB - 1)
                close(mm)

            ada_turn(N_ADA // 4 - 1)

            bank = open_job("lt")
            pe.wait_ge(lg_loaded, 16)
            for h in range(HEADS):
                mm = turn(bank[:, h * NPG:(h + 1) * NPG], lg[:].rearrange("g (t h) -> g t h", h=HEADS)[:, :, h], NPG)
            close(mm)
            bank = open_job("cc")
            pe.wait_ge(samp_dve, 2)
            pe.matmul(bank[:, :], con[:, C_TRI:C_TRI + P], LT[:].rearrange("p h b g -> p (h b g)"),
                      start=True, stop=False)
            close(pe.matmul(bank[:, :], ones, EX[:].rearrange("p h b g -> p (h b g)"), start=False, stop=True))
            bank = open_job("cl")
            pe.matmul(bank[:, 0:64], ones, small[:, 0, :], start=True, stop=False)
            close(pe.matmul(bank[:, 0:64], ones[0:NB, :], small[0:NB, 1, :], start=False, stop=True))
            bank = open_job("sn")
            for h in range(HEADS):
                c = C_B64 + HD * (h % 2)
                mm = pe.matmul(bank[:, h * NB:(h + 1) * NB], con[:, c:c + 1].broadcast_to((P, P)),
                               small[:, 3, (h // 2) * NB:(h // 2 + 1) * NB], start=True, stop=True)
            close(mm)
            bank = open_job("mt")
            pe.wait_ge(samp_dve, 3)
            close(turn(bank[0:64, 0:P], small[:, 5, :]))
            bank = open_job("mb")
            pe.wait_ge(samp_dve, 4)
            close(pe.matmul(bank[:, 0:64], ones[0:64, :], small[0:64, 7, :], start=True, stop=True))
            bank = open_job("dn")
            pe.wait_ge(samp_dve, 6)
            close(pe.matmul(bank[:, 0:64], ones, small[:, 6, :], start=True, stop=True))
            pe.wait_ge(samp_dve, 7)
            turned = open_job("ov")

            def gather(b):
                pe.wait_ge(vm_ready, b + 1)
                for t in range(4):
                    mm = pe.matmul(turned[:, t * NB + b:t * NB + b + 1], vm[:, b % 2, t * P:(t + 1) * P],
                                   ones[0:HEADS, 0:1], start=True, stop=True)
                return mm

            for b in range(NB):
                if b >= 4:
                    pe.wait_ge(vm_ready, b - 3)
                for g in range(8):
                    pe.wait_ge(v_page[g], 16 * (b + 1))
                    mm = pe.matmul(Gp[b // 2 % 2][0:HEADS, b % 2, :], SC[:, :, b, g], vp[:, g, :],
                                   start=g == 0, stop=g == 7)
                    mm.then_inc(v_used, 1)
                if b >= 1:
                    gather(b - 1).then_inc(vm_used, 1)
            close(gather(NB - 1))

            pe.wait_ge(g_ready, 5)
            wait_emptied(pe, ("o", HEADS - 1))
            run("out_even", N_OUT_EVEN, 2, KD, G_hi, G_lo, "D")

            def ffn(layer, i):
                norm(i)
                for t, ((_, kt), (n0, n1)) in enumerate(zip(THIRDS, ffn_starts(layer))):
                    run(("gu", layer, t), n0, kt // 2, KD, H_hi, H_lo, "gu", first=i if t == 0 else None)
                    pe.wait_ge(g_ready, G_FFN[layer] + sum(x for _, x in THIRDS[:t + 1]))
                    run(("dn", layer, t), n1, 2, kt, G_hi, G_lo, "D")

            ffn(0, 1)

            norm(2)
            def head_block(h, q):
                base_a, base_d = runs[("head", h)]
                if h == 0 and q < 2:
                    if q == 0:
                        first_pair(2, head_start(0), base_a, base_d)
                    return
                if q == 0:
                    pe.wait_ge(slot_act, base_a)
                    pe.wait_ge(slot_dve, base_d)
                n = head_start(h) + q
                pe.wait_ge(lo_ready, n + 1)
                if q >= 2:
                    pe.wait_ge(slot_act, base_a + q - 1)
                product(n % 4, n % 2, KD, H_hi, H_lo).then_inc(block_done, 1)

            def over_features(name, h, src):
                for c in range(2):
                    bank = open_job((name, h, c))
                    for e in range(4):
                        mm = pe.matmul(bank[:, 0:CH], con[:, C_M512:C_M512 + P], src[:, e, c * CH:(c + 1) * CH],
                                       start=e == 0, stop=e == 3)
                    close(mm)

            def values_of(h, b):
                bank = open_job(("vb", h, b))
                if b == 0:
                    wait_emptied(pe, ("rvs", h))
                close(pe.matmul(bank[:, :], con[0:NB, C_ID + b:C_ID + b + 1].broadcast_to((NB, P)), vsn[:],
                                start=True, stop=True))

            def query(h, b):
                bank = open_job(("so", h, b))
                pe.wait_ge(qs_ready, h + 1)
                pe.wait_ge(st_updated, h * NB + b + 1)
                for d in range(2):
                    mm = pe.matmul(bank[0:NB, :], qz[:, d, b * NB:(b + 1) * NB], st[:, b % 2, d, :],
                                   start=d == 0, stop=d == 1)
                close(mm)

            for h in range(RH + 1):
                for q in range(HEAD_BLOCKS):
                    if h > 0 and q >= 4:
                        values_of(h - 1, q - 4)
                    if h < RH:
                        head_block(h, q)
                    if h > 0 and q >= 4:
                        query(h - 1, q - 4)
                    elif h > 0 and q == 0:
                        wait_emptied(pe, ("ro", h - 1, 3))
                        over_features("rm", h - 1, RVT)
                    elif h > 0 and q == 1:
                        pe.wait_ge(ret_act, 5 * h - 1)
                        over_features("rv", h - 1, RSQ)
                if h < RH:
                    pe.wait_ge(slot_act, runs[("head", h)][0] + HEAD_BLOCKS)
                    for b in range(TB):
                        bank = open_job(("rvn", h, b))
                        for e in range(4):
                            mm = turn(bank[:, e * P:(e + 1) * P], RVT[:, e, NB + b * P:NB + (b + 1) * P])
                        close(mm)
                    rows_of(("rvs", h), RVT)
                    pe.wait_ge(rope_ready, 4 * h + 4)
                    for b in range(TB):
                        bank = open_job(("rkn", h, b))
                        for d in range(2):
                            mm = turn(bank[:, d * P:(d + 1) * P], QKR[:, 2 + d, NB + b * P:NB + (b + 1) * P])
                        close(mm)
                if h > 0:
                    bank = open_job(("sot", h - 1))
                    pe.wait_ge(osum_ready, 2 * h)
                    for e in range(4):
                        mm = turn(bank[:, e * NB:(e + 1) * NB], osum[:, e * P:(e + 1) * P], NB)
                    close(mm)
                if h < RH:
                    for j in range(TB):
                        bank = open_job(("ra", h, j))
                        for d in range(2):
                            mm = pe.matmul(bank[:, 0:L - j * P], QKR[:, 2 + d, NB + j * P:NB + (j + 1) * P],
                                           QKR[:, d, NB + j * P:T], start=d == 0, stop=d == 1)
                        close(mm)
                    wait_emptied(pe, ("rkn", h, TB - 1))
                    for d in range(2):
                        bank = open_job(("rst", h, d))
                        for b in range(TB):
                            mm = pe.matmul(bank[:, :], KDN[:, b, d * P:(d + 1) * P], RVN[:, b, :],
                                           start=b == 0, stop=b == TB - 1)
                        close(mm)
                    wait_emptied(pe, ("ra", h, TB - 1))
                    for e in range(4):
                        bank = open_job(("ro", h, e))
                        for j in range(TB):
                            mm = pe.matmul(bank[:, j * P:L], RVN[:, j, e * P:(e + 1) * P], AD[:, j, 0:L - j * P],
                                           start=j == 0, stop=j == TB - 1)
                        close(mm)
                if h in (2, RH):
                    pair = 0 if h == 2 else 1
                    pe.wait_ge(g_ready, 27 + 10 * (pair + 1))
                    run(("out", pair), out_start(pair), 2, KD, G_hi, G_lo, "D")
            ffn(1, 3)

            norm(4)
            for f in range(2):
                pe.wait_ge(y_ready, 4 * f + 4)
                for b in range(TB):
                    bank = open_job(("y", b, f))
                    for k in range(4):
                        mm = turn(bank[:, k * P:(k + 1) * P], YT[:, 4 * f + k, NB + b * P:NB + (b + 1) * P])
                    close(mm)
                bank = open_job(("ys", f))
                for k in range(4):
                    mm = turn(bank[0:NB, k * P:(k + 1) * P], YT[:, 4 * f + k, 0:NB])
                close(mm)

        @block.scalar
        def _(act):
            n = Tally(act)

            def f(out, in_, func, **kw):
                return nc.scalar.activation(out, in_, func, **kw)

            rows = [(rows_v[V_MIXG:V_MIXG + 16], A["norm_mix_g"].rearrange("l (k p) -> (l k) p", p=P)),
                    (rows_v[V_FFNG:V_FFNG + 16], A["norm_ffn_g"].rearrange("l (k p) -> (l k) p", p=P)),
                    (rows_v[V_FING:V_FING + 8], A["final_norm_g"].rearrange("(k p) -> k p", p=P)),
                    (rows_v[V_CB:V_CB + 4], A["conv_b"][0].rearrange("(k p) -> k p", p=P)),
                    (rows_v[V_CG:V_CG + 4], A["conv_norm_g"][0].rearrange("(k p) -> k p", p=P)),
                    (rows_v[V_CNB:V_CNB + 4], A["conv_norm_b"][0].rearrange("(k p) -> k p", p=P)),
                    (rows_v[V_RG:V_RG + 16], A["ret_norm_g"][0].rearrange("(k p) -> k p", p=P)),
                    (rows_a[:], A["ada_b"].rearrange("l (k p) -> (l k) p", p=P)),
                    (rows_c[:], A["conv_w"][0].rearrange("w (k p) -> (w k) p", p=P)),
                    (rows_s[:, 0, :], A["state_conv"][0, 0:4].rearrange("b w c -> (b w) c")),
                    (rows_s[:, 1, :], A["state_conv"][0, 4:8].rearrange("b w c -> (b w) c")),
                    (wf[:], A["w_in_even"][0][:, 1536:1536 + P].rearrange("(k p) m -> p k m", p=P)),
                    (bfg[:], A["b_forget"].broadcast_to((P, HEADS)))]
            assert len(rows) == N_ROW_LOADS
            for dst, src in rows:
                act.dma_start(dst, src).then_inc(rows_loaded, 16)
            store(act, A["conv_sample"][0, :, 0:CW - 2, :], A["state_conv"][0, :, 1:CW - 1, :])
            act.wait_ge(x_loaded, 80)
            n.up(f(cn_silu[:], cn[:], ACT.Silu), c_silu)

            def squares(i):
                for k in range(KD):
                    if i == 0:
                        wait_emptied(act, ("xT", k))
                    else:
                        act.wait_ge(x_ready, X_BEFORE[i] + k + 1)
                    if k >= 2:
                        act.wait_ge(sq_used, (KD - 1) * i + k - 1)
                    n.up(f(sq[:, k % 2, :], X[:, k, :], ACT.Square), sq_ready)
                act.wait_ge(var_ready, i + 1)
                n.up(f(rstd[:], rstd[:], ACT.Sqrt), rstd_ready)

            def modulate(i):
                shift = mod_at(L_OF[i], 0 if i % 2 == 0 else 3)
                for k in range(KD):
                    act.wait_ge(scaled_ready, KD * i + k + 1)
                    n.up(f(H_hi[:, k, NB:T], scaled[:, k % 2, NB:T], ACT.Identity,
                           bias=mod[:, shift + k, 0:1]), hh_ready)

            def split_hi(j, m, kt):
                act.wait_ge(raw_loaded[j], raw_count(m) if isinstance(m, int) else m[0])
                if not isinstance(m, int):
                    act.wait_ge(block_done, m[1])
                elif m >= 4:
                    act.wait_ge(block_done, m - 3)
                f(w_hi[:, j, 0:kt, :], raw[:, j, 0:kt, :], ACT.Copy).then_inc(hi_ready, 1)

            def ahead(m):
                if m < N_BLOCKS:
                    split_hi(m % 4, m, k_tiles(m))

            def product_done(m):
                act.wait_ge(block_done, m + 1)

            def slot(j):
                return Gp[j % 2][:, :, 0:CH]

            def halves(ap):
                return ap.rearrange("p (c n) -> p c n", c=2)

            def take_rows(g):
                act.wait_ge(ada_used, 4 * g + 4)
                if g >= 2:
                    wait_job(act, ("ada", g - 2))
                n.up(f(ada_rows(g), Gp[g % 2][0:9, 0, :], ACT.Copy), ada_taken)

            squares(0)
            for g in range(ADA_FIRST):
                take_rows(g)
            act.wait_ge(rows_loaded, 16 * N_ROW_LOADS)
            n.up(f(wf_hi[:], wf[:], ACT.Copy), lf_act)
            ahead(0)
            ahead(1)
            modulate(0)
            for i in range(2):
                n.up(f(small[:, i, 0:1], one_col, ACT.Copy), slot_act)
            for m in range(20):
                if m + 2 < N_OUT_EVEN:
                    ahead(m + 2)
                product_done(m)
                kind, j = m // 4, m % 4
                if kind == 1:
                    if j >= 2:
                        act.wait_ge(u_ready, j - 1)
                    n.up(f(halves(gate[:, j % 2, :]), slot(m), ACT.Sigmoid), slot_act)
                else:
                    if kind == 4:
                        act.wait_ge(u_ready, 4)
                    n.up(f(halves((AT, None, QT, KT, VT)[kind][:, j, :]), slot(m), ACT.Copy), slot_act)
                if m == 1:
                    for c in range(2):
                        wait_job(act, ("flT", c))
                        n.up(f(flt[:, c * CH:(c + 1) * CH], Jp[jobs.bank(("flT", c))][0:HEADS, 0:CH], ACT.Copy),
                             emptied["A"])

            stage = [0, 0]
            turn_ = [0]

            def stage_out(name, part, width, dst):
                s = turn_[0] % 2
                turn_[0] += 1
                wait_job(act, name)
                if stage[s]:
                    act.wait_ge(stage_stored[s], 16 * stage[s])
                bank = Jp[jobs.bank(name)]
                n.up(f(kn_out[0:part, s, 0:width], bank[0:part, 0:width], ACT.Copy), emptied["A"])
                n.own(emptied["A"])
                store(act, dst, kn_out[0:part, s, 0:width], stage_stored[s])
                stage[s] += 1

            for g in range(ADA_FIRST, ADA_ATT):
                take_rows(g)
            act.wait_ge(lf_dve, 2)
            n.up(f(lf[:], lf[:], ACT.Exp), lf_act)
            n.own(lf_act)
            n.up(f(lf[:], lf[:], ACT.Ln, bias=one_col), lf_act)
            act.wait_ge(lf_dve, 3)
            store(act, A["logf_prompt"][0, 0].rearrange("(b p) h -> p b h", p=P), lf[:, 1:5, :])
            store(act, A["logf_sample"][0, :, 0, :], lf[0:NB, 0, :])
            act.wait_ge(cv_ready, 4)
            stage_out("cpo", CW - 1, 512, A["conv_prompt"][0, 0])
            stage_out("cso", NB, 512, A["conv_sample"][0, :, CW - 2, :])
            wait_job(act, "qs")
            n.up(f(qsn[:], Jp[jobs.bank("qs")][0:NB, :], ACT.Copy), emptied["A"])
            for b in range(NB):
                wait_job(act, ("qb", b))
                n.up(f(QB[:, b, :], Jp[jobs.bank(("qb", b))][:, :], ACT.Copy, scale=FOX_SCALE), emptied["A"])
            for t in range(4):
                wait_emptied(act, ("cm", t, 1))
                n.up(f(sq4[:, t, :], CV[:, t, :], ACT.Square), conv_act)
            act.wait_ge(conv_var, 1)
            n.up(f(CR[:], CR[:], ACT.Sqrt), conv_act)
            for t in range(4):
                act.wait_ge(conv_normed, t + 1)
                if t >= 2:
                    act.wait_ge(g_ready, t - 1)
                n.up(f(full[:, t % 2, :], CV[:, t, :], ACT.Silu, bias=vec[:, V_CNB + t:V_CNB + t + 1],
                       scale=vec[:, V_CG + t:V_CG + t + 1]), full_ready)
                n.own(full_ready)
                n.up(f(G_hi[:, 4 + t, :], full[:, t % 2, :], ACT.Copy), ghi_ready)
            wait_job(act, "cumT")
            n.up(f(cum8[:], Jp[jobs.bank("cumT")][0:8, :], ACT.Copy), emptied["A"])
            for b in range(TB):
                stage_out(("kn", b), P, 512, A["k_prompt"][0, 0, b * P:(b + 1) * P].rearrange("p h d -> p (h d)"))
            for b in range(TB):
                wait_job(act, ("vn", b))
                n.up(f(VN[:, b, :], Jp[jobs.bank(("vn", b))][:, :], ACT.Copy), emptied["A"])
                n.own(emptied["A"])
                store(act, A["v_prompt"][0, 0, b * P:(b + 1) * P].rearrange("p h d -> p (h d)"), VN[:, b, :], v_stored)
            stage_out("ks", NB, 512, A["k_sample"][0, :, 0].rearrange("p h d -> p (h d)"))
            stage_out("vs", NB, 512, A["v_sample"][0, :, 0].rearrange("p h d -> p (h d)"))

            def row_of_sums(h):
                wait_job(act, ("ckb", h))
                if h >= 2:
                    wait_emptied(act, ("s", h - 2, TB - 1))
                n.up(f(ckb[:, h % 2, :], Jp[jobs.bank(("ckb", h))][:, :], ACT.Copy), emptied["A"])

            def exps(h, q):
                x = h * TB + q
                act.wait_ge(max_ready, x + 1)
                w = SS[:, q, 0:(q + 1) * P]
                n.up(f(w, w, ACT.Exp, bias=nm[:, x:x + 1], accum_out=rs[:, x:x + 1]), exp_ready)

            row_of_sums(0)
            for q in range(TB):
                exps(0, q)
            for h in range(HEADS):
                if h + 1 < HEADS:
                    row_of_sums(h + 1)
                if h >= 1:
                    wait_job(act, ("o", h - 1))
                for q in range(TB):
                    wait_job(act, ("pt", h, q))
                    n.up(f(PTS[:, 0:q + 1, q * P:(q + 1) * P],
                           Jp[jobs.bank(("pt", h, q))][:, 0:(q + 1) * P].rearrange("p (b c) -> p b c", c=P),
                           ACT.Copy), emptied["A"])
                    if h + 1 < HEADS:
                        exps(h + 1, q)
                    if q % 2:
                        take_rows(ADA_ATT + (h * TB + q) // 2)
                wait_job(act, ("o", h))
                rows_ = slice(HD * (h % 2), HD * (h % 2) + HD)
                n.up(f(G_hi[rows_, h // 2, NB:T], Jp[jobs.bank(("o", h))][rows_, :], ACT.Copy), ohi_ready)

            ahead(N_OUT_EVEN)
            ahead(N_OUT_EVEN + 1)
            wait_job(act, "lt")
            n.up(f(LT[:].rearrange("p h b g -> p (h b g)"), Jp[jobs.bank("lt")][:, :], ACT.Copy), emptied["A"])
            wait_job(act, "cl")
            n.up(f(small[:, 2, :], Jp[jobs.bank("cl")][:, 0:64], ACT.Copy), emptied["A"])
            act.wait_ge(samp_dve, 5)
            n.up(f(small[:, 4, :], small[:, 4, :], ACT.Exp), samp_act)
            n.up(f(SC[:], SC[:], ACT.Exp), samp_act)

            def gates(layer):
                for t, ((_, kt), (n0, n1)) in enumerate(zip(THIRDS, ffn_starts(layer))):
                    base_a, base_d = runs[("gu", layer, t)]
                    g0 = G_FFN[layer] + sum(x for _, x in THIRDS[:t])

                    def body(i, n0=n0, base_d=base_d, g0=g0):
                        for j in range(4):
                            m = n0 + 4 * i + j + 2
                            jj = (j + 2) % 4
                            if isinstance(i, int):
                                ahead(m)
                            else:
                                split_hi(jj, (16 * (n0 // 4 + N_ADA // 4 + 1 + (j + 2) // 4) + 16 * i, m - 3), KD)
                            if j % 2 == 0:
                                act.wait_ge(block_done, n0 + 4 * i + j + 1)
                                act.wait_ge(slot_dve, base_d + 2 * i + j // 2 - 1)
                                f(halves(gate[:, j // 2, :]), slot(0), ACT.Silu).then_inc(slot_act, 1)
                            else:
                                act.wait_ge(slot_dve, base_d + 2 * i + j // 2 + 1)
                                f(G_hi[:, ds(2 * i + j // 2, 1), :].rearrange("p o n -> p (o n)"),
                                  full[:, j // 2, :], ACT.Copy).then_inc(ghi_ready, 1)

                    with act.Fori(0, kt // 2 - 1) as i:
                        body(i)
                    body(kt // 2 - 1)
                    for q in range(KD):
                        ahead(n1 + q + 2)

            act.wait_ge(pages_loaded, 32)
            act.wait_ge(v_stored, 16 * TB)
            value_pages(act, 1)
            for q in range(KD):
                ahead(N_OUT_EVEN + q + 2)
            squares(1)
            modulate(1)
            gates(0)
            squares(2)
            modulate(2)

            sto = [0, 0]
            def tail(h, q):
                if q == 0:
                    wait_emptied(act, ("rm", h, 1))
                    for e in range(4):
                        n.up(f(RSQ[:, e, :], RVT[:, e, :], ACT.Square), ret_act)
                elif q == 1:
                    act.wait_ge(ret_dve, h + 1)
                    n.up(f(rsd[:], rsd[:], ACT.Sqrt), ret_act)
                elif q < 4:
                    for e in (2 * q - 4, 2 * q - 3):
                        act.wait_ge(ret_gated, 4 * h + e + 1)
                        n.up(f(G_hi[:, 4 * (h % 2) + e, :], GS[:, e, :], ACT.Copy), ghi_ready)
                else:
                    g = h * NB + q - 4
                    act.wait_ge(st_loaded[g % 2], 16 * (g // 2 + 1))
                    n.up(f(st[:, g % 2], st[:, g % 2], ACT.Copy, scale=GAMMA[h]), st_scaled)

            for h in range(RH + 1):
                for q in range(HEAD_BLOCKS):
                    if h < RH:
                        m = head_start(h) + q
                        ahead(m + 2)
                    if h > 0 and q >= 4:
                        tail(h - 1, q)
                    if h < RH:
                        product_done(m)
                        src = slot(m)
                        if q == 8 and h > 0:
                            act.wait_ge(g_ready, 27 + 5 * (h - 1) + 4)
                        if q < 2:
                            o = f(halves(QK[:, q, :]), src, ACT.Copy)
                        elif q < 4:
                            o = f(halves(QK[:, q, :]), src, ACT.Copy, scale=DK ** -0.5)
                        elif q < 8:
                            o = f(halves(RVT[:, q - 4, :]), src, ACT.Copy)
                        else:
                            o = f(halves(GS[:, q - 8, :]), src, ACT.Silu)
                        n.up(o, slot_act)
                    if h > 0 and q < 4:
                        tail(h - 1, q)
                if h > 0:
                    act.wait_ge(osum_ready, 2 * h - 1)
                    n.up(f(stat[:, 1:2], stat[:, 1:2], ACT.Sqrt), osum_root)
                if h == RH:
                    for q in range(KD):
                        ahead(out_start(1) + q + 2)
                    break
                for b in range(TB):
                    wait_job(act, ("rvn", h, b))
                    n.up(f(RVN[:, b, :], Jp[jobs.bank(("rvn", h, b))][:, :], ACT.Copy), emptied["A"])
                wait_job(act, ("rvs", h))
                n.up(f(vsn[:], Jp[jobs.bank(("rvs", h))][0:NB, :], ACT.Copy), emptied["A"])
                for b in range(TB):
                    wait_job(act, ("rkn", h, b))
                    c0 = C_KDEC + b * RH + h
                    n.up(f(KDN[:, b, :], Jp[jobs.bank(("rkn", h, b))][:, 0:DK], ACT.Copy,
                           scale=con[:, c0:c0 + 1]), emptied["A"])
                for d in range(2):
                    wait_job(act, ("rst", h, d))
                    if sto[d]:
                        act.wait_ge(stage_stored[d], 16 * (stage[d] + sto[d]))
                    n.up(f(so[:, d, :], Jp[jobs.bank(("rst", h, d))][:, :], ACT.Copy), emptied["A"])
                    n.own(emptied["A"])
                    store(act, A["ret_prompt"][0, 0, h, d * P:(d + 1) * P, :], so[:, d, :], stage_stored[d])
                    sto[d] += 1
                for e in range(4):
                    wait_job(act, ("ro", h, e))
                    n.up(f(RVT[:, e, NB:T], Jp[jobs.bank(("ro", h, e))][:, :], ACT.Copy), emptied["A"])
                if h == 2:
                    for q in range(KD):
                        ahead(out_start(0) + q + 2)
            squares(3)
            modulate(3)
            gates(1)
            squares(4)
            for f in range(2):
                for b in range(TB + 1):
                    name = ("y", b, f) if b < TB else ("ys", f)
                    if jobs.emptied(name)[0] == "A":
                        part = P if b < TB else NB
                        wait_job(act, name)
                        n.up(nc.scalar.activation(yo[0:part, 5 * f + b, :], Jp[jobs.bank(name)][0:part, :], ACT.Copy),
                             emptied["A"])

        @block.vector
        def _(dve):
            n = Tally(dve)
            v = nc.vector

            def step(instruction):
                n.up(instruction, dve_step)
                n.own(dve_step)

            def bank_of(name):
                wait_job(dve, name)
                return Jp[jobs.bank(name)]

            def lo(m, j=None, kt=KD):
                if isinstance(m, int):
                    if m >= N_BLOCKS:
                        return
                    j, kt = m % 4, k_tiles(m)
                dve.wait_ge(hi_ready, m + 1)
                v.tensor_tensor(w_lo[:, j, 0:kt, :], raw[:, j, 0:kt, :], w_hi[:, j, 0:kt, :].bitcast(f32),
                                ALU.subtract).then_inc(lo_ready, 1)

            def minus_hi(out, whole, hi):
                return v.tensor_tensor(out, whole, hi.bitcast(f32), ALU.subtract)

            n.up(v.memset(full_s[:, 0, 0:1], 0.0), slot_dve)
            bank = bank_of("xs")
            n.up(v.tensor_copy(X[:, :, 0:NB], bank[:, 0:KD * NB].rearrange("p (k b) -> p k b", b=NB)), emptied["D"])
            for k in range(KD):
                n.up(v.tensor_copy(X[:, k, NB:T], bank_of(("xT", k))[:, :]), emptied["D"])
            n.up(v.tensor_copy(cT[:].rearrange("p k b -> p (k b)"), bank_of("cT")[:, 0:KD * 9]), emptied["D"])
            n.up(v.tensor_copy(vec[:], bank_of("vec")[:, 0:V_END]), emptied["D"])
            for g in range(2):
                bank = bank_of(("sc", g))
                for t in range(4):
                    o = v.tensor_copy(US[:, t, 4 * g:4 * g + 4, 0:CW - 1],
                                      bank[:, t * 120:(t + 1) * 120].rearrange("p (b w) -> p b w", b=4))
                n.up(o, emptied["D"])

            def rstd_parts(i):
                for c in range(2):
                    n.up(v.tensor_scalar(rstd[:, c * CH:(c + 1) * CH], bank_of(("ss", i, c))[:, 0:CH],
                                         EPS, None, ALU.add), emptied["D"])
                n.own(emptied["D"])
                n.up(v.reciprocal(rstd[:], rstd[:]), var_ready)

            def modulate(i):
                layer, second = L_OF[i], i % 2
                shift, scale = mod_at(layer, 3 * second), mod_at(layer, 3 * second + 1)
                g = (V_FFNG if second else V_MIXG) + layer * KD
                step(v.scalar_tensor_tensor(coef[:], mod[:, scale:scale + KD, :], 1.0,
                                            vec[:, g:g + KD].unsqueeze(2).broadcast_to((P, KD, 9)),
                                            ALU.add, ALU.mult))
                dve.wait_ge(rstd_ready, i + 1)
                if i == 1:
                    dve.wait_ge(v_stored, 16 * TB)
                step(v.tensor_tensor(full_s[:], X[:, :, 0:NB],
                                     rstd[:, 0:NB].unsqueeze(1).broadcast_to((P, KD, NB)), ALU.mult))
                step(v.tensor_tensor(full_s[:], full_s[:], coef[:, :, 1:9], ALU.mult))
                step(v.tensor_tensor(full_s[:], full_s[:], mod[:, shift:shift + KD, 1:9], ALU.add))
                step(v.tensor_copy(H_hi[:, :, 0:NB], full_s[:]))
                minus_hi(H_lo[:, :, 0:NB], full_s[:], H_hi[:, :, 0:NB])
                for k in range(KD + 1):
                    if k < KD:
                        if k >= 2:
                            dve.wait_ge(hh_ready, KD * i + k - 1)
                            n.own(h_ready)
                        n.up(v.scalar_tensor_tensor(scaled[:, k % 2, NB:T], X[:, k, NB:T], coef[:, k, 0:1],
                                                    rstd[:, NB:T], ALU.mult, ALU.mult), scaled_ready)
                    if k >= 1:
                        dve.wait_ge(hh_ready, KD * i + k)
                        n.own(scaled_ready, back=1 if k < KD else 0)
                        n.up(v.scalar_tensor_tensor(H_lo[:, k - 1, NB:T], scaled[:, (k - 1) % 2, NB:T],
                                                    mod[:, shift + k - 1, 0:1], H_hi[:, k - 1, NB:T].bitcast(f32),
                                                    ALU.add, ALU.subtract), h_ready)

            def update(m, n_block, part):
                g = part + m
                dve.wait_ge(block_done, n_block + 1)
                src = Gp[n_block % 2]
                if m >= 2:
                    n.own(x_ready, back=1)
                n.up(v.tensor_tensor(upd_s[:, m % 2, :], src[:, 0, 0:NB], mod[:, g, 1:9], ALU.mult), dve_step)
                v.scalar_tensor_tensor(X[:, m, NB:CH], src[:, 0, NB:CH], mod[:, g, 0:1], X[:, m, NB:CH],
                                       ALU.mult, ALU.add)
                n.up(v.scalar_tensor_tensor(X[:, m, CH:T], src[:, 1, 0:CH], mod[:, g, 0:1], X[:, m, CH:T],
                                            ALU.mult, ALU.add), slot_dve)
                n.own(dve_step)
                n.up(v.tensor_tensor(X[:, m, 0:NB], X[:, m, 0:NB], upd_s[:, m % 2, :], ALU.add), x_ready)

            rstd_parts(0)
            def ada_mod(g):
                n.up(v.tensor_tensor(mod[:, 4 * g:4 * g + 4, :],
                                     bank_of(("ada", g))[:, 0:36].rearrange("p (m c) -> p m c", c=9),
                                     vec[:, V_ADAB + 4 * g:V_ADAB + 4 * g + 4].unsqueeze(2).broadcast_to((P, 4, 9)),
                                     ALU.add), emptied["D"])

            for g in range(ADA_FIRST):
                ada_mod(g)
            n.own(emptied["D"])
            dve.wait_ge(lf_act, 1)
            n.up(minus_hi(wf_lo[:], wf[:], wf_hi[:]), lf_dve)
            lo(0)
            lo(1)
            modulate(0)

            def log_forget():
                n.up(v.tensor_tensor(lf_a[:], bank_of("fl")[:, 0:40].rearrange("p (b h) -> p b h", h=8),
                                     bfg[:].unsqueeze(1).broadcast_to((P, 5, HEADS)), ALU.add), emptied["D"])
                n.own(emptied["D"])
                step(v.tensor_scalar(lf_b[:], lf_a[:], 0.0, None, ALU.min))
                n.up(v.scalar_tensor_tensor(lf[:], lf_a[:], -1.0, lf_a[:], ALU.mult, ALU.min), lf_dve)

            def tap(t, w):
                cw = vec[:, V_CW + w * 4 + t:V_CW + w * 4 + t + 1]
                n.own(conv_step, back=1)
                if w == 0:
                    o = v.tensor_scalar(CV[:, t, NB:T], UP[:, t, 0:L], cw, vec[:, V_CB + t:V_CB + t + 1],
                                        ALU.mult, ALU.add)
                else:
                    o = v.scalar_tensor_tensor(CV[:, t, NB:T], UP[:, t, w:w + L], cw, CV[:, t, NB:T],
                                               ALU.mult, ALU.add)
                n.up(o, conv_step)

            taps = [(t, w) for t0 in (0, 2) for w in range(CW) for t in (t0, t0 + 1)]
            n.count[conv_step.name] = 0
            for m in range(20):
                if m + 2 < N_OUT_EVEN:
                    lo(m + 2)
                if 4 <= m < 8:
                    t = m - 4
                    dve.wait_ge(slot_act, runs["in_even"][0] + m + 1)
                    v.tensor_tensor(UP[:, t, CW - 1:], AT[:, t, NB:T], gate[:, t % 2, NB:T], ALU.mult)
                    n.up(v.tensor_tensor(US[:, t, :, CW - 1], AT[:, t, 0:NB], gate[:, t % 2, 0:NB], ALU.mult), u_ready)
                    if m == 7:
                        dve.wait_ge(pad_ready, 1)
                        n.own(u_ready)
                if m >= 8:
                    for t, w in taps[(m - 8) * len(taps) // 12:(m - 7) * len(taps) // 12]:
                        tap(t, w)
            for t in range(4):
                step(v.tensor_tensor(usw[:], US[:, t, :, 0:CW],
                                     vec[:, V_CW + t:V_END:4].unsqueeze(1).broadcast_to((P, NB, CW)), ALU.mult))
                step(v.tensor_reduce(CV[:, t, 0:NB], usw[:], AX.X, ALU.add))
                n.own(conv_step)
                n.up(v.tensor_scalar(CV[:, t, 0:NB], CV[:, t, 0:NB], vec[:, V_CB + t:V_CB + t + 1], None, ALU.add),
                     cv_ready)
            log_forget()
            for g in range(ADA_FIRST, ADA_ATT):
                ada_mod(g)
            dve.wait_ge(lf_act, 3)
            n.up(v.tensor_tensor(lf[:], lf_b[:], lf[:], ALU.subtract), lf_dve)
            for t in range(4):
                for c in range(2):
                    cols = slice(c * CH, (c + 1) * CH)
                    n.own(cv_ready)
                    n.up(v.tensor_tensor(CV[:, t, cols], CV[:, t, cols], bank_of(("cm", t, c))[:, 0:CH], ALU.subtract),
                         emptied["D"])
            for t in range(4):
                for c in range(2):
                    n.up(v.tensor_scalar(CR[:, t, c * CH:(c + 1) * CH], bank_of(("cq", t, c))[:, 0:CH], EPS, None,
                                         ALU.add), emptied["D"])
            n.own(emptied["D"])
            n.up(v.reciprocal(CR[:], CR[:]), conv_var)
            dve.wait_ge(conv_act, 5)
            for t in range(4):
                n.up(v.tensor_tensor(CV[:, t, :], CV[:, t, :], CR[:, t, :], ALU.mult), conv_normed)
            for t in range(4):
                dve.wait_ge(ghi_ready, t + 1)
                n.up(minus_hi(G_lo[:, 4 + t, :], full[:, t % 2, :], G_hi[:, 4 + t, :]), g_ready)
            n.up(v.tensor_copy(cumul[:].rearrange("p b h -> p (b h)"), bank_of("cum")[:, 0:32]), emptied["D"])
            wait_emptied(dve, "vs")
            n.up(v.tensor_copy(vts[:], VT[:, :, 0:NB]), samp_dve)

            def weigh(h, q):
                x, w = h * TB + q, (q + 1) * P
                if q == 0:
                    wait_emptied(dve, ("ckb", h))
                n.up(v.scalar_tensor_tensor(SS[:, q, 0:w], bank_of(("s", h, q))[:, 0:w], FOX_SCALE,
                                            ckb[:, h % 2, 0:w], ALU.mult, ALU.subtract), emptied["D"])
                n.own(emptied["D"])
                n.up(v.tensor_reduce(nm[:, x:x + 1], SS[:, q, 0:w], AX.X, ALU.max, negate=True), max_ready)

            def inverse(x):
                dve.wait_ge(exp_ready, x + 1)
                n.up(v.reciprocal(ri[:, x:x + 1], rs[:, x:x + 1]), ri_ready)

            def dots(x):
                for g in range(2 * x, 2 * x + 2):
                    dve.wait_ge(prod_ready, g + 1)
                    n.up(v.tensor_reduce(SC[:, :, g // 8, g % 8], prod[:, g % 2, :].rearrange("p (h d) -> p h d", d=HD),
                                         AX.X, ALU.add), page_dot)

            for q in range(TB):
                weigh(0, q)
            inverse(0)
            for h in range(HEADS):
                for q in range(TB):
                    x = h * TB + q
                    if x + 1 < HEADS * TB:
                        inverse(x + 1)
                    if h + 1 < HEADS:
                        weigh(h + 1, q)
                    if ada_turned(x) is not None:
                        ada_mod(ada_turned(x))
                    dots(x)
                rows_ = slice(HD * (h % 2), HD * (h % 2) + HD)
                dve.wait_ge(ohi_ready, h + 1)
                n.up(minus_hi(G_lo[rows_, h // 2, NB:T], bank_of(("o", h))[rows_, :], G_hi[rows_, h // 2, NB:T]),
                     emptied["D"])

            ada_mod(N_ADA // 4 - 1)
            lo(N_OUT_EVEN)
            lo(N_OUT_EVEN + 1)
            wait_emptied(dve, "lt")
            step(v.memset(EX[:, :, :, 0], 0.0))
            for g in range(1, 8):
                step(v.tensor_tensor(EX[:, :, :, g], EX[:, :, :, g - 1], LT[:, :, :, g - 1], ALU.add))

            def hb(ap):
                return ap.rearrange("p (h b) -> p h b", b=NB)

            v.tensor_tensor(hb(small[:, 0, :]), EX[:, :, :, 7], LT[:, :, :, 7], ALU.add)
            v.tensor_tensor(hb(small[0:NB, 1, :]), con[0:NB, C_ID:C_ID + NB].unsqueeze(1).broadcast_to((NB, HEADS, NB)),
                            lf[0:NB, 0, :].unsqueeze(2).broadcast_to((NB, HEADS, NB)), ALU.mult)
            n.up(v.tensor_tensor(small[:, 3, 0:32].rearrange("p (t b) -> p t b", b=NB), QT[:, :, 0:NB], KT[:, :, 0:NB],
                                 ALU.mult), samp_dve)
            n.own(page_dot)
            sc = SC[:].rearrange("p h b g -> p (h b g)")
            n.up(v.tensor_tensor(sc, sc, bank_of("cc")[:, :], ALU.subtract), emptied["D"])
            wait_emptied(dve, "cl")
            n.up(v.scalar_tensor_tensor(small[:, 4, :], bank_of("sn")[:, 0:64], FOX_SCALE * HD, small[:, 2, :], ALU.mult,
                                        ALU.subtract), emptied["D"])
            n.own(emptied["D"])
            n.up(v.tensor_reduce(hb(small[:, 5, :]), SC[:], AX.X, ALU.max), samp_dve)
            n.up(v.tensor_reduce(small[0:64, 6, 0:1], bank_of("mt")[0:64, 0:P], AX.X, ALU.max), emptied["D"])
            n.own(emptied["D"])
            n.up(v.tensor_scalar(small[0:64, 7, :], ident[0:64, 0:64], small[0:64, 6, 0:1], None, ALU.mult), samp_dve)
            n.up(v.tensor_tensor(small[:, 5, :], bank_of("mb")[:, 0:64], small[:, 4, :], ALU.max), emptied["D"])
            n.own(emptied["D"])

            def over_pages(i):
                return hb(small[:, i, :]).unsqueeze(3).broadcast_to((P, HEADS, NB, 8))

            v.tensor_tensor(small[:, 4, :], small[:, 4, :], small[:, 5, :], ALU.subtract)
            n.up(v.tensor_tensor(SC[:], SC[:], over_pages(5), ALU.subtract), samp_dve)
            dve.wait_ge(samp_act, 2)
            n.up(v.tensor_reduce(hb(small[:, 6, :]), SC[:], AX.X, ALU.add), samp_dve)
            n.up(v.tensor_tensor(small[:, 0, :], bank_of("dn")[:, 0:64], small[:, 4, :], ALU.add), emptied["D"])
            n.own(emptied["D"])
            step(v.reciprocal(small[:, 0, :], small[:, 0, :]))
            v.tensor_tensor(small[:, 4, :], small[:, 4, :], small[:, 0, :], ALU.mult)
            n.up(v.tensor_tensor(SC[:], SC[:], over_pages(0), ALU.mult), samp_dve)
            n.own(samp_dve)
            for e in range(2):
                r = slice(HD * e, HD * e + HD)
                o = v.tensor_tensor(full_s[r, 0:4, :], vts[r], small[r, 4, :].rearrange("p (t e b) -> p t e b", e=2, b=NB)[:, :, e, :],
                                    ALU.mult)
            step(o)
            own_head = con[0:HEADS, C_ID:C_ID + HEADS].unsqueeze(2).broadcast_to((HEADS, HEADS, HD))
            for b in range(NB):
                dve.wait_ge(v_used, 8 * b + 8)
                if b >= 2:
                    dve.wait_ge(vm_used, b - 1)
                n.up(v.tensor_tensor(vm[:, b % 2, :].rearrange("p (h d) -> p h d", d=HD),
                                     Gp[b // 2 % 2][0:HEADS, b % 2, :].rearrange("p (h d) -> p h d", d=HD),
                                     own_head, ALU.mult), vm_ready)
            n.up(v.tensor_tensor(full_s[:, 0:4, :], full_s[:, 0:4, :],
                                 bank_of("ov")[:, 0:32].rearrange("p (t b) -> p t b", b=NB), ALU.add), emptied["D"])
            n.own(emptied["D"])
            step(v.tensor_copy(G_hi[:, 0:4, 0:NB], full_s[:, 0:4, :]))
            n.up(minus_hi(G_lo[:, 0:4, 0:NB], full_s[:, 0:4, :], G_hi[:, 0:4, 0:NB]), g_ready)

            for q in range(KD):
                lo(N_OUT_EVEN + q + 2)
                update(q, N_OUT_EVEN + q, mod_at(0, 2))

            def ffn(layer, i):
                rstd_parts(i)
                modulate(i)
                ghi0 = 4 + 38 * layer
                for t, ((_, kt), (n0, n1)) in enumerate(zip(THIRDS, ffn_starts(layer))):
                    base_a, base_d = runs[("gu", layer, t)]
                    done = sum(x for _, x in THIRDS[:t])

                    def body(i, n0=n0, base_a=base_a, done=done):
                        for j in range(4):
                            m = n0 + 4 * i + j + 2
                            if isinstance(i, int):
                                lo(m)
                            else:
                                lo(m, (j + 2) % 4, KD)
                            if j % 2 == 0:
                                dve.wait_ge(block_done, n0 + 4 * i + j + 2)
                                dve.wait_ge(slot_act, base_a + 2 * i + j // 2 + 1)
                                dve.wait_ge(ghi_ready, ghi0 + done + 2 * i + j // 2 - 1)
                                dst, up = full[:, j // 2, :], gate[:, j // 2, :]
                                v.tensor_tensor(dst.rearrange("p (c n) -> p c n", c=2), up.rearrange("p (c n) -> p c n", c=2),
                                                Gp[1][:, :, 0:CH], ALU.mult).then_inc(slot_dve, 1)
                            else:
                                dve.wait_ge(ghi_ready, ghi0 + done + 2 * i + j // 2 + 1)
                                g = ds(2 * i + j // 2, 1)
                                minus_hi(G_lo[:, g, :].rearrange("p o n -> p (o n)"), full[:, j // 2, :],
                                         G_hi[:, g, :].rearrange("p o n -> p (o n)")).then_inc(g_ready, 1)

                    with dve.Fori(0, kt // 2 - 1) as i_:
                        body(i_)
                    body(kt // 2 - 1)
                    n.skip(slot_dve, kt)
                    n.skip(g_ready, kt)
                    for q in range(KD):
                        lo(n1 + q + 2)
                        update(q, n1 + q, mod_at(layer, 5))

            ffn(0, 1)

            rstd_parts(2)
            modulate(2)
            cos, sin = con[:, C_COS:C_COS + T], con[:, C_SIN:C_SIN + T]

            def rope(x):
                a, b = QK[:, x, :], QK[:, x + 1, :]
                for out, c, s, op in ((x, cos, sin, ALU.subtract), (x + 1, sin, cos, ALU.add)):
                    v.tensor_tensor(QKR[:, out, :], a, c, ALU.mult)
                    step(v.tensor_tensor(rsd[:], b, s, ALU.mult))
                    n.up(v.tensor_tensor(QKR[:, out, :], QKR[:, out, :], rsd[:], op), rope_ready)
                    n.own(rope_ready)

            def tail(h, q):
                if q == 0:
                    for c in range(2):
                        cols = slice(c * CH, (c + 1) * CH)
                        bank = bank_of(("rm", h, c))
                        n.up(v.tensor_tensor(RVT[:, :, cols], RVT[:, :, cols],
                                             bank[:, 0:CH].unsqueeze(1).broadcast_to((P, 4, CH)), ALU.subtract),
                             emptied["D"])
                elif q == 1:
                    for c in range(2):
                        n.up(v.tensor_scalar(rsd[:, c * CH:(c + 1) * CH], bank_of(("rv", h, c))[:, 0:CH], EPS, None,
                                             ALU.add), emptied["D"])
                    n.own(emptied["D"])
                    n.up(v.reciprocal(rsd[:], rsd[:]), ret_dve)
                elif q < 4:
                    pair = (2 * q - 4, 2 * q - 3)
                    if q == 2:
                        dve.wait_ge(ret_act, 5 * h + 5)
                    for e in pair:
                        g = V_RG + 4 * h + e
                        n.up(v.scalar_tensor_tensor(RVT[:, e, :], RVT[:, e, :], vec[:, g:g + 1], rsd[:],
                                                    ALU.mult, ALU.mult), dve_step)
                    for i, e in enumerate(pair):
                        n.own(dve_step, back=1 - i)
                        n.up(v.tensor_tensor(GS[:, e, :], RVT[:, e, :], GS[:, e, :], ALU.mult), ret_gated)
                    for e in pair:
                        dve.wait_ge(ghi_ready, 26 + 4 * h + e + 1)
                        n.up(minus_hi(G_lo[:, 4 * (h % 2) + e, :], GS[:, e, :], G_hi[:, 4 * (h % 2) + e, :]), g_ready)
                else:
                    b = q - 4
                    if b >= 1:
                        add_row(h, b - 1)
                    dve.wait_ge(st_scaled, h * NB + b + 1)
                    bank = bank_of(("vb", h, b))
                    n.up(v.scalar_tensor_tensor(st[:, b % 2, 0, :], bank[:, :], kq_s[:, 2, b:b + 1],
                                                st[:, b % 2, 0, :], ALU.mult, ALU.add), emptied["D"])
                    n.up(v.scalar_tensor_tensor(st[:, b % 2, 1, :], bank[:, :], kq_s[:, 3, b:b + 1],
                                                st[:, b % 2, 1, :], ALU.mult, ALU.add), st_updated)

            def add_row(h, b):
                bank = bank_of(("so", h, b))
                if b == 0:
                    n.up(v.tensor_copy(osum[:], bank[0:NB, :]), emptied["D"])
                else:
                    n.own(emptied["D"])
                    n.up(v.tensor_tensor(osum[:], osum[:], bank[0:NB, :], ALU.add), emptied["D"])

            def norm_rows(h):
                add_row(h, NB - 1)
                n.own(emptied["D"])
                step(v.tensor_reduce(stat[:, 0:1], osum[:], AX.X, ALU.add))
                step(v.tensor_scalar(stat[:, 0:1], stat[:, 0:1], 1.0 / DV, None, ALU.mult))
                step(v.tensor_scalar(osum[:], osum[:], stat[:, 0:1], None, ALU.subtract))
                step(v.tensor_tensor(rsd[0:NB, 0:DV], osum[:], osum[:], ALU.mult))
                step(v.tensor_reduce(stat[:, 1:2], rsd[0:NB, 0:DV], AX.X, ALU.add))
                step(v.tensor_scalar(stat[:, 1:2], stat[:, 1:2], 1.0 / DV, EPS, ALU.mult, ALU.add))
                n.up(v.reciprocal(stat[:, 1:2], stat[:, 1:2]), osum_ready)
                dve.wait_ge(osum_root, h + 1)
                n.up(v.tensor_scalar(osum[:], osum[:], stat[:, 1:2], None, ALU.mult), osum_ready)

            def gate_rows(h):
                bank = bank_of(("sot", h))
                for e in range(4):
                    g = V_RG + 4 * h + e
                    o = v.scalar_tensor_tensor(gs_s[:, e, :], bank[:, e * NB:(e + 1) * NB], vec[:, g:g + 1],
                                               gs_s[:, e, :], ALU.mult, ALU.mult)
                n.up(o, emptied["D"])
                n.own(emptied["D"])
                n.own(g_ready)
                tiles = slice(4 * (h % 2), 4 * (h % 2) + 4)
                step(v.tensor_copy(G_hi[:, tiles, 0:NB], gs_s[:]))
                n.up(minus_hi(G_lo[:, tiles, 0:NB], gs_s[:], G_hi[:, tiles, 0:NB]), g_ready)

            step(v.memset(qz[:], 0.0))
            for h in range(RH + 1):
                for q in range(HEAD_BLOCKS):
                    if h < RH:
                        lo(head_start(h) + q + 2)
                        if q in (4, 6):
                            dve.wait_ge(slot_act, runs[("head", h)][0] + q - 2)
                            rope(q - 4)
                    if h > 0:
                        tail(h - 1, q)
                if h > 0:
                    norm_rows(h - 1)
                if h < RH:
                    n.own(st_updated)
                    step(v.tensor_copy(kq_s[:], QKR[:, :, 0:NB]))
                    for d in range(2):
                        o = v.tensor_copy(qz[:, d, 0:NB * NB:NB + 1], kq_s[:, d, :])
                    n.up(o, qs_ready)
                if h > 0:
                    gate_rows(h - 1)
                if h < RH:
                    n.own(g_ready)
                    dve.wait_ge(slot_act, runs[("head", h)][0] + HEAD_BLOCKS)
                    step(v.tensor_copy(gs_s[:], GS[:, :, 0:NB]))
                    dve.wait_ge(dec_loaded, 16 * (h + 1))
                    for j in range(TB):
                        w = L - j * P
                        n.up(v.tensor_tensor(AD[:, j, 0:w], bank_of(("ra", h, j))[:, 0:w], dec[:, 0:w], ALU.mult),
                             emptied["D"])
                if h in (2, RH):
                    n0 = out_start(0 if h == 2 else 1)
                    for q in range(KD):
                        lo(n0 + q + 2)
                        update(q, n0 + q, mod_at(1, 2))
            ffn(1, 3)
            rstd_parts(4)
            dve.wait_ge(rstd_ready, 5)
            for k in range(KD):
                n.up(v.scalar_tensor_tensor(YT[:, k, :], X[:, k, :], vec[:, V_FING + k:V_FING + k + 1], rstd[:],
                                            ALU.mult, ALU.mult), y_ready)
            for b in range(1, TB, 2):
                n.up(v.tensor_copy(yo[:, 5 + b, :], bank_of(("y", b, 1))[:, :]), emptied["D"])

        @block.gpsimd
        def _(pool):
            v = nc.gpsimd
            v.memset(UP[:, :, 0:CW - 1], 0.0).then_inc(pad_ready, 1)

            def divide(x):
                pool.wait_ge(ri_ready, x + 1)
                w = SS[:, x % TB, 0:(x % TB + 1) * P]
                v.tensor_scalar(w, w, ri[:, x:x + 1], 1.0, ALU.mult, ALU.mult).then_inc(p_ready, 1)

            divide(0)
            for h in range(HEADS):
                for q in range(TB):
                    x = h * TB + q
                    if x + 1 < HEADS * TB:
                        divide(x + 1)
                    for g in range(2 * x, 2 * x + 2):
                        pool.wait_ge(k_page[g % 4], 16 * (g // 4 + 1))
                        if g % 8 == 0:
                            wait_emptied(pool, ("qb", g // 8))
                        if g >= 2:
                            pool.wait_ge(page_dot, g - 1)
                        v.tensor_tensor(prod[:, g % 2, :], kp[:, g % 4, :], QB[:, g // 8, :], ALU.mult).then_inc(prod_ready, 1)
            pool.wait_ge(pages_loaded, 32)
            wait_emptied(pool, "vs")
            for s in range(2):
                pool.wait_ge(stage_stored[s], 16 * 4)
            v.indirect_dma_start(lg[:], None, A["cache_logf"][0].rearrange("n p h -> n (p h)"),
                                 bass.IndirectOffsetOnAxis(pt_col[:, 0:1], 0)).then_inc(lg_loaded, 16)

            pool.wait_ge(h_ready, KD * 3)

            def load_state(h, b):
                pool.dma_start(st[:, b % 2], A["state_ret"][0, b, h:h + 1, :, :].rearrange("o (d p) e -> p (o d) e", p=P)
                               if isinstance(h, int) else
                               A["state_ret"][0, b, ds(h, 1), :, :].rearrange("o (d p) e -> p (o d) e", p=P)
                               ).then_inc(st_loaded[b % 2], 16)

            for b in range(2):
                load_state(0, b)
            for h in range(RH):
                for b in range(NB):
                    g = h * NB + b
                    pool.wait_ge(st_updated, g + 1)
                    store(pool, A["ret_sample"][0, b, h].rearrange("(d p) e -> p d e", p=P), st[:, b % 2], st_stored[b % 2])
                    if g + 2 < RH * NB:
                        pool.wait_ge(st_stored[b % 2], 16 * (g // 2 + 1))
                        wait_job(pool, ("so", h, b))
                        load_state((g + 2) // NB, (g + 2) % NB)

        @block.sync
        def _(sp):
            sp.dma_start(con[:], A["consts"]).then_inc(x_loaded, 16)
            sp.dma_start(xn[:], A["x_prompt"][0].rearrange("(b p) d -> p b d", p=P)).then_inc(x_loaded, 16)
            sp.dma_start(xsn[:], A["x_sample"][:, 0, :]).then_inc(x_loaded, 16)
            sp.dma_start(cn[0:1, :], A["c_prompt"]).then_inc(x_loaded, 16)
            sp.dma_start(cn[1:9, :], A["c_sample"]).then_inc(x_loaded, 16)
            sp.dma_start(pt_row[:], A["page_table"].rearrange("b g -> (b g)").rearrange("(o n) -> o n", o=1)).then_inc(pages_loaded, 16)
            sp.dma_start(pt_col[:], A["page_table"].rearrange("b g -> (b g)").rearrange("(n o) -> n o", o=1)).then_inc(pages_loaded, 16)

            def columns(w, k0, kt, c0):
                return w[k0 * P:(k0 + kt) * P, ds(c0, P)].rearrange("(k p) m -> p k m", p=P)

            def load(j, src, kt=KD):
                sp.dma_start(raw[:, j, 0:kt, :], src).then_inc(raw_loaded[j], 16)

            def load_ada(m, layer, c0):
                load(m % 4, columns(A["ada_w"][layer], 0, KD, c0))

            for m in range(4 * ADA_FIRST):
                if m >= 4:
                    sp.wait_ge(ada_used, m - 3)
                load_ada(m, 0, m * P)

            def load_n(n, w, k0, c0, kt=KD):
                if n < 4:
                    sp.wait_ge(ada_used, 4 * ADA_FIRST + n - 3)
                elif N_OUT_EVEN <= n < N_OUT_EVEN + 4:
                    sp.wait_ge(ada_used, N_ADA + n - N_OUT_EVEN - 3)
                else:
                    sp.wait_ge(lo_ready, n - 3)
                load(n % 4, columns(w, k0, kt, c0), kt)

            w = A["w_in_even"][0]
            for n, c0 in enumerate([1544 + P * j for j in range(4)] + [2056 + P * j for j in range(4)]
                                   + [P * j for j in range(12)]):
                load_n(n, w, 0, c0)
            for m in range(4 * ADA_FIRST, 4 * ADA_ATT):
                if m < 4 * ADA_FIRST + 4:
                    sp.wait_ge(lo_ready, N_OUT_EVEN + m - 4 * ADA_FIRST - 3)
                else:
                    sp.wait_ge(ada_used, m - 3)
                load_ada(m, 0, m * P)

            for m in range(4 * ADA_ATT, 4 * ADA_ATT + 4):
                sp.wait_ge(ada_used, m - 3)
                load_ada(m, 0, m * P)
            sp.wait_ge(pages_loaded, 32)
            sp.wait_ge(g_ready, 4)

            for j in range(4):
                page(sp, j, cache_k, kp, j, k_page)
            in_layer0 = N_ADA // 8 - ADA_ATT
            for layer, first, end in ((0, 1, in_layer0), (1, in_layer0, NPG // 4)):
                with sp.Fori(first, end) as i:
                    for j in range(4):
                        sp.wait_ge(ada_used, 4 * ADA_ATT + 4 * i + j - 3)
                        load(j, columns(A["ada_w"][layer], 0, KD, (4 * ADA_ATT - 48 * layer + j) * P + i * 512))
                        sp.wait_ge(prod_ready, 4 * i + j - 3)
                        page(sp, 4 * i + j, cache_k, kp, j, k_page)
            for j in range(4):
                load_n(N_OUT_EVEN + j, A["w_out_even"][0], 0, P * j)
            sp.wait_ge(v_stored, 16 * TB)
            wait_job(sp, ("o", HEADS - 1))
            value_pages(sp, 0)
            for j in range(4, 8):
                load_n(N_OUT_EVEN + j, A["w_out_even"][0], 0, P * j)

            def ffn(layer):
                wg, wu, wd = A["w_ffn_gate"][layer], A["w_ffn_up"][layer], A["w_ffn_down"][layer]
                for (k0, kt), (n0, n1) in zip(THIRDS, ffn_starts(layer)):
                    with sp.Fori(0, kt // 2) as i:
                        for j in range(4):
                            sp.wait_ge(lo_ready, n0 + 4 * i + j - 3)
                            load(j, columns(wu if j % 2 else wg, 0, KD, (k0 + j // 2) * P + 2 * P * i))
                    with sp.Fori(0, 2) as i:
                        for j in range(4):
                            sp.wait_ge(lo_ready, n1 + 4 * i + j - 3)
                            load(j, columns(wd, k0, kt, 4 * P * i + j * P), kt)

            ffn(0)
            w = A["w_in_odd"][0]
            for h in range(RH):
                cols = ([h * DK + P * j for j in range(2)] + [D + h * DK + P * j for j in range(2)]
                        + [2 * D + h * DV + P * j for j in range(4)] + [4 * D + h * DV + P * j for j in range(4)])
                for j in range(HEAD_BLOCKS):
                    load_n(head_start(h) + j, w, 0, cols[j])
                if h >= 1:
                    wait_emptied(sp, ("ra", h - 1, TB - 1))
                sp.dma_start(dec[:], A["decay"][h]).then_inc(dec_loaded, 16)
                if h >= 2:
                    for j in range(KD):
                        load_n(out_start(h - 2) + j, A["w_out_odd"][0], (h - 2) * KD, P * j)
            ffn(1)
            for f in range(2):
                cols = slice(f * 512, (f + 1) * 512)
                for b in range(TB):
                    wait_emptied(sp, ("y", b, f))
                    store(sp, A["y_prompt"][0, b * P:(b + 1) * P, cols], yo[:, 5 * f + b, :])
                wait_emptied(sp, ("ys", f))
                store(sp, A["y_sample"][:, 0, cols], yo[0:NB, 5 * f + TB, :])
            for s in {s.name: s for s in outs}.values():
                sp.wait_ge(s, 16 * sum(o.name == s.name for o in outs))


def constants():
    c = np.zeros((P, C_END), np.float32)
    i = np.arange(P)
    c[:, C_ID:C_ID + P] = np.eye(P)
    c[:, C_MEAN:C_MEAN + P] = 1.0 / D
    c[:, C_B64:C_B64 + P] = (i[:, None] // 64 == i[None, :] // 64) / 64.0
    c[:, C_M512:C_M512 + P] = 1.0 / DV
    c[:, C_ONE:C_ONE + P] = 1.0
    c[:, C_TRI:C_TRI + P] = i[:, None] <= i[None, :]
    c[:, C_NEG:C_NEG + P] = np.where(i[None, :] <= i[:, None], 0.0, MASKED)
    inv = (np.float32(1) / np.power(np.float32(10000), np.linspace(0, 1, P, dtype=np.float32))).astype(np.float32)
    pos = np.concatenate([np.full(NB, PAST), np.arange(L)]).astype(np.float32)
    angle = (pos[None, :] * inv[:, None]).astype(np.float32).astype(np.float64)
    c[:, C_COS:C_COS + T] = np.cos(angle)
    c[:, C_SIN:C_SIN + T] = np.sin(angle)
    for b in range(TB):
        for h in range(RH):
            c[:, C_KDEC + b * RH + h] = GAMMA[h] ** (L - 1 - (b * P + i))
    dist = np.arange(L)[None, :] - i[:, None]
    decay = np.stack([np.where(dist >= 0, g ** np.maximum(dist, 0.0), 0.0) for g in GAMMA]).astype(np.float32)
    return c, decay


_INS = ["x_prompt", "x_sample", "cache_k", "cache_v", "cache_logf", "state_conv", "state_ret", "page_table",
        "c_prompt", "c_sample", "ada_w", "ada_b", "norm_mix_g", "norm_ffn_g", "w_in_even", "b_forget",
        "conv_w", "conv_b", "conv_norm_g", "conv_norm_b", "w_out_even", "w_in_odd", "ret_norm_g", "w_out_odd",
        "w_ffn_gate", "w_ffn_up", "w_ffn_down", "final_norm_g"]
_OUTS = [("y_prompt", (1, L, D)), ("y_sample", (NB, 1, D)), ("k_prompt", (1, 1, L, HEADS, HD)),
         ("v_prompt", (1, 1, L, HEADS, HD)), ("logf_prompt", (1, 1, L, HEADS)),
         ("conv_prompt", (1, 1, CW - 1, 512)), ("ret_prompt", (1, 1, RH, DK, DV)),
         ("k_sample", (1, NB, 1, HEADS, HD)), ("v_sample", (1, NB, 1, HEADS, HD)),
         ("logf_sample", (1, NB, 1, HEADS)), ("conv_sample", (1, NB, CW - 1, 512)),
         ("ret_sample", (1, NB, RH, DK, DV))]


def kernel(**inputs):
    import concourse.bacc as bacc
    from concourse.bass_utils import run_bass_kernel_spmd

    nc = bacc.Bacc("TRN2", target_bir_lowering=False, num_devices=1)
    arrays = {f"in_{n}": np.ascontiguousarray(inputs[n]) for n in _INS}
    arrays["in_consts"], arrays["in_decay"] = constants()
    aps = {n[3:]: nc.dram_tensor(n, a.shape, mybir.dt.from_np(a.dtype), kind="ExternalInput").ap()
           for n, a in arrays.items()}
    for n, shape in _OUTS:
        aps[n] = nc.dram_tensor(f"out_{n}", shape, mybir.dt.float32, kind="ExternalOutput").ap()
    build(nc, aps)
    r = run_bass_kernel_spmd(nc, [arrays], core_ids=[0])
    return tuple(r.results[0][f"out_{n}"] for n, _ in _OUTS)
```

```python
import math
from contextlib import ExitStack

import concourse.bass as bass
import concourse.mybir as mybir
import numpy as np

P = 128
D = 1024
KD = D // P
L = 512
TB = L // P
NB = 8
T = NB + L
CH = T // 2
HEADS = 8
HD = 64
PAST = 1024
PAGES = PAST // P
NPG = NB * PAGES
CW = 31
RH = 4
DK = 256
DV = 512
FF = 2816
EPS = 1e-6
FOX_SCALE = HD ** -0.5
MASKED = -1e30
THIRDS = ((0, 8), (8, 8), (16, 6))
assert sum(n for _, n in THIRDS) * P == FF
GAMMA = [1.0 - 2.0 ** (-5.0 - h) for h in range(RH)]

C_ID, C_B64, C_TRI, C_NEG = (P * i for i in range(4))
C_MEAN, C_M512, C_ONE = (4 * P + i for i in range(3))
C_GRP = 4 * P + 4
C_COS = C_GRP + 16
C_SIN = C_COS + T
C_KDEC = C_SIN + T
C_END = C_KDEC + TB * RH

N_IN_EVEN = 0
N_OUT_EVEN = 20
N_FFN = (28, 160)
N_ODD = 96
N_BLOCKS = 228
HEAD_BLOCKS = 12
N_ADA = 96
ADA_FIRST = 4
ADA_ATT = 8
ADA_NORM = 18
ADA_LATE = 22


def ada_by(x):
    return 4 * ADA_ATT + 4 * (ADA_NORM - 1 - ADA_ATT) * (x + 1) // (HEADS * TB)


def ada_rows_at(x):
    return ada_by(x) // 4 - 1 if ada_by(x) // 4 > ada_by(x - 1) // 4 else None


def ada_turned(x):
    return ada_rows_at(x - 1) if x > 0 else None


LATE_BLOCKS = (2, 2, 1, 1, 1, 1)
LATE_TURNS = {4: ADA_LATE, 7: ADA_LATE + 1}


def ada_norm_groups(i):
    return range(ADA_NORM + 2 * (i - 1), ADA_NORM + 2 * i) if i in (1, 2) else ()


def ffn_starts(layer):
    at, out = N_FFN[layer], []
    for _, tiles in THIRDS:
        out.append((at, at + 2 * tiles))
        at += 2 * tiles + KD
    return out


def head_start(h):
    return N_ODD + HEAD_BLOCKS * h + (KD if h == RH - 1 else 0)


def state_at(h, q):
    if h == RH:
        return q + 2 if q < NB - 2 else None
    return q - 4 if h > 0 and q >= 4 else None


def query_at(h, q):
    if h == RH:
        return q + 1 if 1 <= q < NB - 1 else None
    return state_at(h, q)


def out_start(pair):
    return head_start(2 + pair) + HEAD_BLOCKS


def k_tiles(n):
    for layer in range(2):
        down = ffn_starts(layer)[2][1]
        if down <= n < down + KD:
            return THIRDS[2][1]
    return KD


V_MIXG, V_FFNG, V_FING, V_CB, V_CG, V_CNB, V_RG = 0, 16, 32, 40, 44, 48, 52
V_ROWS = 68
V_ADAB = V_ROWS
V_CW = V_ADAB + N_ADA
V_END = V_CW + CW * 4


def psum_jobs():
    jobs = [(("xT", k), "D") for k in range(KD)] + [("xs", "D")]
    jobs += [("cT", "D"), ("vec", "D"), (("sc", 0), "D"), (("sc", 1), "D")]

    def norm(i):
        return [(("ss", i, 0), "D"), (("ss", i, 1), "D")]

    jobs += norm(0) + [(("ada", g), "D") for g in range(ADA_FIRST)] + [(("flT", c), "A") for c in range(2)] + [("fl", "D")]
    jobs += [(("cm", t, c), "D") for t in range(4) for c in range(2)]
    jobs += [("cpo", "A"), ("cso", "A")]
    jobs += [("qs", "A")] + [(("qb", b), "A") for b in range(NB)]
    jobs += [(("ada", g), "D") for g in range(ADA_FIRST, ADA_ATT)]
    jobs += [(("cq", c), "D") for c in range(2)] + [(("cb", t, c), "D") for t in range(4) for c in range(2)]
    jobs += [("cum", "D"), ("cumT", "A")]
    jobs += [(("kn", tb), "A") for tb in range(TB)] + [(("vn", tb), "A") for tb in range(TB)]
    jobs += [("ks", "A"), ("vs", "A")]
    jobs += [(("ckb", 0), "A")] + [(("s", 0, q), "D") for q in range(TB)]
    for h in range(HEADS):
        if h + 1 < HEADS:
            jobs += [(("ckb", h + 1), "A")]
        for q in range(TB):
            jobs += [(("pt", h, q), "A")]
            if h + 1 < HEADS:
                jobs += [(("s", h + 1, q), "D")]
            if ada_turned(h * TB + q) is not None:
                jobs += [(("ada", ada_turned(h * TB + q)), "D")]
        jobs += [(("o", h), "D")]
    jobs += [(("ada", ADA_NORM - 2), "D")]
    jobs += [("lt", "A"), ("cc", "D"), ("cl", "A"), ("sn", "D")]
    jobs += [("mt", "D"), ("mb", "D"), ("dn", "D"), ("ov", "D"), (("ada", ADA_NORM - 1), "D")]
    for i in (1, 2):
        jobs += norm(i) + [(("adr", g), "A") for g in ada_norm_groups(i)]
        jobs += [(("ada", g), "D") for g in ada_norm_groups(i)]
    for h in range(RH + 1):
        for q in range(HEAD_BLOCKS):
            b = state_at(h, q)
            if b is not None:
                jobs += [(("vb", h - 1, b), "D")]
            b = query_at(h, q)
            if b is not None:
                jobs += [(("so", h - 1, b), "D")]
            if h > 0 and q == 0:
                jobs += [(("rm", h - 1, c), "D") for c in range(2)]
            if h > 0 and q == 1:
                jobs += [(("rv", h - 1, c), "D") for c in range(2)]
            if h == RH and q in LATE_TURNS:
                jobs += [(("ada", LATE_TURNS[q]), "D")]
        if h < RH:
            jobs += [(("rvn", h, tb), "A") for tb in range(TB)]
            jobs += [(("rvs", h), "A")]
            jobs += [(("rkn", h, tb), "A") for tb in range(TB)]
        if h < RH:
            jobs += [(("ra", h, j), "D") for j in range(TB)]
            jobs += [(("rst", h, d), "A") for d in range(2)]
        if h > 0:
            jobs += [(("sot", h - 1), "D")]
        if h < RH:
            for e in range(4):
                early = h == RH - 1 and e < 2
                jobs += [(("vb", h, e), "D")] if early else []
                jobs += [(("ro", h, e), "A")]
                jobs += [(("so", h, e), "D")] if early else []
    jobs += norm(3) + norm(4)
    for f in range(2):
        jobs += [(("y", tb, f), "D" if tb % 2 and f else "A") for tb in range(TB)] + [(("ys", f), "A")]
    return jobs


class Jobs:

    def __init__(self):
        jobs = psum_jobs()
        self.index = {name: i for i, (name, _) in enumerate(jobs)}
        assert len(self.index) == len(jobs)
        self.engine = [e for _, e in jobs]
        count = {"A": 0, "D": 0}
        self.nth = []
        for e in self.engine:
            count[e] += 1
            self.nth.append(count[e])

    def bank(self, name):
        return self.index[name] % 4

    def done(self, name):
        return self.index[name] + 1

    def emptied(self, name):
        i = self.index[name]
        return self.engine[i], self.nth[i]


class Tally:

    def __init__(self, eng):
        self.eng, self.count = eng, {}

    def up(self, instruction, sem):
        instruction.then_inc(sem, 1)
        self.count[sem.name] = self.count.get(sem.name, 0) + 1

    def skip(self, sem, n):
        self.count[sem.name] = self.count.get(sem.name, 0) + n

    def own(self, sem, back=0):
        count = self.count.get(sem.name, 0)
        if count > back:
            self.eng.wait_ge(sem, count - back)


def build(nc, A):
    f32, f32r, i32 = mybir.dt.float32, mybir.dt.float32r, mybir.dt.int32
    ACT, ALU, AX = mybir.ActivationFunctionType, mybir.AluOpType, mybir.AxisListType
    ds = bass.ds
    jobs = Jobs()

    at = [(nc.sbuf_base + 63) // 64 * 64]

    def sb(name, shape, dtype=f32):
        t = nc.alloc_sbuf_tensor_at(name, shape, dtype, offset=at[0])
        at[0] += (math.prod(shape[1:]) * 4 + 31) // 32 * 32
        assert at[0] <= nc.sbuf_usable_end, (name, at[0])
        return t

    X = sb("X", [P, KD, T])
    con = sb("con", [P, C_END])
    vec = sb("vec", [P, V_END])
    mod = sb("mod", [P, N_ADA, 9])
    coef = sb("coef", [P, KD, 9])
    raw = sb("raw", [P, 4, KD, P])
    w_hi = sb("w_hi", [P, 4, KD, P], f32r)
    w_lo = sb("w_lo", [P, 4, KD, P], f32r)
    lf = sb("lf", [P, 5, HEADS])
    lf_a = sb("lf_a", [P, 5, HEADS])
    lf_b = sb("lf_b", [P, 5, HEADS])
    bfg = sb("bfg", [P, HEADS])
    cT = sb("cT", [P, KD, 9])
    g_at = at[0]
    G_hi = sb("G_hi", [P, KD, T], f32r)
    gl_at = at[0]
    G_lo = sb("G_lo", [P, KD, T], f32r)
    h_at = at[0]
    H_hi = sb("H_hi", [P, KD, T], f32r)
    H_lo = sb("H_lo", [P, KD, T], f32r)
    free_at = at[0]
    sq = sb("sq", [P, 2, T])
    sqa = sb("sqa", [P, T])
    rstd = sb("rstd", [P, T])
    scaled_at = at[0]
    scaled = sb("scaled", [P, 2, T])
    full = sb("full", [P, 2, T])
    full_s = sb("full_s", [P, KD, NB])
    upd_s = sb("upd_s", [P, 2, NB])
    gate_at = at[0]
    gate = sb("gate", [P, 2, T])
    scratch_end = max(at[0], free_at + 10 * 512 * 4)
    at[0] = h_at
    xn = sb("xn", [P, TB, D])
    xsn = sb("xsn", [NB, D])
    cn = sb("cn", [9, D])
    cn_silu = sb("cn_silu", [9, D])
    rows_s = sb("rows_s", [120, 2, 512])
    at[0] = scratch_end
    QT = sb("QT", [P, 4, T])
    KT = sb("KT", [P, 4, T])
    vt_at = at[0]
    VT = sb("VT", [P, 4, T])
    us_at = at[0]
    US = sb("US", [P, 4, NB, CW + 1])
    SC = sb("SC", [P, HEADS, NB, 8])
    small = sb("small", [P, 8, 64])
    up_at = at[0]
    UP = sb("UP", [P, 4, CW - 1 + L])
    usw = sb("usw", [P, NB, CW])
    even_end = at[0]
    at[0] = scratch_end
    wf = sb("wf", [P, KD, P])
    wf_hi = sb("wf_hi", [P, KD, P], f32r)
    wf_lo = sb("wf_lo", [P, KD, P], f32r)
    assert at[0] <= vt_at
    at[0] = scaled_at
    flt = sb("flt", [HEADS, T])
    at[0] = vt_at
    rows_v = sb("rows_v", [V_ROWS, P])
    rows_a = sb("rows_a", [N_ADA, P])
    rows_c = sb("rows_c", [CW * 4, P])
    at[0] = vt_at
    AT = sb("AT", [P, 4, T])
    at[0] = g_at
    CV = sb("CV", [P, 4, T])
    at[0] = gl_at
    CR = sb("CR", [8, T])
    back = sb("back", [8, 4 * P])
    at[0] = h_at
    QB = sb("QB", [P, NB, 512])
    VN = sb("VN", [P, TB, 512])
    PTS = sb("PTS", [P, TB, 512])
    assert at[0] <= free_at
    at[0] = h_at + NB * 512 * 4
    sq4 = sb("sq4", [P, 4, T])
    at[0] = free_at
    SS = sb("SS", [P, TB, 512])
    kp = sb("kp", [P, 4, 512])
    prod = sb("prod", [P, 2, 512])
    assert at[0] <= scratch_end
    at[0] = free_at
    LT = sb("LT", [P, HEADS, NB, 8])
    EX = sb("EX", [P, HEADS, NB, 8])
    at[0] = h_at + NB * 512 * 4
    vp = sb("vp", [P, 8, 512])
    at[0] = gate_at
    rows_early = sb("rows_early", [9, 2, 512])
    at[0] = vt_at
    rows_late = sb("rows_late", [9, 2, 512])
    at[0] = scratch_end
    spare = sb("spare", [P, 8, KD, P])
    rows_norm = sb("rows_norm", [9, 2, 512])
    at[0] = h_at
    vm = sb("vm", [HEADS, 2, 512])
    at[0] = up_at
    ckb = sb("ckb", [P, 2, L])
    ko_at = at[0]
    kn_out = sb("kn_out", [P, 2, 512])
    assert at[0] <= even_end
    at[0] = us_at
    qsn = sb("qsn", [NB, 512])
    cum8 = sb("cum8", [HEADS, L])
    at[0] = even_end
    cumul = sb("cumul", [P, TB, HEADS])
    nm = sb("nm", [P, HEADS * TB])
    rs = sb("rs", [P, HEADS * TB])
    ri = sb("ri", [P, HEADS * TB])
    pt_row = sb("pt_row", [1, NPG], i32)
    pt_col = sb("pt_col", [NPG, 1], i32)
    at[0] = ko_at
    lg = sb("lg", [NPG, P * HEADS])
    vts = sb("vts", [P, 4, NB])
    at[0] = free_at
    dec = sb("dec", [P, L])
    raw_at = at[0]
    QK = sb("QK", [P, 4, T])
    qkr_at = at[0]
    QKR = sb("QKR", [P, 4, T])
    RVT = sb("RVT", [P, 4, T])
    rvn_at = at[0]
    RVN = sb("RVN", [P, TB, DV])
    KDN = sb("KDN", [P, TB, DK])
    GS = sb("GS", [P, 4, T])
    st = sb("st", [P, 2, 2, DV])
    so = sb("so", [P, 2, DV])
    rsd = sb("rsd", [P, T])
    vsn = sb("vsn", [NB, DV])
    osum = sb("osum", [NB, DV])
    kq_s = sb("kq_s", [P, 4, NB])
    gs_s = sb("gs_s", [P, 4, NB])
    qz = sb("qz", [P, 2, NB * NB])
    stat = sb("stat", [NB, 2])
    at[0] = raw_at
    AD = sb("AD", [P, TB, L])
    at[0] = raw_at
    st_a = sb("st_a", [P, 2, 2, DV])
    at[0] = h_at
    late = sb("late", [P, 8, KD, P])
    at[0] = qkr_at
    st_q = sb("st_q", [P, 2, 2, DV])
    at[0] = rvn_at
    RSQ = sb("RSQ", [P, 4, T])
    at[0] = g_at
    YT = sb("YT", [P, KD, T])
    yo = sb("yo", [P, 10, 512])
    assert at[0] <= free_at

    ctx = ExitStack()
    with ctx:
        def sem(name):
            return ctx.enter_context(nc.semaphore(name))

        Gp = [ctx.enter_context(nc.psum_tensor(f"product{i}", [P, 2, 512], f32)) for i in range(2)]
        Jp = [ctx.enter_context(nc.psum_tensor(f"job{i}", [P, 512], f32)) for i in range(4)]

        ident_loaded, xn_loaded = sem("ident_loaded"), [sem(f"xn_loaded{i}") for i in range(2)]
        x_loaded, rows_loaded, pages_loaded = sem("x_loaded"), sem("rows_loaded"), sem("pages_loaded")
        raw_loaded = [sem(f"raw_loaded{i}") for i in range(4)]
        k_page = [sem(f"k_page{i}") for i in range(4)]
        v_page = [sem(f"v_page{i}") for i in range(8)]
        spare_loaded = [sem(f"spare_loaded{i}") for i in range(8)]
        late_used, late_taken = sem("late_used"), sem("late_taken")
        lg_loaded, dec_loaded = sem("lg_loaded"), sem("dec_loaded")
        st_loaded = [sem(f"st_loaded{i}") for i in range(6)]
        st_stored = [sem(f"st_stored{i}") for i in range(6)]
        stage_stored = [sem(f"stage_stored{i}") for i in range(2)]
        out_done, v_stored = sem("out_done"), sem("v_stored")
        block_done, ada_used, job_done = sem("block_done"), sem("ada_used"), sem("job_done")
        ada_taken = sem("ada_taken")
        sq_used, v_used = sem("sq_used"), sem("v_used")
        vm_used = sem("vm_used")
        slot_act, slot_dve = sem("slot_act"), sem("slot_dve")
        emptied = {"A": sem("emptied_act"), "D": sem("emptied_dve")}
        c_silu, sq_ready, rstd_ready = sem("c_silu"), sem("sq_ready"), sem("rstd_ready")
        full_ready, hh_ready, hi_ready = sem("full_ready"), sem("hh_ready"), sem("hi_ready")
        ghi_ready, exp_ready, lf_act = sem("ghi_ready"), sem("exp_ready"), sem("lf_act")
        conv_act, ohi_ready, st_scaled = sem("conv_act"), sem("ohi_ready"), sem("st_scaled")
        samp_act, ret_act, osum_root = sem("samp_act"), sem("ret_act"), sem("osum_root")
        x_ready, var_ready, vm_ready = sem("x_ready"), sem("var_ready"), sem("vm_ready")
        scaled_ready, h_ready, lo_ready = sem("scaled_ready"), sem("h_ready"), sem("lo_ready")
        g_ready, dve_step, lf_dve = sem("g_ready"), sem("dve_step"), sem("lf_dve")
        u_ready, cv_ready, conv_var = sem("u_ready"), sem("cv_ready"), sem("conv_var")
        conv_step, ret_gated = sem("conv_step"), sem("ret_gated")
        max_ready, ri_ready, page_dot = sem("max_ready"), sem("ri_ready"), sem("page_dot")
        samp_dve, rope_ready = sem("samp_dve"), sem("rope_ready")
        ret_dve, st_updated, qs_ready = sem("ret_dve"), sem("st_updated"), sem("qs_ready")
        osum_ready, y_ready = sem("osum_ready"), sem("y_ready")
        pair_dve = sem("pair_dve")
        pad_ready, p_ready, prod_ready = sem("pad_ready"), sem("p_ready"), sem("prod_ready")
        conv_pool, pair_pool, tap_pool = sem("conv_pool"), sem("pair_pool"), sem("tap_pool")
        outs = []

        def store(eng, dst, src, done=None):
            s = done or out_done
            outs.append(s)
            eng.dma_start(dst, src).then_inc(s, 16)

        cache_k = A["cache_k"][0].rearrange("n p h d -> n p (h d)")
        cache_v = A["cache_v"][0].rearrange("n p h d -> n p (h d)")

        def page(eng, g, cache, ring, j, arrived):
            n = eng.value_load(pt_row[0:1, ds(g, 1)], min_val=0, max_val=cache.shape[0] - 1)
            eng.dma_start(ring[:, j, :], cache[ds(n, 1), :, :].rearrange("o p n -> p (o n)")).then_inc(arrived[j], 16)

        def value_pages(eng, first):
            for j in range(first, PAGES, 2):
                page(eng, j, cache_v, vp, j, v_page)
            with eng.Fori(1, NB) as i:
                for j in range(first, PAGES, 2):
                    eng.wait_ge(v_used, PAGES * i + j - PAGES + 1)
                    page(eng, PAGES * i + j, cache_v, vp, j, v_page)

        def wait_job(eng, name):
            eng.wait_ge(job_done, jobs.done(name))

        def wait_emptied(eng, name):
            e, n = jobs.emptied(name)
            eng.wait_ge(emptied[e], n)

        ident = con[:, C_ID:C_ID + P]
        ones = con[:, C_ONE:C_ONE + 1].broadcast_to((P, P))
        one_col = con[:, C_ONE:C_ONE + 1]

        runs, ra, rd = {}, 2, 2
        for name, a, d in (
            [("in_even", 20, 0), ("out_even", 0, KD)]
            + [x for t, (_, n) in enumerate(THIRDS) for x in ((("gu", 0, t), n, n), (("dn", 0, t), 0, KD))]
            + [(("head", h), HEAD_BLOCKS, 0) for h in range(3)] + [(("out", 0), 0, KD), (("head", 3), HEAD_BLOCKS, 0), (("out", 1), 0, KD)]
            + [x for t, (_, n) in enumerate(THIRDS) for x in ((("gu", 1, t), n, n), (("dn", 1, t), 0, KD))]
        ):
            runs[name] = (ra, rd)
            ra, rd = ra + a, rd + d
        N_ROW_LOADS, G_FFN = 13, (5, 47)
        X_BEFORE = (0, 0, 24, 40, 64)
        L_OF = (0, 0, 1, 1)

        def raw_count(n, ada=False):
            if ada:
                before = 0 if n < 4 * ADA_FIRST else N_OUT_EVEN
            else:
                before = 4 * ADA_FIRST if n < N_OUT_EVEN else 4 * ADA_NORM
            return 16 * ((n + before) // 4 + 1)

        def ada_rows(g):
            if g >= ADA_LATE:
                return dec[0:9, :]
            return (rows_early if g < ADA_ATT else rows_late if g < ADA_NORM else rows_norm)[:, g % 2, :]

        def st_slot(h, b):
            return b % 2 if h < RH - 1 or b >= 6 else b

        def st_load(h, b):
            if h < RH - 1 or b < 2:
                return (h * NB + b) // 2 + 1
            return 1 if b < 6 else (RH - 1) * NB // 2 + 2

        def state(h, b):
            s = st_slot(h, b)
            return (st, st_q, st_a)[s // 2][:, s % 2]

        def spare_states_left(eng):
            for s in range(2, 6):
                eng.wait_ge(st_stored[s], 16)

        def mod_at(layer, part):
            return layer * 48 + part * KD

        block = ctx.enter_context(nc.Block())

        @block.tensor
        def _(pe):
            def open_job(name):
                i = jobs.index[name]
                if i >= 4:
                    pe.wait_ge(emptied[jobs.engine[i - 4]], jobs.nth[i - 4])
                return Jp[i % 4]

            def close(mm):
                mm.then_inc(job_done, 1)

            def turn(out, src, n=P):
                return pe.transpose(out, src, ident[0:n, 0:n])

            pe.wait_ge(ident_loaded, 16)
            for k in range(KD):
                if k % 4 == 0:
                    pe.wait_ge(xn_loaded[k // 4], 16)
                bank = open_job(("xT", k))
                for b in range(TB):
                    mm = turn(bank[:, b * P:(b + 1) * P], xn[:, b, k * P:(k + 1) * P])
                close(mm)
            bank = open_job("xs")
            pe.wait_ge(x_loaded, 64)
            for k in range(KD):
                mm = turn(bank[:, k * NB:(k + 1) * NB], xsn[:, k * P:(k + 1) * P], NB)
            close(mm)
            bank = open_job("cT")
            pe.wait_ge(c_silu, 1)
            for k in range(KD):
                mm = turn(bank[:, k * 9:(k + 1) * 9], cn_silu[:, k * P:(k + 1) * P], 9)
            close(mm)
            bank = open_job("vec")
            pe.wait_ge(rows_loaded, 16 * N_ROW_LOADS)
            turn(bank[:, 0:V_ROWS], rows_v[:], V_ROWS)
            turn(bank[:, V_ADAB:V_ADAB + N_ADA], rows_a[:], N_ADA)
            close(turn(bank[:, V_CW:V_END], rows_c[:], CW * 4))
            for g in range(2):
                bank = open_job(("sc", g))
                for t in range(4):
                    mm = turn(bank[:, t * 120:(t + 1) * 120], rows_s[:, g, t * P:(t + 1) * P], 120)
                close(mm)

            def norm(i):
                pe.wait_ge(sq_used, (KD - 2) * (i + 1))
                banks = [open_job(("ss", i, c)) for c in range(2)]

                def mean(c, src, **kw):
                    return pe.matmul(banks[c][:, 0:CH], con[:, C_MEAN:C_MEAN + 1].broadcast_to((P, P)),
                                     src[:, c * CH:(c + 1) * CH], **kw)

                for c in range(2):
                    mean(c, sqa, start=True, stop=False)
                pe.wait_ge(sq_ready, KD * (i + 1))
                for c in range(2):
                    close(mean(c, sq[:, 1, :], start=False, stop=True))
                for g in ada_norm_groups(i):
                    bank = open_job(("adr", g))
                    for j in range(4):
                        b = 4 * (g % 2) + j
                        pe.wait_ge(spare_loaded[b], 16 * i)
                        for k in range(KD):
                            mm = pe.matmul(bank[0:9, j * P:(j + 1) * P], cT[:, k, :], spare[:, b, k, :],
                                           start=k == 0, stop=k == KD - 1)
                    close(mm)

            def norm_turns(i):
                for g in ada_norm_groups(i):
                    ada_turn(g)

            norm(0)

            def ada_block(m):
                g, j = m // 4, m % 4
                if j == 0 and g >= 2:
                    pe.wait_ge(ada_taken, g - 1)
                pe.wait_ge(raw_loaded[j], raw_count(m, ada=True))
                for k in range(KD):
                    mm = pe.matmul(Gp[g % 2][0:9, 0, j * P:(j + 1) * P], cT[:, k, :], raw[:, j, k, :],
                                   start=k == 0, stop=k == KD - 1)
                mm.then_inc(ada_used, 1)

            def ada_turn(g):
                bank = open_job(("ada", g))
                if g < ADA_NORM:
                    pe.wait_ge(ada_taken, g + 1)
                elif g < ADA_LATE:
                    wait_emptied(pe, ("adr", g))
                else:
                    pe.wait_ge(late_taken, g - ADA_LATE + 1)
                for j in range(4):
                    mm = turn(bank[:, j * 9:(j + 1) * 9], ada_rows(g)[:, j * P:(j + 1) * P], 9)
                close(mm)

            def ada_groups(first, end, begun=0):
                for g in range(first, end):
                    for j in range(4 if g >= first + begun else 0):
                        ada_block(4 * g + j)
                    if g > first:
                        ada_turn(g - 1)
                ada_turn(end - 1)

            wait_emptied(pe, "cT")
            ada_groups(0, ADA_FIRST)

            def product(j, slot, kt, hi, lo):
                for c in range(2):
                    cols = slice(c * CH, (c + 1) * CH)
                    for k in range(kt):
                        for p, (w, x) in enumerate(((w_lo, hi), (w_hi, lo), (w_hi, hi))):
                            mm = pe.matmul(Gp[slot][:, c, 0:CH], w[:, j, k, :], x[:, k, cols],
                                           start=k == 0 and p == 0, stop=k == kt - 1 and p == 2)
                return mm

            def first_pair(ready, before, n0, kt, hi, lo, base_a, base_d):
                for k in range(kt):
                    pe.wait_ge(ready, before + k + 1)
                    for j in range(2):
                        if k == 0:
                            slots_free(base_a, base_d - 1 + j)
                            pe.wait_ge(lo_ready, n0 + 1 + j)
                        for c in range(2):
                            for p, (w, x) in enumerate(((w_lo, hi), (w_hi, lo), (w_hi, hi))):
                                mm = pe.matmul(Gp[j][:, c, 0:CH], w[:, j, k, :], x[:, k, c * CH:(c + 1) * CH],
                                               start=k == 0 and p == 0, stop=k == kt - 1 and p == 2)
                        if k == kt - 1:
                            mm.then_inc(block_done, 1)

            def slots_free(base_a, base_d):
                pe.wait_ge(slot_act, base_a)
                if base_d > 0:
                    pe.wait_ge(slot_dve, base_d)

            def run(name, n0, bodies, kt, hi, lo, engine, first=None, between=None):
                base_a, base_d = runs[name]
                if first is None:
                    slots_free(base_a, base_d - 1)

                def body(i, js=range(4)):
                    for j in js:
                        pe.wait_ge(lo_ready, n0 + 4 * i + j + 1)
                        if engine == "gu" and isinstance(i, int) and j == 1:
                            pe.wait_ge(slot_dve, base_d)
                        elif engine == "gu":
                            s, base = (slot_act, base_a) if j % 2 == 0 else (slot_dve, base_d)
                            pe.wait_ge(s, base + 2 * i + j // 2)
                        elif engine == "A":
                            pe.wait_ge(slot_act, base_a + 4 * i + j - 1)
                        else:
                            pe.wait_ge(slot_dve, base_d + 4 * i + j - 1)
                        product(j, j % 2, kt, hi, lo).then_inc(block_done, 1)

                if first is not None:
                    first_pair(*first, n0, kt, hi, lo, base_a, base_d)
                    if between:
                        between()
                    body(0, range(2, 4))
                with pe.Fori(0 if first is None else 1, bodies) as i:
                    body(i)

            def forget_gates():
                pe.wait_ge(lf_dve, 1)
                for c in range(2):
                    bank = open_job(("flT", c))
                    for k in range(KD):
                        for p, (w, x) in enumerate(((wf_lo, H_hi), (wf_hi, H_lo), (wf_hi, H_hi))):
                            mm = pe.matmul(bank[:, 0:CH], w[:, k, :], x[:, k, c * CH:(c + 1) * CH],
                                           start=k == 0 and p == 0, stop=k == KD - 1 and p == 2)
                    close(mm)

            def forget_columns():
                wait_emptied(pe, ("flT", 1))
                bank = open_job("fl")
                for b in range(5):
                    c0 = 0 if b == 0 else NB + (b - 1) * P
                    mm = turn(bank[:, b * 8:(b + 1) * 8], flt[:, c0:c0 + P], HEADS)
                close(mm)

            run("in_even", N_IN_EVEN, 5, KD, H_hi, H_lo, "A", first=(h_ready, 0), between=forget_gates)
            forget_columns()

            pe.wait_ge(slot_act, runs["in_even"][0] + 20)
            pe.wait_ge(slot_act, runs["in_even"][0] + 20)
            for m in range(4 * ADA_FIRST, 4 * ADA_FIRST + 8):
                ada_block(m)
            for t in range(4):
                pe.wait_ge(cv_ready, t + 1)
                for c in range(2):
                    bank = open_job(("cm", t, c))
                    close(pe.matmul(bank[:, 0:CH], con[:, C_B64:C_B64 + P], CV[:, t, c * CH:(c + 1) * CH],
                                    start=True, stop=True))
            bank = open_job("cpo")
            for t in range(4):
                mm = turn(bank[0:CW - 1, t * P:(t + 1) * P], UP[:, t, L:L + CW - 1])
            close(mm)
            bank = open_job("cso")
            for t in range(4):
                mm = turn(bank[0:NB, t * P:(t + 1) * P], US[:, t, :, CW - 1])
            close(mm)

            def rows_of(name, src):
                bank = open_job(name)
                for t in range(4):
                    mm = turn(bank[0:NB, t * P:(t + 1) * P], src[:, t, 0:NB])
                close(mm)

            rows_of("qs", QT)
            wait_emptied(pe, "qs")
            for b in range(NB):
                bank = open_job(("qb", b))
                close(pe.matmul(bank[:, :], con[0:NB, C_ID + b:C_ID + b + 1].broadcast_to((NB, P)), qsn[:],
                                start=True, stop=True))
            ada_groups(ADA_FIRST, ADA_ATT, begun=2)
            pe.wait_ge(conv_act, 4)
            for c in range(2):
                bank = open_job(("cq", c))
                for t in range(4):
                    mm = pe.matmul(bank[0:8, 0:CH], con[:, C_GRP + 6 - 2 * t:C_GRP + 14 - 2 * t],
                                   sq4[:, t, c * CH:(c + 1) * CH], start=t == 0, stop=t == 3)
                close(mm)
            pe.wait_ge(conv_act, 5)
            for t in range(4):
                for c in range(2):
                    bank = open_job(("cb", t, c))
                    close(pe.matmul(bank[:, 0:CH], back[:, t * P:(t + 1) * P],
                                    CR[:, c * CH:(c + 1) * CH], start=True, stop=True))

            bank = open_job("cum")
            pe.wait_ge(lf_dve, 3)
            for q in range(TB):
                for b in range(q + 1):
                    mm = pe.matmul(bank[:, q * 8:(q + 1) * 8], con[:, C_TRI:C_TRI + P] if b == q else ones,
                                   lf[:, 1 + b, :], start=b == 0, stop=b == q)
            close(mm)
            wait_emptied(pe, "cum")
            bank = open_job("cumT")
            for q in range(TB):
                mm = turn(bank[0:8, q * P:(q + 1) * P], cumul[:, q, :])
            close(mm)
            for name, src in (("kn", KT), ("vn", VT)):
                for b in range(TB):
                    bank = open_job((name, b))
                    for t in range(4):
                        mm = turn(bank[:, t * P:(t + 1) * P], src[:, t, NB + b * P:NB + (b + 1) * P])
                    close(mm)
            rows_of("ks", KT)
            rows_of("vs", VT)

            def cum_rows(h):
                bank = open_job(("ckb", h))
                close(pe.matmul(bank[:, :], con[0:8, C_ID + h:C_ID + h + 1].broadcast_to((8, P)), cum8[:],
                                start=True, stop=True))

            def scores(h, q):
                bank = open_job(("s", h, q))
                rows = slice(HD * (h % 2), HD * (h % 2) + HD)
                n = (q + 1) * P
                pe.matmul(bank[:, 0:n], QT[rows, h // 2, NB + q * P:NB + (q + 1) * P],
                          KT[rows, h // 2, NB:NB + n], start=True, stop=False)
                close(pe.matmul(bank[:, n - P:n], ident, con[:, C_NEG:C_NEG + P], start=False, stop=True))

            wait_emptied(pe, "cumT")
            cum_rows(0)
            for q in range(TB):
                scores(0, q)
            for h in range(HEADS):
                if h + 1 < HEADS:
                    cum_rows(h + 1)
                for q in range(TB):
                    bank = open_job(("pt", h, q))
                    pe.wait_ge(p_ready, h * TB + q + 1)
                    for b in range(q + 1):
                        mm = turn(bank[:, b * P:(b + 1) * P], SS[:, q, b * P:(b + 1) * P])
                    close(mm)
                    if h + 1 < HEADS:
                        scores(h + 1, q)
                    x = h * TB + q
                    for m in range(ada_by(x - 1), ada_by(x)):
                        ada_block(m)
                    if ada_turned(x) is not None:
                        ada_turn(ada_turned(x))
                bank = open_job(("o", h))
                wait_emptied(pe, ("pt", h, TB - 1))
                rows = slice(HD * (h % 2), HD * (h % 2) + HD)
                for b in range(TB):
                    mm = pe.matmul(bank[rows, b * P:L], VN[:, b, h * HD:(h + 1) * HD], PTS[:, b, b * P:L],
                                   start=b == 0, stop=b == TB - 1)
                close(mm)

            ada_turn(ADA_NORM - 2)

            bank = open_job("lt")
            pe.wait_ge(lg_loaded, 16)
            for h in range(HEADS):
                mm = turn(bank[:, h * NPG:(h + 1) * NPG], lg[:].rearrange("g (t h) -> g t h", h=HEADS)[:, :, h], NPG)
            close(mm)
            for m in range(4 * ADA_NORM - 4, 4 * ADA_NORM - 2):
                ada_block(m)
            bank = open_job("cc")
            pe.wait_ge(samp_dve, 2)
            pe.matmul(bank[:, :], con[:, C_TRI:C_TRI + P], LT[:].rearrange("p h b g -> p (h b g)"),
                      start=True, stop=False)
            close(pe.matmul(bank[:, :], ones, EX[:].rearrange("p h b g -> p (h b g)"), start=False, stop=True))
            bank = open_job("cl")
            pe.matmul(bank[:, 0:64], ones, small[:, 0, :], start=True, stop=False)
            close(pe.matmul(bank[:, 0:64], ones[0:NB, :], small[0:NB, 1, :], start=False, stop=True))
            bank = open_job("sn")
            for h in range(HEADS):
                c = C_B64 + HD * (h % 2)
                mm = pe.matmul(bank[:, h * NB:(h + 1) * NB], con[:, c:c + 1].broadcast_to((P, P)),
                               small[:, 3, (h // 2) * NB:(h // 2 + 1) * NB], start=True, stop=True)
            close(mm)
            ada_block(4 * ADA_NORM - 2)
            bank = open_job("mt")
            pe.wait_ge(samp_dve, 3)
            close(turn(bank[0:64, 0:P], small[:, 5, :]))
            ada_block(4 * ADA_NORM - 1)
            bank = open_job("mb")
            pe.wait_ge(samp_dve, 4)
            close(pe.matmul(bank[:, 0:64], ones[0:64, :], small[0:64, 7, :], start=True, stop=True))
            bank = open_job("dn")
            pe.wait_ge(samp_dve, 6)
            close(pe.matmul(bank[:, 0:64], ones, small[:, 6, :], start=True, stop=True))
            pe.wait_ge(samp_dve, 7)
            turned = open_job("ov")

            def gather(b):
                pe.wait_ge(vm_ready, b + 1)
                for t in range(4):
                    mm = pe.matmul(turned[:, t * NB + b:t * NB + b + 1], vm[:, b % 2, t * P:(t + 1) * P],
                                   one_col[0:HEADS], start=True, stop=True)
                return mm

            for b in range(NB):
                if b >= 4:
                    pe.wait_ge(vm_ready, b - 3)
                elif b == 2:
                    pe.wait_ge(ada_taken, ADA_NORM)
                for g in range(8):
                    pe.wait_ge(v_page[g], 16 * (b + 1))
                    mm = pe.matmul(Gp[b // 2 % 2][0:HEADS, b % 2, :], SC[:, :, b, g], vp[:, g, :],
                                   start=g == 0, stop=g == 7)
                    mm.then_inc(v_used, 1)
                if b >= 1:
                    gather(b - 1).then_inc(vm_used, 1)
            close(gather(NB - 1))
            ada_turn(ADA_NORM - 1)

            pe.wait_ge(g_ready, 5)
            wait_emptied(pe, ("o", HEADS - 1))
            run("out_even", N_OUT_EVEN, 2, KD, G_hi, G_lo, "D")

            def ffn(layer, i):
                norm(i)
                for t, ((_, kt), (n0, n1)) in enumerate(zip(THIRDS, ffn_starts(layer))):
                    run(("gu", layer, t), n0, kt // 2, KD, H_hi, H_lo, "gu", first=(h_ready, KD * i) if t == 0 else None)
                    if t == 0:
                        norm_turns(i)
                    run(("dn", layer, t), n1, 2, kt, G_hi, G_lo, "D",
                        first=(g_ready, G_FFN[layer] + sum(x for _, x in THIRDS[:t])))

            ffn(0, 1)

            norm(2)
            def head_block(h, q):
                base_a, base_d = runs[("head", h)]
                if h == 0 and q < 2:
                    if q == 0:
                        first_pair(h_ready, KD * 2, head_start(0), KD, H_hi, H_lo, base_a, base_d)
                    return
                if q < 2:
                    slots_free(base_a, base_d - 1 + q)
                n = head_start(h) + q
                pe.wait_ge(lo_ready, n + 1)
                if q >= 2:
                    pe.wait_ge(slot_act, base_a + q - 1)
                product(n % 4, n % 2, KD, H_hi, H_lo).then_inc(block_done, 1)

            def over_features(name, h, tiles):
                for c in range(2):
                    bank = open_job((name, h, c))
                    for e in tiles:
                        mm = pe.matmul(bank[:, 0:CH], con[:, C_M512:C_M512 + 1].broadcast_to((P, P)),
                                       RSQ[:, e, c * CH:(c + 1) * CH], start=e == tiles[0], stop=e == tiles[1])
                    close(mm)

            def values_of(h, b):
                bank = open_job(("vb", h, b))
                if b == 0:
                    wait_emptied(pe, ("rvs", h))
                close(pe.matmul(bank[:, :], con[0:NB, C_ID + b:C_ID + b + 1].broadcast_to((NB, P)), vsn[:],
                                start=True, stop=True))

            def query(h, b):
                bank = open_job(("so", h, b))
                pe.wait_ge(qs_ready, h + 1)
                pe.wait_ge(st_updated, h * NB + b + 1)
                for d in range(2):
                    mm = pe.matmul(bank[0:NB, :], qz[:, d, b * NB:(b + 1) * NB], state(h, b)[:, d, :],
                                   start=d == 0, stop=d == 1)
                close(mm)

            def late_step(q):
                if q < len(LATE_BLOCKS):
                    for b in range(sum(LATE_BLOCKS[:q]), sum(LATE_BLOCKS[:q + 1])):
                        pe.wait_ge(spare_loaded[b], 16 * 3)
                        if b == 0:
                            pe.wait_ge(slot_act, runs[("head", RH - 1)][0] + HEAD_BLOCKS)
                        for k in range(KD):
                            mm = pe.matmul(Gp[b // 4][0:9, 0, b % 4 * P:(b % 4 + 1) * P], cT[:, k, :], late[:, b, k, :],
                                           start=k == 0, stop=k == KD - 1)
                        mm.then_inc(late_used, 1)
                if q in LATE_TURNS:
                    ada_turn(LATE_TURNS[q])

            for h in range(RH + 1):
                for q in range(HEAD_BLOCKS):
                    if state_at(h, q) is not None:
                        values_of(h - 1, state_at(h, q))
                    if h < RH:
                        head_block(h, q)
                    if query_at(h, q) is not None:
                        query(h - 1, query_at(h, q))
                    if h > 0 and q == 0:
                        pe.wait_ge(pair_pool, 2 * h - 1)
                        pe.wait_ge(pair_dve, 2 * h - 1)
                        over_features("rm", h - 1, (0, 1))
                    elif h > 0 and q == 1:
                        pe.wait_ge(pair_pool, 2 * h)
                        pe.wait_ge(pair_dve, 2 * h)
                        over_features("rv", h - 1, (0, 2))
                    if h == RH:
                        late_step(q)
                if h == 0:
                    norm_turns(2)
                if h < RH:
                    pe.wait_ge(slot_act, runs[("head", h)][0] + HEAD_BLOCKS)
                    for b in range(TB):
                        bank = open_job(("rvn", h, b))
                        for e in range(4):
                            mm = turn(bank[:, e * P:(e + 1) * P], RVT[:, e, NB + b * P:NB + (b + 1) * P])
                        close(mm)
                    rows_of(("rvs", h), RVT)
                    pe.wait_ge(rope_ready, 4 * h + 4)
                    for b in range(TB):
                        bank = open_job(("rkn", h, b))
                        for d in range(2):
                            mm = turn(bank[:, d * P:(d + 1) * P], QKR[:, 2 + d, NB + b * P:NB + (b + 1) * P])
                        close(mm)
                if h < RH:
                    for j in range(TB):
                        bank = open_job(("ra", h, j))
                        for d in range(2):
                            mm = pe.matmul(bank[:, 0:L - j * P], QKR[:, 2 + d, NB + j * P:NB + (j + 1) * P],
                                           QKR[:, d, NB + j * P:T], start=d == 0, stop=d == 1)
                        close(mm)
                    wait_emptied(pe, ("rkn", h, TB - 1))
                    for d in range(2):
                        bank = open_job(("rst", h, d))
                        for b in range(TB):
                            mm = pe.matmul(bank[:, :], KDN[:, b, d * P:(d + 1) * P], RVN[:, b, :],
                                           start=b == 0, stop=b == TB - 1)
                        close(mm)
                if h > 0:
                    bank = open_job(("sot", h - 1))
                    pe.wait_ge(osum_ready, 2 * h)
                    for e in range(4):
                        mm = turn(bank[:, e * NB:(e + 1) * NB], osum[:, e * P:(e + 1) * P], NB)
                    close(mm)
                if h < RH:
                    wait_emptied(pe, ("ra", h, TB - 1))
                    for e in range(4):
                        if h == RH - 1 and e < 2:
                            values_of(h, e)
                        bank = open_job(("ro", h, e))
                        for j in range(TB):
                            mm = pe.matmul(bank[:, j * P:L], RVN[:, j, e * P:(e + 1) * P], AD[:, j, 0:L - j * P],
                                           start=j == 0, stop=j == TB - 1)
                        close(mm)
                        if h == RH - 1 and e < 2:
                            query(h, e)
                if h in (2, RH):
                    pair = 0 if h == 2 else 1
                    pe.wait_ge(g_ready, 27 + 10 * (pair + 1))
                    run(("out", pair), out_start(pair), 2, KD, G_hi, G_lo, "D")
            ffn(1, 3)

            norm(4)
            for f in range(2):
                pe.wait_ge(y_ready, 4 * f + 4)
                for b in range(TB):
                    bank = open_job(("y", b, f))
                    for k in range(4):
                        mm = turn(bank[:, k * P:(k + 1) * P], YT[:, 4 * f + k, NB + b * P:NB + (b + 1) * P])
                    close(mm)
                bank = open_job(("ys", f))
                for k in range(4):
                    mm = turn(bank[0:NB, k * P:(k + 1) * P], YT[:, 4 * f + k, 0:NB])
                close(mm)

        @block.scalar
        def _(act):
            n = Tally(act)

            def f(out, in_, func, **kw):
                return nc.scalar.activation(out, in_, func, **kw)

            rows = [(rows_v[V_MIXG:V_MIXG + 16], A["norm_mix_g"].rearrange("l (k p) -> (l k) p", p=P)),
                    (rows_v[V_FFNG:V_FFNG + 16], A["norm_ffn_g"].rearrange("l (k p) -> (l k) p", p=P)),
                    (rows_v[V_FING:V_FING + 8], A["final_norm_g"].rearrange("(k p) -> k p", p=P)),
                    (rows_v[V_CB:V_CB + 4], A["conv_b"][0].rearrange("(k p) -> k p", p=P)),
                    (rows_v[V_CG:V_CG + 4], A["conv_norm_g"][0].rearrange("(k p) -> k p", p=P)),
                    (rows_v[V_CNB:V_CNB + 4], A["conv_norm_b"][0].rearrange("(k p) -> k p", p=P)),
                    (rows_v[V_RG:V_RG + 16], A["ret_norm_g"][0].rearrange("(k p) -> k p", p=P)),
                    (rows_a[:], A["ada_b"].rearrange("l (k p) -> (l k) p", p=P)),
                    (rows_c[:], A["conv_w"][0].rearrange("w (k p) -> (w k) p", p=P)),
                    (rows_s[:, 0, :], A["state_conv"][0, 0:4].rearrange("b w c -> (b w) c")),
                    (rows_s[:, 1, :], A["state_conv"][0, 4:8].rearrange("b w c -> (b w) c")),
                    (wf[:], A["w_in_even"][0][:, 1536:1536 + P].rearrange("(k p) m -> p k m", p=P)),
                    (bfg[:], A["b_forget"].broadcast_to((P, HEADS)))]
            assert len(rows) == N_ROW_LOADS
            for dst, src in rows:
                act.dma_start(dst, src).then_inc(rows_loaded, 16)
            store(act, A["conv_sample"][0, :, 0:CW - 2, :], A["state_conv"][0, :, 1:CW - 1, :])
            act.wait_ge(x_loaded, 64)
            n.up(f(cn_silu[:], cn[:], ACT.Silu), c_silu)

            def squares(i):
                for k in range(KD):
                    if i == 0:
                        wait_emptied(act, "xs")
                    else:
                        act.wait_ge(x_ready, X_BEFORE[i] + k + 1)
                    if k >= 2:
                        act.wait_ge(sq_used, (KD - 2) * i + max(1, k - 2))
                    elif i > 0:
                        wait_emptied(act, ("ss", i - 1, 1))
                    n.up(f(sq[:, k % 2, :], X[:, k, :], ACT.Square), sq_ready)
                act.wait_ge(var_ready, i + 1)
                n.up(f(rstd[:], rstd[:], ACT.Sqrt), rstd_ready)

            def modulate(i):
                shift = mod_at(L_OF[i], 0 if i % 2 == 0 else 3)
                for k in range(KD):
                    act.wait_ge(scaled_ready, KD * i + k + 1)
                    n.up(f(H_hi[:, k, NB:T], scaled[:, k % 2, NB:T], ACT.Identity,
                           bias=mod[:, shift + k, 0:1]), hh_ready)

            def split_hi(j, m, kt):
                act.wait_ge(raw_loaded[j], raw_count(m) if isinstance(m, int) else m[0])
                if not isinstance(m, int):
                    act.wait_ge(block_done, m[1])
                elif m >= 4:
                    act.wait_ge(block_done, m - 3)
                f(w_hi[:, j, 0:kt, :], raw[:, j, 0:kt, :], ACT.Copy).then_inc(hi_ready, 1)

            def ahead(m):
                if m < N_BLOCKS:
                    split_hi(m % 4, m, k_tiles(m))

            def product_done(m):
                act.wait_ge(block_done, m + 1)

            def slot(j):
                return Gp[j % 2][:, :, 0:CH]

            def halves(ap):
                return ap.rearrange("p (c n) -> p c n", c=2)

            def take_rows(g):
                act.wait_ge(ada_used, 4 * g + 4)
                if g >= 2:
                    wait_job(act, ("ada", g - 2))
                n.up(f(ada_rows(g), Gp[g % 2][0:9, 0, :], ACT.Copy), ada_taken)

            def take_norm_rows(i):
                for g in ada_norm_groups(i):
                    wait_job(act, ("adr", g))
                    n.up(f(ada_rows(g), Jp[jobs.bank(("adr", g))][0:9, :], ACT.Copy), emptied["A"])

            squares(0)
            act.wait_ge(rows_loaded, 16 * N_ROW_LOADS)
            n.up(f(wf_hi[:], wf[:], ACT.Copy), lf_act)
            for g in range(ADA_FIRST):
                take_rows(g)
            for i in range(2):
                n.up(f(small[:, i, 0:1], one_col, ACT.Copy), slot_act)
            ahead(0)
            ahead(1)
            modulate(0)
            for m in range(20):
                if m + 2 < N_OUT_EVEN:
                    ahead(m + 2)
                product_done(m)
                kind, j = m // 4, m % 4
                if kind == 1:
                    if j >= 2:
                        act.wait_ge(u_ready, j - 1)
                    n.up(f(halves(gate[:, j % 2, :]), slot(m), ACT.Sigmoid), slot_act)
                else:
                    if kind == 4:
                        act.wait_ge(u_ready, 4)
                    n.up(f(halves((AT, None, QT, KT, VT)[kind][:, j, :]), slot(m), ACT.Copy), slot_act)
                if m == 1:
                    for c in range(2):
                        wait_job(act, ("flT", c))
                        n.up(f(flt[:, c * CH:(c + 1) * CH], Jp[jobs.bank(("flT", c))][0:HEADS, 0:CH], ACT.Copy),
                             emptied["A"])

            stage = [0, 0]
            turn_ = [0]

            def stage_out(name, part, width, dst):
                s = turn_[0] % 2
                turn_[0] += 1
                wait_job(act, name)
                if stage[s]:
                    act.wait_ge(stage_stored[s], 16 * stage[s])
                bank = Jp[jobs.bank(name)]
                n.up(f(kn_out[0:part, s, 0:width], bank[0:part, 0:width], ACT.Copy), emptied["A"])
                n.own(emptied["A"])
                store(act, dst, kn_out[0:part, s, 0:width], stage_stored[s])
                stage[s] += 1

            act.wait_ge(cv_ready, 4)
            stage_out("cpo", CW - 1, 512, A["conv_prompt"][0, 0])
            stage_out("cso", NB, 512, A["conv_sample"][0, :, CW - 2, :])
            wait_job(act, "qs")
            n.up(f(qsn[:], Jp[jobs.bank("qs")][0:NB, :], ACT.Copy), emptied["A"])
            for b in range(NB):
                wait_job(act, ("qb", b))
                n.up(f(QB[:, b, :], Jp[jobs.bank(("qb", b))][:, :], ACT.Copy, scale=FOX_SCALE), emptied["A"])
            for t in range(4):
                wait_emptied(act, ("cm", t, 1))
                n.up(f(sq4[:, t, :], CV[:, t, :], ACT.Square), conv_act)
            for g in range(ADA_FIRST, ADA_ATT):
                take_rows(g)
            act.wait_ge(lf_dve, 2)
            n.up(f(lf[:], lf[:], ACT.Exp), lf_act)
            n.own(lf_act)
            n.up(f(lf[:], lf[:], ACT.Ln, bias=one_col), lf_act)
            act.wait_ge(lf_dve, 3)
            store(act, A["logf_prompt"][0, 0].rearrange("(b p) h -> p b h", p=P), lf[:, 1:5, :])
            store(act, A["logf_sample"][0, :, 0, :], lf[0:NB, 0, :])
            act.wait_ge(conv_var, 1)
            n.up(f(CR[:], CR[:], ACT.Sqrt), conv_act)
            for t in range(4):
                wait_emptied(act, ("cb", t, 1))
                if t >= 2:
                    act.wait_ge(g_ready, t - 1)
                n.up(f(full[:, t % 2, :], CV[:, t, :], ACT.Silu, bias=vec[:, V_CNB + t:V_CNB + t + 1],
                       scale=vec[:, V_CG + t:V_CG + t + 1]), full_ready)
                n.own(full_ready)
                n.up(f(G_hi[:, 4 + t, :], full[:, t % 2, :], ACT.Copy), ghi_ready)
            wait_job(act, "cumT")
            n.up(f(cum8[:], Jp[jobs.bank("cumT")][0:8, :], ACT.Copy), emptied["A"])
            for b in range(TB):
                stage_out(("kn", b), P, 512, A["k_prompt"][0, 0, b * P:(b + 1) * P].rearrange("p h d -> p (h d)"))
            for b in range(TB):
                wait_job(act, ("vn", b))
                n.up(f(VN[:, b, :], Jp[jobs.bank(("vn", b))][:, :], ACT.Copy), emptied["A"])
                n.own(emptied["A"])
                store(act, A["v_prompt"][0, 0, b * P:(b + 1) * P].rearrange("p h d -> p (h d)"), VN[:, b, :], v_stored)
            stage_out("ks", NB, 512, A["k_sample"][0, :, 0].rearrange("p h d -> p (h d)"))
            stage_out("vs", NB, 512, A["v_sample"][0, :, 0].rearrange("p h d -> p (h d)"))

            def row_of_sums(h):
                wait_job(act, ("ckb", h))
                if h >= 2:
                    wait_emptied(act, ("s", h - 2, TB - 1))
                n.up(f(ckb[:, h % 2, :], Jp[jobs.bank(("ckb", h))][:, :], ACT.Copy), emptied["A"])

            def exps(h, q):
                x = h * TB + q
                act.wait_ge(max_ready, x + 1)
                w = SS[:, q, 0:(q + 1) * P]
                n.up(f(w, w, ACT.Exp, bias=nm[:, x:x + 1], accum_out=rs[:, x:x + 1]), exp_ready)

            def load_ada(m):
                act.wait_ge(ada_used, m - 3)
                layer, c0 = m // 48, m % 48 * P
                act.dma_start(raw[:, m % 4, :, :], A["ada_w"][layer][:, c0:c0 + P].rearrange("(k p) m -> p k m", p=P)
                              ).then_inc(raw_loaded[m % 4], 16)

            row_of_sums(0)
            for q in range(TB):
                exps(0, q)
            for h in range(HEADS):
                if h + 1 < HEADS:
                    row_of_sums(h + 1)
                if h >= 1:
                    wait_job(act, ("o", h - 1))
                for q in range(TB):
                    wait_job(act, ("pt", h, q))
                    n.up(f(PTS[:, 0:q + 1, q * P:(q + 1) * P],
                           Jp[jobs.bank(("pt", h, q))][:, 0:(q + 1) * P].rearrange("p (b c) -> p b c", c=P),
                           ACT.Copy), emptied["A"])
                    if h + 1 < HEADS:
                        exps(h + 1, q)
                    x = h * TB + q
                    if ada_rows_at(x) is not None:
                        take_rows(ada_rows_at(x))
                    for m in range(ada_by(x - 2) + 4 if x else ada_by(-1) + 4, min(ada_by(x - 1) + 4, 4 * ADA_NORM)):
                        load_ada(m)
                wait_job(act, ("o", h))
                rows_ = slice(HD * (h % 2), HD * (h % 2) + HD)
                n.up(f(G_hi[rows_, h // 2, NB:T], Jp[jobs.bank(("o", h))][rows_, :], ACT.Copy), ohi_ready)

            for m in range(ada_by(HEADS * TB - 2) + 4, 4 * ADA_NORM):
                load_ada(m)
            wait_job(act, "lt")
            n.up(f(LT[:].rearrange("p h b g -> p (h b g)"), Jp[jobs.bank("lt")][:, :], ACT.Copy), emptied["A"])
            wait_job(act, "cl")
            n.up(f(small[:, 2, :], Jp[jobs.bank("cl")][:, 0:64], ACT.Copy), emptied["A"])
            act.wait_ge(samp_dve, 5)
            n.up(f(small[:, 4, :], small[:, 4, :], ACT.Exp), samp_act)
            n.up(f(SC[:], SC[:], ACT.Exp), samp_act)

            def gates(layer):
                for t, ((_, kt), (n0, n1)) in enumerate(zip(THIRDS, ffn_starts(layer))):
                    base_a, base_d = runs[("gu", layer, t)]
                    g0 = G_FFN[layer] + sum(x for _, x in THIRDS[:t])

                    def body(i, n0=n0, base_d=base_d, g0=g0):
                        for j in range(4):
                            m = n0 + 4 * i + j + 2
                            jj = (j + 2) % 4
                            if isinstance(i, int):
                                ahead(m)
                            else:
                                split_hi(jj, (16 * (n0 // 4 + ADA_NORM + 1 + (j + 2) // 4) + 16 * i, m - 3), KD)
                            if j % 2 == 0:
                                act.wait_ge(block_done, n0 + 4 * i + j + 1)
                                act.wait_ge(slot_dve, base_d + 2 * i + j // 2 - 1)
                                f(halves(gate[:, j // 2, :]), slot(0), ACT.Silu).then_inc(slot_act, 1)
                            else:
                                act.wait_ge(slot_dve, base_d + 2 * i + j // 2 + 1)
                                f(G_hi[:, ds(2 * i + j // 2, 1), :].rearrange("p o n -> p (o n)"),
                                  full[:, j // 2, :], ACT.Copy).then_inc(ghi_ready, 1)

                    with act.Fori(0, kt // 2 - 1) as i:
                        body(i)
                    body(kt // 2 - 1)
                    for q in range(KD):
                        ahead(n1 + q + 2)

            take_rows(ADA_NORM - 1)
            act.wait_ge(pages_loaded, 32)
            act.wait_ge(v_stored, 16 * TB)
            value_pages(act, 1)
            ahead(N_OUT_EVEN)
            ahead(N_OUT_EVEN + 1)
            for q in range(KD):
                ahead(N_OUT_EVEN + q + 2)
            squares(1)
            modulate(1)
            take_norm_rows(1)
            gates(0)
            squares(2)
            modulate(2)
            take_norm_rows(2)

            sto = [0, 0]
            def tail(h, q):
                if q == 0:
                    wait_emptied(act, ("rm", h, 1))
                    for e in range(4):
                        n.up(f(RSQ[:, e, :], RVT[:, e, :], ACT.Square), ret_act)
                elif q == 3:
                    for e in range(4):
                        act.wait_ge(ret_gated, 4 * h + e + 1)
                        n.up(f(G_hi[:, 4 * (h % 2) + e, :], GS[:, e, :], ACT.Copy), ghi_ready)

            def root_rows(h):
                act.wait_ge(osum_ready, 2 * h + 1)
                n.up(f(stat[:, 1:2], stat[:, 1:2], ACT.Sqrt), osum_root)

            def decay_state(h, b):
                act.wait_ge(st_loaded[st_slot(h, b)], 16 * st_load(h, b))
                n.up(f(state(h, b), state(h, b), ACT.Copy, scale=GAMMA[h]), st_scaled)

            for h in range(RH + 1):
                for q in range(HEAD_BLOCKS):
                    if h < RH:
                        m = head_start(h) + q
                        ahead(m + 2)
                    if h > 0 and q == 2:
                        act.wait_ge(ret_dve, h)
                        n.up(f(rsd[:], rsd[:], ACT.Sqrt), ret_act)
                    if state_at(h, q) is not None:
                        decay_state(h - 1, state_at(h, q))
                    if h < RH:
                        product_done(m)
                        src = slot(m)
                        if q == 8 and h > 0:
                            act.wait_ge(g_ready, 27 + 5 * (h - 1) + 4)
                        if q < 2:
                            o = f(halves(QK[:, q, :]), src, ACT.Copy)
                        elif q < 4:
                            o = f(halves(QK[:, q, :]), src, ACT.Copy, scale=DK ** -0.5)
                        elif q < 8:
                            o = f(halves(RVT[:, q - 4, :]), src, ACT.Copy)
                        else:
                            o = f(halves(GS[:, q - 8, :]), src, ACT.Silu)
                        n.up(o, slot_act)
                    if h > 0:
                        tail(h - 1, q)
                    if h == RH and q in (2, 6):
                        g = ADA_LATE + q // 4
                        act.wait_ge(late_used, 4 * (q // 4) + 4)
                        if q == 2:
                            wait_emptied(act, ("ra", RH - 1, TB - 1))
                        else:
                            wait_job(act, ("ada", g - 1))
                        n.up(f(ada_rows(g), Gp[q // 4][0:9, 0, :], ACT.Copy), late_taken)
                if h == RH:
                    root_rows(h - 1)
                if h == RH:
                    for q in range(KD):
                        ahead(out_start(1) + q + 2)
                    break
                for b in range(TB):
                    wait_job(act, ("rvn", h, b))
                    n.up(f(RVN[:, b, :], Jp[jobs.bank(("rvn", h, b))][:, :], ACT.Copy), emptied["A"])
                wait_job(act, ("rvs", h))
                n.up(f(vsn[:], Jp[jobs.bank(("rvs", h))][0:NB, :], ACT.Copy), emptied["A"])
                for b in range(TB):
                    wait_job(act, ("rkn", h, b))
                    c0 = C_KDEC + b * RH + h
                    n.up(f(KDN[:, b, :], Jp[jobs.bank(("rkn", h, b))][:, 0:DK], ACT.Copy,
                           scale=con[:, c0:c0 + 1]), emptied["A"])
                if h > 0:
                    root_rows(h - 1)
                for d in range(2):
                    wait_job(act, ("rst", h, d))
                    if sto[d]:
                        act.wait_ge(stage_stored[d], 16 * (stage[d] + sto[d]))
                    n.up(f(so[:, d, :], Jp[jobs.bank(("rst", h, d))][:, :], ACT.Copy), emptied["A"])
                    n.own(emptied["A"])
                    store(act, A["ret_prompt"][0, 0, h, d * P:(d + 1) * P, :], so[:, d, :], stage_stored[d])
                    sto[d] += 1
                for e in range(4):
                    if h == RH - 1 and e < 2:
                        decay_state(h, e)
                    wait_job(act, ("ro", h, e))
                    n.up(f(RVT[:, e, NB:T], Jp[jobs.bank(("ro", h, e))][:, :], ACT.Copy), emptied["A"])
                if h == 2:
                    for q in range(KD):
                        ahead(out_start(0) + q + 2)
            spare_states_left(act)
            squares(3)
            modulate(3)
            gates(1)
            squares(4)
            for f in range(2):
                for b in range(TB + 1):
                    name = ("y", b, f) if b < TB else ("ys", f)
                    if jobs.emptied(name)[0] == "A":
                        part = P if b < TB else NB
                        wait_job(act, name)
                        n.up(nc.scalar.activation(yo[0:part, 5 * f + b, :], Jp[jobs.bank(name)][0:part, :], ACT.Copy),
                             emptied["A"])

        @block.vector
        def _(dve):
            n = Tally(dve)
            v = nc.vector

            def step(instruction):
                n.up(instruction, dve_step)
                n.own(dve_step)

            def bank_of(name):
                wait_job(dve, name)
                return Jp[jobs.bank(name)]

            def lo(m, j=None, kt=KD):
                if isinstance(m, int):
                    if m >= N_BLOCKS:
                        return
                    j, kt = m % 4, k_tiles(m)
                dve.wait_ge(hi_ready, m + 1)
                v.tensor_tensor(w_lo[:, j, 0:kt, :], raw[:, j, 0:kt, :], w_hi[:, j, 0:kt, :].bitcast(f32),
                                ALU.subtract).then_inc(lo_ready, 1)

            def minus_hi(out, whole, hi):
                return v.tensor_tensor(out, whole, hi.bitcast(f32), ALU.subtract)

            for i in range(2):
                n.up(v.memset(full_s[:, i, 0:1], 0.0), slot_dve)
            for k in range(KD):
                n.up(v.tensor_copy(X[:, k, NB:T], bank_of(("xT", k))[:, :]), emptied["D"])
            bank = bank_of("xs")
            n.up(v.tensor_copy(X[:, :, 0:NB], bank[:, 0:KD * NB].rearrange("p (k b) -> p k b", b=NB)), emptied["D"])
            n.up(v.tensor_copy(cT[:].rearrange("p k b -> p (k b)"), bank_of("cT")[:, 0:KD * 9]), emptied["D"])
            n.up(v.tensor_copy(vec[:], bank_of("vec")[:, 0:V_END]), emptied["D"])
            for g in range(2):
                bank = bank_of(("sc", g))
                for t in range(4):
                    o = v.tensor_copy(US[:, t, 4 * g:4 * g + 4, 0:CW - 1],
                                      bank[:, t * 120:(t + 1) * 120].rearrange("p (b w) -> p b w", b=4))
                n.up(o, emptied["D"])

            def rstd_parts(i):
                for c in range(2):
                    n.up(v.tensor_scalar(rstd[:, c * CH:(c + 1) * CH], bank_of(("ss", i, c))[:, 0:CH],
                                         EPS, None, ALU.add), emptied["D"])
                n.own(emptied["D"])
                n.up(v.reciprocal(rstd[:], rstd[:]), var_ready)

            def modulate(i):
                layer, second = L_OF[i], i % 2
                shift, scale = mod_at(layer, 3 * second), mod_at(layer, 3 * second + 1)
                g = (V_FFNG if second else V_MIXG) + layer * KD
                step(v.scalar_tensor_tensor(coef[:], mod[:, scale:scale + KD, :], 1.0,
                                            vec[:, g:g + KD].unsqueeze(2).broadcast_to((P, KD, 9)),
                                            ALU.add, ALU.mult))
                step(v.tensor_tensor(full_s[:], X[:, :, 0:NB], coef[:, :, 1:9], ALU.mult))
                if i == 1:
                    dve.wait_ge(v_stored, 16 * TB)
                dve.wait_ge(rstd_ready, i + 1)

                def scale(k):
                    if k >= 2:
                        dve.wait_ge(hh_ready, KD * i + k - 1)
                        n.own(h_ready)
                    n.up(v.scalar_tensor_tensor(scaled[:, k % 2, NB:T], X[:, k, NB:T], coef[:, k, 0:1],
                                                rstd[:, NB:T], ALU.mult, ALU.mult), scaled_ready)

                scale(0)
                scale(1)
                if i == 0:
                    lo(0)
                    lo(1)
                step(v.tensor_tensor(full_s[:], full_s[:],
                                     rstd[:, 0:NB].unsqueeze(1).broadcast_to((P, KD, NB)), ALU.mult))
                step(v.tensor_tensor(full_s[:], full_s[:], mod[:, shift:shift + KD, 1:9], ALU.add))
                step(v.tensor_copy(H_hi[:, :, 0:NB], full_s[:]))
                minus_hi(H_lo[:, :, 0:NB], full_s[:], H_hi[:, :, 0:NB])
                for k in range(KD):
                    dve.wait_ge(hh_ready, KD * i + k + 1)
                    n.own(scaled_ready, back=1 if k < KD - 1 else 0)
                    n.up(v.scalar_tensor_tensor(H_lo[:, k, NB:T], scaled[:, k % 2, NB:T],
                                                mod[:, shift + k, 0:1], H_hi[:, k, NB:T].bitcast(f32),
                                                ALU.add, ALU.subtract), h_ready)
                    if k + 2 < KD:
                        scale(k + 2)

            def update(m, n_block, part):
                g = part + m
                dve.wait_ge(block_done, n_block + 1)
                src = Gp[n_block % 2]
                if m >= 2:
                    n.own(x_ready, back=1)
                n.up(v.tensor_tensor(upd_s[:, m % 2, :], src[:, 0, 0:NB], mod[:, g, 1:9], ALU.mult), dve_step)
                v.scalar_tensor_tensor(X[:, m, NB:CH], src[:, 0, NB:CH], mod[:, g, 0:1], X[:, m, NB:CH],
                                       ALU.mult, ALU.add)
                n.up(v.scalar_tensor_tensor(X[:, m, CH:T], src[:, 1, 0:CH], mod[:, g, 0:1], X[:, m, CH:T],
                                            ALU.mult, ALU.add), slot_dve)
                n.own(dve_step)
                n.up(v.tensor_tensor(X[:, m, 0:NB], X[:, m, 0:NB], upd_s[:, m % 2, :], ALU.add), x_ready)

            rstd_parts(0)
            def ada_mod(g):
                n.up(v.tensor_tensor(mod[:, 4 * g:4 * g + 4, :],
                                     bank_of(("ada", g))[:, 0:36].rearrange("p (m c) -> p m c", c=9),
                                     vec[:, V_ADAB + 4 * g:V_ADAB + 4 * g + 4].unsqueeze(2).broadcast_to((P, 4, 9)),
                                     ALU.add), emptied["D"])

            dve.wait_ge(lf_act, 1)
            n.up(minus_hi(wf_lo[:], wf[:], wf_hi[:]), lf_dve)
            for g in range(ADA_FIRST):
                ada_mod(g)
            n.own(emptied["D"])
            modulate(0)

            def log_forget():
                n.up(v.tensor_tensor(lf_a[:], bank_of("fl")[:, 0:40].rearrange("p (b h) -> p b h", h=8),
                                     bfg[:].unsqueeze(1).broadcast_to((P, 5, HEADS)), ALU.add), emptied["D"])
                n.own(emptied["D"])
                step(v.tensor_scalar(lf_b[:], lf_a[:], 0.0, None, ALU.min))
                n.up(v.scalar_tensor_tensor(lf[:], lf_a[:], -1.0, lf_a[:], ALU.mult, ALU.min), lf_dve)

            def tap(t, w):
                cw = vec[:, V_CW + w * 4 + t:V_CW + w * 4 + t + 1]
                n.own(conv_step, back=2)
                if w == 0:
                    o = v.tensor_scalar(CV[:, t, NB:T], UP[:, t, 0:L], cw, vec[:, V_CB + t:V_CB + t + 1],
                                        ALU.mult, ALU.add)
                else:
                    o = v.scalar_tensor_tensor(CV[:, t, NB:T], UP[:, t, w:w + L], cw, CV[:, t, NB:T],
                                               ALU.mult, ALU.add)
                n.up(o, conv_step)

            taps = [(t, w) for w in range(CW) for t in range(3)]
            n.count[conv_step.name] = 0
            for m in range(20):
                if m + 2 < N_OUT_EVEN:
                    lo(m + 2)
                if 4 <= m < 8:
                    t = m - 4
                    dve.wait_ge(slot_act, runs["in_even"][0] + m + 1)
                    v.tensor_tensor(UP[:, t, CW - 1:], AT[:, t, NB:T], gate[:, t % 2, NB:T], ALU.mult)
                    n.up(v.tensor_tensor(US[:, t, :, CW - 1], AT[:, t, 0:NB], gate[:, t % 2, 0:NB], ALU.mult), u_ready)
                    if m == 7:
                        dve.wait_ge(pad_ready, 1)
                        n.own(u_ready)
                if m >= 8:
                    for t, w in taps[(m - 8) * len(taps) // 12:(m - 7) * len(taps) // 12]:
                        tap(t, w)
            for t in range(4):
                step(v.tensor_tensor(usw[:], US[:, t, :, 0:CW],
                                     vec[:, V_CW + t:V_END:4].unsqueeze(1).broadcast_to((P, NB, CW)), ALU.mult))
                step(v.tensor_reduce(CV[:, t, 0:NB], usw[:], AX.X, ALU.add))
                n.own(conv_step)
                if t == 3:
                    dve.wait_ge(conv_pool, CW)
                n.up(v.tensor_scalar(CV[:, t, 0:NB], CV[:, t, 0:NB], vec[:, V_CB + t:V_CB + t + 1], None, ALU.add),
                     cv_ready)
            v.tensor_copy(back[:].rearrange("p (g d) -> p g d", d=HD),
                          con[0:8, C_ID:C_ID + 8].unsqueeze(2).broadcast_to((8, 8, HD)))
            log_forget()
            for t in range(4):
                for c in range(2):
                    cols = slice(c * CH, (c + 1) * CH)
                    n.own(cv_ready)
                    n.up(v.tensor_tensor(CV[:, t, cols], CV[:, t, cols], bank_of(("cm", t, c))[:, 0:CH], ALU.subtract),
                         emptied["D"])
            for g in range(ADA_FIRST, ADA_ATT):
                ada_mod(g)
            dve.wait_ge(lf_act, 3)
            n.up(v.tensor_tensor(lf[:], lf_b[:], lf[:], ALU.subtract), lf_dve)
            for c in range(2):
                n.up(v.tensor_scalar(CR[:, c * CH:(c + 1) * CH], bank_of(("cq", c))[0:8, 0:CH], EPS, None, ALU.add),
                     emptied["D"])
            n.own(emptied["D"])
            n.up(v.reciprocal(CR[:], CR[:]), conv_var)
            for t in range(4):
                for c in range(2):
                    cols = slice(c * CH, (c + 1) * CH)
                    n.up(v.tensor_tensor(CV[:, t, cols], CV[:, t, cols], bank_of(("cb", t, c))[:, 0:CH], ALU.mult),
                         emptied["D"])
            for t in range(4):
                dve.wait_ge(ghi_ready, t + 1)
                n.up(minus_hi(G_lo[:, 4 + t, :], full[:, t % 2, :], G_hi[:, 4 + t, :]), g_ready)
            n.up(v.tensor_copy(cumul[:].rearrange("p b h -> p (b h)"), bank_of("cum")[:, 0:32]), emptied["D"])
            wait_emptied(dve, "vs")
            n.up(v.tensor_copy(vts[:], VT[:, :, 0:NB]), samp_dve)

            def weigh(h, q):
                x, w = h * TB + q, (q + 1) * P
                if q == 0:
                    wait_emptied(dve, ("ckb", h))
                n.up(v.scalar_tensor_tensor(SS[:, q, 0:w], bank_of(("s", h, q))[:, 0:w], FOX_SCALE,
                                            ckb[:, h % 2, 0:w], ALU.mult, ALU.subtract), emptied["D"])
                n.own(emptied["D"])
                n.up(v.tensor_reduce(nm[:, x:x + 1], SS[:, q, 0:w], AX.X, ALU.max, negate=True), max_ready)

            def inverse(x):
                dve.wait_ge(exp_ready, x + 1)
                n.up(v.reciprocal(ri[:, x:x + 1], rs[:, x:x + 1]), ri_ready)

            def dots(x):
                for g in range(2 * x, 2 * x + 2):
                    dve.wait_ge(prod_ready, g + 1)
                    n.up(v.tensor_reduce(SC[:, :, g // 8, g % 8], prod[:, g % 2, :].rearrange("p (h d) -> p h d", d=HD),
                                         AX.X, ALU.add), page_dot)

            for q in range(TB):
                weigh(0, q)
            inverse(0)
            for h in range(HEADS):
                for q in range(TB):
                    x = h * TB + q
                    if x + 1 < HEADS * TB:
                        inverse(x + 1)
                    if h + 1 < HEADS:
                        weigh(h + 1, q)
                    if ada_turned(x) is not None:
                        ada_mod(ada_turned(x))
                    dots(x)
                rows_ = slice(HD * (h % 2), HD * (h % 2) + HD)
                dve.wait_ge(ohi_ready, h + 1)
                n.up(minus_hi(G_lo[rows_, h // 2, NB:T], bank_of(("o", h))[rows_, :], G_hi[rows_, h // 2, NB:T]),
                     emptied["D"])

            ada_mod(ADA_NORM - 2)
            wait_emptied(dve, "lt")
            step(v.memset(EX[:, :, :, 0], 0.0))
            for g in range(1, 8):
                step(v.tensor_tensor(EX[:, :, :, g], EX[:, :, :, g - 1], LT[:, :, :, g - 1], ALU.add))

            def hb(ap):
                return ap.rearrange("p (h b) -> p h b", b=NB)

            v.tensor_tensor(hb(small[:, 0, :]), EX[:, :, :, 7], LT[:, :, :, 7], ALU.add)
            v.tensor_tensor(hb(small[0:NB, 1, :]), con[0:NB, C_ID:C_ID + NB].unsqueeze(1).broadcast_to((NB, HEADS, NB)),
                            lf[0:NB, 0, :].unsqueeze(2).broadcast_to((NB, HEADS, NB)), ALU.mult)
            n.up(v.tensor_tensor(small[:, 3, 0:32].rearrange("p (t b) -> p t b", b=NB), QT[:, :, 0:NB], KT[:, :, 0:NB],
                                 ALU.mult), samp_dve)
            n.own(page_dot)
            sc = SC[:].rearrange("p h b g -> p (h b g)")
            n.up(v.tensor_tensor(sc, sc, bank_of("cc")[:, :], ALU.subtract), emptied["D"])
            wait_emptied(dve, "cl")
            n.up(v.scalar_tensor_tensor(small[:, 4, :], bank_of("sn")[:, 0:64], FOX_SCALE * HD, small[:, 2, :], ALU.mult,
                                        ALU.subtract), emptied["D"])
            n.own(emptied["D"])
            n.up(v.tensor_reduce(hb(small[:, 5, :]), SC[:], AX.X, ALU.max), samp_dve)
            n.up(v.tensor_reduce(small[0:64, 6, 0:1], bank_of("mt")[0:64, 0:P], AX.X, ALU.max), emptied["D"])
            n.own(emptied["D"])
            n.up(v.tensor_scalar(small[0:64, 7, :], ident[0:64, 0:64], small[0:64, 6, 0:1], None, ALU.mult), samp_dve)
            n.up(v.tensor_tensor(small[:, 5, :], bank_of("mb")[:, 0:64], small[:, 4, :], ALU.max), emptied["D"])
            n.own(emptied["D"])

            def over_pages(i):
                return hb(small[:, i, :]).unsqueeze(3).broadcast_to((P, HEADS, NB, 8))

            v.tensor_tensor(small[:, 4, :], small[:, 4, :], small[:, 5, :], ALU.subtract)
            n.up(v.tensor_tensor(SC[:], SC[:], over_pages(5), ALU.subtract), samp_dve)
            dve.wait_ge(samp_act, 2)
            n.up(v.tensor_reduce(hb(small[:, 6, :]), SC[:], AX.X, ALU.add), samp_dve)
            n.up(v.tensor_tensor(small[:, 0, :], bank_of("dn")[:, 0:64], small[:, 4, :], ALU.add), emptied["D"])
            n.own(emptied["D"])
            step(v.reciprocal(small[:, 0, :], small[:, 0, :]))
            v.tensor_tensor(small[:, 4, :], small[:, 4, :], small[:, 0, :], ALU.mult)
            n.up(v.tensor_tensor(SC[:], SC[:], over_pages(0), ALU.mult), samp_dve)
            n.own(samp_dve)
            for e in range(2):
                r = slice(HD * e, HD * e + HD)
                o = v.tensor_tensor(full_s[r, 0:4, :], vts[r], small[r, 4, :].rearrange("p (t e b) -> p t e b", e=2, b=NB)[:, :, e, :],
                                    ALU.mult)
            step(o)
            own_head = con[0:HEADS, C_ID:C_ID + HEADS].unsqueeze(2).broadcast_to((HEADS, HEADS, HD))
            for b in range(NB):
                dve.wait_ge(v_used, 8 * b + 8)
                if b >= 2:
                    dve.wait_ge(vm_used, b - 1)
                n.up(v.tensor_tensor(vm[:, b % 2, :].rearrange("p (h d) -> p h d", d=HD),
                                     Gp[b // 2 % 2][0:HEADS, b % 2, :].rearrange("p (h d) -> p h d", d=HD),
                                     own_head, ALU.mult), vm_ready)
            n.up(v.tensor_tensor(full_s[:, 0:4, :], full_s[:, 0:4, :],
                                 bank_of("ov")[:, 0:32].rearrange("p (t b) -> p t b", b=NB), ALU.add), emptied["D"])
            n.own(emptied["D"])
            ada_mod(ADA_NORM - 1)
            step(v.tensor_copy(G_hi[:, 0:4, 0:NB], full_s[:, 0:4, :]))
            n.up(minus_hi(G_lo[:, 0:4, 0:NB], full_s[:, 0:4, :], G_hi[:, 0:4, 0:NB]), g_ready)

            lo(N_OUT_EVEN)
            lo(N_OUT_EVEN + 1)
            for q in range(KD):
                lo(N_OUT_EVEN + q + 2)
                update(q, N_OUT_EVEN + q, mod_at(0, 2))

            def ffn(layer, i):
                rstd_parts(i)
                modulate(i)
                ghi0 = 4 + 38 * layer
                for t, ((_, kt), (n0, n1)) in enumerate(zip(THIRDS, ffn_starts(layer))):
                    base_a, base_d = runs[("gu", layer, t)]
                    done = sum(x for _, x in THIRDS[:t])

                    def body(i, n0=n0, base_a=base_a, done=done):
                        for j in range(4):
                            m = n0 + 4 * i + j + 2
                            if isinstance(i, int):
                                lo(m)
                            else:
                                lo(m, (j + 2) % 4, KD)
                            if j % 2 == 0:
                                dve.wait_ge(block_done, n0 + 4 * i + j + 2)
                                dve.wait_ge(slot_act, base_a + 2 * i + j // 2 + 1)
                                dve.wait_ge(ghi_ready, ghi0 + done + 2 * i + j // 2 - 1)
                                dst, up = full[:, j // 2, :], gate[:, j // 2, :]
                                v.tensor_tensor(dst.rearrange("p (c n) -> p c n", c=2), up.rearrange("p (c n) -> p c n", c=2),
                                                Gp[1][:, :, 0:CH], ALU.mult).then_inc(slot_dve, 1)
                            else:
                                dve.wait_ge(ghi_ready, ghi0 + done + 2 * i + j // 2 + 1)
                                g = ds(2 * i + j // 2, 1)
                                minus_hi(G_lo[:, g, :].rearrange("p o n -> p (o n)"), full[:, j // 2, :],
                                         G_hi[:, g, :].rearrange("p o n -> p (o n)")).then_inc(g_ready, 1)

                    with dve.Fori(0, kt // 2 - 1) as i_:
                        body(i_)
                    body(kt // 2 - 1)
                    if t == 0:
                        for g in ada_norm_groups(i):
                            ada_mod(g)
                    n.skip(slot_dve, kt)
                    n.skip(g_ready, kt)
                    for q in range(KD):
                        lo(n1 + q + 2)
                        update(q, n1 + q, mod_at(layer, 5))

            ffn(0, 1)

            rstd_parts(2)
            modulate(2)
            cos, sin = con[:, C_COS:C_COS + T], con[:, C_SIN:C_SIN + T]

            def rope(x):
                a, b = QK[:, x, :], QK[:, x + 1, :]
                for out, c, s, op in ((x, cos, sin, ALU.subtract), (x + 1, sin, cos, ALU.add)):
                    v.tensor_tensor(QKR[:, out, :], a, c, ALU.mult)
                    step(v.tensor_tensor(rsd[:], b, s, ALU.mult))
                    n.up(v.tensor_tensor(QKR[:, out, :], QKR[:, out, :], rsd[:], op), rope_ready)
                    n.own(rope_ready)

            def pair_sum(h):
                wait_emptied(dve, ("ro", h, 1))
                wait_job(dve, ("ro", h, 3))
                n.up(v.tensor_tensor(RSQ[:, 0, :], RVT[:, 0, :], RVT[:, 1, :], ALU.add), pair_dve)

            def tail(h, q):
                if q == 0:
                    for c in range(2):
                        cols = slice(c * CH, (c + 1) * CH)
                        bank = bank_of(("rm", h, c))
                        n.up(v.tensor_tensor(RVT[:, :, cols], RVT[:, :, cols],
                                             bank[:, 0:CH].unsqueeze(1).broadcast_to((P, 4, CH)), ALU.subtract),
                             emptied["D"])
                elif q == 1:
                    dve.wait_ge(ret_act, 5 * h + 2)
                    n.up(v.tensor_tensor(RSQ[:, 0, :], RSQ[:, 0, :], RSQ[:, 1, :], ALU.add), pair_dve)
                    for c in range(2):
                        n.up(v.tensor_scalar(rsd[:, c * CH:(c + 1) * CH], bank_of(("rv", h, c))[:, 0:CH], EPS, None,
                                             ALU.add), emptied["D"])
                    n.own(emptied["D"])
                    n.up(v.reciprocal(rsd[:], rsd[:]), ret_dve)
                elif q == 2:
                    dve.wait_ge(ret_act, 5 * h + 5)
                    for e in range(4):
                        g = V_RG + 4 * h + e
                        n.up(v.scalar_tensor_tensor(RVT[:, e, :], RVT[:, e, :], vec[:, g:g + 1], rsd[:],
                                                    ALU.mult, ALU.mult), dve_step)
                    for e in range(4):
                        n.own(dve_step, back=3 - e)
                        n.up(v.tensor_tensor(GS[:, e, :], RVT[:, e, :], GS[:, e, :], ALU.mult), ret_gated)
                elif q == 3:
                    for e in range(4):
                        dve.wait_ge(ghi_ready, 26 + 4 * h + e + 1)
                        n.up(minus_hi(G_lo[:, 4 * (h % 2) + e, :], GS[:, e, :], G_hi[:, 4 * (h % 2) + e, :]), g_ready)

            def new_state(h, b):
                if b >= 1 and h < RH - 1:
                    add_row(h, b - 1)
                dve.wait_ge(st_scaled, h * NB + b + 1)
                bank = bank_of(("vb", h, b))
                for d in range(2):
                    s = state(h, b)[:, d, :]
                    n.up(v.scalar_tensor_tensor(s, bank[:, :], kq_s[:, 2 + d, b:b + 1], s, ALU.mult, ALU.add),
                         (emptied["D"], st_updated)[d])

            def add_row(h, b):
                bank = bank_of(("so", h, b))
                if b == 0:
                    n.up(v.tensor_copy(osum[:], bank[0:NB, :]), emptied["D"])
                else:
                    n.own(emptied["D"])
                    n.up(v.tensor_tensor(osum[:], osum[:], bank[0:NB, :], ALU.add), emptied["D"])

            def norm_rows(h):
                if h < RH - 1:
                    add_row(h, NB - 1)
                n.own(emptied["D"])
                step(v.tensor_reduce(stat[:, 0:1], osum[:], AX.X, ALU.add))
                step(v.tensor_scalar(stat[:, 0:1], stat[:, 0:1], 1.0 / DV, None, ALU.mult))
                step(v.tensor_scalar(osum[:], osum[:], stat[:, 0:1], None, ALU.subtract))
                step(v.tensor_tensor(rsd[0:NB, 0:DV], osum[:], osum[:], ALU.mult))
                step(v.tensor_reduce(stat[:, 1:2], rsd[0:NB, 0:DV], AX.X, ALU.add))
                step(v.tensor_scalar(stat[:, 1:2], stat[:, 1:2], 1.0 / DV, EPS, ALU.mult, ALU.add))
                n.up(v.reciprocal(stat[:, 1:2], stat[:, 1:2]), osum_ready)

            def scale_rows(h):
                dve.wait_ge(osum_root, h + 1)
                n.up(v.tensor_scalar(osum[:], osum[:], stat[:, 1:2], None, ALU.mult), osum_ready)

            def gate_rows(h):
                bank = bank_of(("sot", h))
                for e in range(4):
                    g = V_RG + 4 * h + e
                    o = v.scalar_tensor_tensor(gs_s[:, e, :], bank[:, e * NB:(e + 1) * NB], vec[:, g:g + 1],
                                               gs_s[:, e, :], ALU.mult, ALU.mult)
                n.up(o, emptied["D"])
                n.own(emptied["D"])
                n.own(g_ready)
                tiles = slice(4 * (h % 2), 4 * (h % 2) + 4)
                step(v.tensor_copy(G_hi[:, tiles, 0:NB], gs_s[:]))
                n.up(minus_hi(G_lo[:, tiles, 0:NB], gs_s[:], G_hi[:, tiles, 0:NB]), g_ready)

            step(v.memset(qz[:], 0.0))
            for h in range(RH + 1):
                for q in range(HEAD_BLOCKS):
                    if h < RH:
                        lo(head_start(h) + q + 2)
                    if h > 0 and q == 0:
                        pair_sum(h - 1)
                    if h < RH and h > 0:
                        tail(h - 1, q)
                    if state_at(h, q) is not None:
                        new_state(h - 1, state_at(h, q))
                    if h == RH:
                        if query_at(h, q) is not None:
                            add_row(h - 1, query_at(h, q))
                        tail(h - 1, q)
                        if q in LATE_TURNS:
                            ada_mod(LATE_TURNS[q])
                    if h < RH and q in (4, 6):
                        dve.wait_ge(slot_act, runs[("head", h)][0] + q - 2)
                        rope(q - 4)
                if h == 0:
                    for g in ada_norm_groups(2):
                        ada_mod(g)
                if h > 0:
                    norm_rows(h - 1)
                if h < RH:
                    n.own(st_updated)
                    step(v.tensor_copy(kq_s[:], QKR[:, :, 0:NB]))
                    for d in range(2):
                        o = v.tensor_copy(qz[:, d, 0:NB * NB:NB + 1], kq_s[:, d, :])
                    n.up(o, qs_ready)
                if h < RH:
                    dve.wait_ge(dec_loaded, 16 * (h + 1))
                    for j in range(TB):
                        w = L - j * P
                        n.up(v.tensor_tensor(AD[:, j, 0:w], bank_of(("ra", h, j))[:, 0:w], dec[:, 0:w], ALU.mult),
                             emptied["D"])
                if h > 0:
                    scale_rows(h - 1)
                    gate_rows(h - 1)
                if h < RH:
                    n.own(g_ready)
                    dve.wait_ge(slot_act, runs[("head", h)][0] + HEAD_BLOCKS)
                    step(v.tensor_copy(gs_s[:], GS[:, :, 0:NB]))
                if h == RH - 1:
                    for b in range(2):
                        new_state(h, b)
                        add_row(h, b)
                if h in (2, RH):
                    n0 = out_start(0 if h == 2 else 1)
                    if h == RH:
                        spare_states_left(dve)
                    for q in range(KD):
                        lo(n0 + q + 2)
                        update(q, n0 + q, mod_at(1, 2))
            ffn(1, 3)
            rstd_parts(4)
            dve.wait_ge(rstd_ready, 5)
            for k in range(KD):
                n.up(v.scalar_tensor_tensor(YT[:, k, :], X[:, k, :], vec[:, V_FING + k:V_FING + k + 1], rstd[:],
                                            ALU.mult, ALU.mult), y_ready)
            for b in range(1, TB, 2):
                n.up(v.tensor_copy(yo[:, 5 + b, :], bank_of(("y", b, 1))[:, :]), emptied["D"])

        @block.gpsimd
        def _(pool):
            v = nc.gpsimd
            n = Tally(pool)
            n.up(v.memset(UP[:, :, 0:CW - 1], 0.0), pad_ready)

            def sum_squares(i):
                for k in range(1, KD - 1):
                    pool.wait_ge(sq_ready, KD * i + k + 1)
                    if k == 1:
                        if i > 0:
                            wait_emptied(pool, ("ss", i - 1, 1))
                        a = sq[:, 0, :]
                    else:
                        n.own(sq_used)
                        a = sqa[:]
                    n.up(v.tensor_tensor(sqa[:], a, sq[:, k % 2, :], ALU.add), sq_used)

            sum_squares(0)
            pool.wait_ge(u_ready, 4)

            def add_tap(w):
                n.own(tap_pool, back=0 if w == CW - 1 else 1)
                n.own(conv_pool)
                n.up(v.tensor_tensor(CV[:, 3, NB:T], CV[:, 3, NB:T], full[:, w % 2, 0:L], ALU.add), conv_pool)

            for w in range(CW):
                cw = vec[:, V_CW + w * 4 + 3:V_CW + w * 4 + 4]
                if w == 0:
                    n.own(pad_ready)
                    n.up(v.tensor_scalar(CV[:, 3, NB:T], UP[:, 3, 0:L], cw, vec[:, V_CB + 3:V_CB + 4],
                                         ALU.mult, ALU.add), conv_pool)
                else:
                    if w >= 2:
                        n.own(conv_pool)
                    n.up(v.tensor_scalar(full[:, w % 2, 0:L], UP[:, 3, w:w + L], cw, 1.0, ALU.mult, ALU.mult), tap_pool)
                if w >= 2:
                    add_tap(w - 1)
            add_tap(CW - 1)

            def divide(x):
                pool.wait_ge(ri_ready, x + 1)
                w = SS[:, x % TB, 0:(x % TB + 1) * P]
                v.tensor_scalar(w, w, ri[:, x:x + 1], 1.0, ALU.mult, ALU.mult).then_inc(p_ready, 1)

            def load_forget_pages():
                pool.wait_ge(pages_loaded, 32)
                wait_emptied(pool, "vs")
                for s in range(2):
                    pool.wait_ge(stage_stored[s], 16 * 4)
                v.indirect_dma_start(lg[:], None, A["cache_logf"][0].rearrange("n p h -> n (p h)"),
                                     bass.IndirectOffsetOnAxis(pt_col[:, 0:1], 0)).then_inc(lg_loaded, 16)

            divide(0)
            for h in range(HEADS):
                for q in range(TB):
                    x = h * TB + q
                    if x + 1 < HEADS * TB:
                        divide(x + 1)
                    if x == TB:
                        load_forget_pages()
                    for g in range(2 * x, 2 * x + 2):
                        pool.wait_ge(k_page[g % 4], 16 * (g // 4 + 1))
                        if g % 8 == 0:
                            wait_emptied(pool, ("qb", g // 8))
                        if g >= 2:
                            pool.wait_ge(page_dot, g - 1)
                        v.tensor_tensor(prod[:, g % 2, :], kp[:, g % 4, :], QB[:, g // 8, :], ALU.mult).then_inc(prod_ready, 1)
            sum_squares(1)
            sum_squares(2)
            pool.wait_ge(h_ready, KD * 3)
            wait_job(pool, ("ada", ADA_LATE - 1))

            def load_state(h, b):
                pool.dma_start(state(h, b), A["state_ret"][0, b, h].rearrange("(d p) e -> p d e", p=P)
                               ).then_inc(st_loaded[st_slot(h, b)], 16)

            for b in range(2):
                load_state(0, b)
            for h in range(RH):
                if h == RH - 1:
                    pool.wait_ge(qs_ready, RH)
                    wait_job(pool, ("ra", h, TB - 1))
                    load_state(h, 2)
                    load_state(h, 3)
                    wait_job(pool, ("ro", h, 3))
                    load_state(h, 4)
                    load_state(h, 5)
                wait_emptied(pool, ("ro", h, 3))
                n.up(v.tensor_tensor(RSQ[:, 1, :], RVT[:, 2, :], RVT[:, 3, :], ALU.add), pair_pool)
                pool.wait_ge(ret_act, 5 * h + 4)
                n.up(v.tensor_tensor(RSQ[:, 2, :], RSQ[:, 2, :], RSQ[:, 3, :], ALU.add), pair_pool)
                for b in range(NB):
                    g = h * NB + b
                    pool.wait_ge(st_updated, g + 1)
                    store(pool, A["ret_sample"][0, b, h].rearrange("(d p) e -> p d e", p=P), state(h, b),
                          st_stored[st_slot(h, b)])
                    if h < RH - 1:
                        nxt = ((g + 2) // NB, (g + 2) % NB)
                    elif b < 2:
                        nxt = (h, b + 6)
                    else:
                        continue
                    pool.wait_ge(st_stored[b % 2], 16 * (g // 2 + 1))
                    wait_job(pool, ("so", h, b))
                    load_state(*nxt)
            spare_states_left(pool)
            sum_squares(3)
            sum_squares(4)

        @block.sync
        def _(sp):
            sp.dma_start(con[:, 0:P], A["consts"][:, 0:P]).then_inc(ident_loaded, 16)
            sp.dma_start(xn[:, :, 0:512], A["x_prompt"][0][:, 0:512].rearrange("(b p) d -> p b d", p=P)).then_inc(xn_loaded[0], 16)
            sp.dma_start(xn[:, :, 512:D], A["x_prompt"][0][:, 512:D].rearrange("(b p) d -> p b d", p=P)).then_inc(xn_loaded[1], 16)
            sp.dma_start(xsn[:], A["x_sample"][:, 0, :]).then_inc(x_loaded, 16)
            sp.dma_start(cn[0:1, :], A["c_prompt"]).then_inc(x_loaded, 16)
            sp.dma_start(cn[1:9, :], A["c_sample"]).then_inc(x_loaded, 16)
            sp.dma_start(con[:, P:], A["consts"][:, P:]).then_inc(x_loaded, 16)
            sp.dma_start(pt_row[:], A["page_table"].rearrange("b g -> (b g)").rearrange("(o n) -> o n", o=1)).then_inc(pages_loaded, 16)
            sp.dma_start(pt_col[:], A["page_table"].rearrange("b g -> (b g)").rearrange("(n o) -> n o", o=1)).then_inc(pages_loaded, 16)

            def columns(w, k0, kt, c0):
                return w[k0 * P:(k0 + kt) * P, ds(c0, P)].rearrange("(k p) m -> p k m", p=P)

            def load(j, src, kt=KD):
                sp.dma_start(raw[:, j, 0:kt, :], src).then_inc(raw_loaded[j], 16)

            def load_ada(m, layer, c0):
                load(m % 4, columns(A["ada_w"][layer], 0, KD, c0))

            for m in range(4 * ADA_FIRST):
                if m >= 4:
                    sp.wait_ge(ada_used, m - 3)
                load_ada(m, 0, m * P)

            def load_n(n, w, k0, c0, kt=KD):
                if n < 4:
                    sp.wait_ge(ada_used, 4 * ADA_FIRST + n - 3)
                elif N_OUT_EVEN <= n < N_OUT_EVEN + 4:
                    sp.wait_ge(ada_used, 4 * ADA_NORM + n - N_OUT_EVEN - 3)
                else:
                    sp.wait_ge(lo_ready, n - 3)
                load(n % 4, columns(w, k0, kt, c0), kt)

            w = A["w_in_even"][0]
            for n, c0 in enumerate([1544 + P * j for j in range(4)] + [2056 + P * j for j in range(4)]
                                   + [P * j for j in range(12)]):
                load_n(n, w, 0, c0)
            def load_spare(i):
                for b in range(8):
                    c0 = (4 * ADA_NORM + 8 * (i - 1) + b - 48) * P
                    sp.dma_start((late if i == 3 else spare)[:, b, :, :], columns(A["ada_w"][1], 0, KD, c0)).then_inc(spare_loaded[b], 16)

            for m in range(4 * ADA_FIRST, 4 * ADA_ATT):
                if m < 4 * ADA_FIRST + 4:
                    sp.wait_ge(lo_ready, N_OUT_EVEN + m - 4 * ADA_FIRST - 3)
                else:
                    sp.wait_ge(ada_used, m - 3)
                load_ada(m, 0, m * P)

            for m in range(4 * ADA_ATT, 4 * ADA_ATT + 4):
                sp.wait_ge(ada_used, m - 3)
                load_ada(m, 0, m * P)
            sp.wait_ge(pages_loaded, 32)
            sp.wait_ge(g_ready, 4)

            for j in range(4):
                page(sp, j, cache_k, kp, j, k_page)
            with sp.Fori(1, NPG // 4) as i:
                for j in range(4):
                    sp.wait_ge(prod_ready, 4 * i + j - 3)
                    page(sp, 4 * i + j, cache_k, kp, j, k_page)
            for j in range(4):
                load_n(N_OUT_EVEN + j, A["w_out_even"][0], 0, P * j)
            sp.wait_ge(v_stored, 16 * TB)
            wait_job(sp, ("o", HEADS - 1))
            value_pages(sp, 0)
            sp.wait_ge(g_ready, 5)
            load_spare(1)
            for j in range(4, 8):
                load_n(N_OUT_EVEN + j, A["w_out_even"][0], 0, P * j)

            def ffn(layer):
                wg, wu, wd = A["w_ffn_gate"][layer], A["w_ffn_up"][layer], A["w_ffn_down"][layer]
                for (k0, kt), (n0, n1) in zip(THIRDS, ffn_starts(layer)):
                    with sp.Fori(0, kt // 2) as i:
                        for j in range(4):
                            sp.wait_ge(lo_ready, n0 + 4 * i + j - 3)
                            load(j, columns(wu if j % 2 else wg, 0, KD, (k0 + j // 2) * P + 2 * P * i))
                    with sp.Fori(0, 2) as i:
                        for j in range(4):
                            sp.wait_ge(lo_ready, n1 + 4 * i + j - 3)
                            load(j, columns(wd, k0, kt, 4 * P * i + j * P), kt)
                    if layer == 0 and k0 == 0:
                        wait_job(sp, ("adr", ADA_NORM + 1))
                        load_spare(2)

            ffn(0)
            w = A["w_in_odd"][0]
            for h in range(RH):
                cols = ([h * DK + P * j for j in range(2)] + [D + h * DK + P * j for j in range(2)]
                        + [2 * D + h * DV + P * j for j in range(4)] + [4 * D + h * DV + P * j for j in range(4)])
                for j in range(HEAD_BLOCKS):
                    load_n(head_start(h) + j, w, 0, cols[j])
                if h >= 1:
                    wait_emptied(sp, ("ra", h - 1, TB - 1))
                sp.dma_start(dec[:], A["decay"][h]).then_inc(dec_loaded, 16)
                if h >= 2:
                    for j in range(KD):
                        if h == RH - 1 and j == 4:
                            sp.wait_ge(block_done, head_start(h) + HEAD_BLOCKS)
                            load_spare(3)
                        load_n(out_start(h - 2) + j, A["w_out_odd"][0], (h - 2) * KD, P * j)
            ffn(1)
            for f in range(2):
                cols = slice(f * 512, (f + 1) * 512)
                for b in range(TB):
                    wait_emptied(sp, ("y", b, f))
                    store(sp, A["y_prompt"][0, b * P:(b + 1) * P, cols], yo[:, 5 * f + b, :])
                wait_emptied(sp, ("ys", f))
                store(sp, A["y_sample"][:, 0, cols], yo[0:NB, 5 * f + TB, :])
            for s in {s.name: s for s in outs}.values():
                sp.wait_ge(s, 16 * sum(o.name == s.name for o in outs))


def constants():
    c = np.zeros((P, C_END), np.float32)
    i = np.arange(P)
    c[:, C_ID:C_ID + P] = np.eye(P)
    c[:, C_MEAN] = 1.0 / D
    c[:, C_B64:C_B64 + P] = (i[:, None] // 64 == i[None, :] // 64) / 64.0
    c[:, C_M512] = 1.0 / DV
    c[:, C_ONE] = 1.0
    for e in range(2):
        c[64 * e:64 * e + 64, C_GRP + 6 + e] = 1.0 / 64.0
    c[:, C_TRI:C_TRI + P] = i[:, None] <= i[None, :]
    c[:, C_NEG:C_NEG + P] = np.where(i[None, :] <= i[:, None], 0.0, MASKED)
    inv = (np.float32(1) / np.power(np.float32(10000), np.linspace(0, 1, P, dtype=np.float32))).astype(np.float32)
    pos = np.concatenate([np.full(NB, PAST), np.arange(L)]).astype(np.float32)
    angle = (pos[None, :] * inv[:, None]).astype(np.float32).astype(np.float64)
    c[:, C_COS:C_COS + T] = np.cos(angle)
    c[:, C_SIN:C_SIN + T] = np.sin(angle)
    for b in range(TB):
        for h in range(RH):
            c[:, C_KDEC + b * RH + h] = GAMMA[h] ** (L - 1 - (b * P + i))
    dist = np.arange(L)[None, :] - i[:, None]
    decay = np.stack([np.where(dist >= 0, g ** np.maximum(dist, 0.0), 0.0) for g in GAMMA]).astype(np.float32)
    return c, decay


_INS = ["x_prompt", "x_sample", "cache_k", "cache_v", "cache_logf", "state_conv", "state_ret", "page_table",
        "c_prompt", "c_sample", "ada_w", "ada_b", "norm_mix_g", "norm_ffn_g", "w_in_even", "b_forget",
        "conv_w", "conv_b", "conv_norm_g", "conv_norm_b", "w_out_even", "w_in_odd", "ret_norm_g", "w_out_odd",
        "w_ffn_gate", "w_ffn_up", "w_ffn_down", "final_norm_g"]
_OUTS = [("y_prompt", (1, L, D)), ("y_sample", (NB, 1, D)), ("k_prompt", (1, 1, L, HEADS, HD)),
         ("v_prompt", (1, 1, L, HEADS, HD)), ("logf_prompt", (1, 1, L, HEADS)),
         ("conv_prompt", (1, 1, CW - 1, 512)), ("ret_prompt", (1, 1, RH, DK, DV)),
         ("k_sample", (1, NB, 1, HEADS, HD)), ("v_sample", (1, NB, 1, HEADS, HD)),
         ("logf_sample", (1, NB, 1, HEADS)), ("conv_sample", (1, NB, CW - 1, 512)),
         ("ret_sample", (1, NB, RH, DK, DV))]


def kernel(**inputs):
    import concourse.bacc as bacc
    from concourse.bass_utils import run_bass_kernel_spmd

    nc = bacc.Bacc("TRN2", target_bir_lowering=False, num_devices=1)
    arrays = {f"in_{n}": np.ascontiguousarray(inputs[n]) for n in _INS}
    arrays["in_consts"], arrays["in_decay"] = constants()
    aps = {n[3:]: nc.dram_tensor(n, a.shape, mybir.dt.from_np(a.dtype), kind="ExternalInput").ap()
           for n, a in arrays.items()}
    for n, shape in _OUTS:
        aps[n] = nc.dram_tensor(f"out_{n}", shape, mybir.dt.float32, kind="ExternalOutput").ap()
    build(nc, aps)
    r = run_bass_kernel_spmd(nc, [arrays], core_ids=[0])
    return tuple(r.results[0][f"out_{n}"] for n, _ in _OUTS)
```
